# Optimizing a Trainium2 kernel written in Bass

```python
import math
import jax, jax.numpy as jnp
from jax import lax
import numpy as np

D_MODEL = 1024
BATCH = 1
SEQ = 512
DEPTH = 2

D_MIX = D_MODEL
DN_HEADS = 4
DN_DK = 128
DN_DV = 128
DN_CONV = 4
DN_CHUNK = 64
DN_WIDTH = DN_HEADS * DN_DV
DN_KEY_WIDTH = DN_HEADS * DN_DK
GLA_HEADS = 4
GLA_DK = 64
GLA_DV = 128
GLA_GATE_RANK = 16
GLA_TAU = 16.0
GLA_CHUNK = 16
GLA_WIDTH = GLA_HEADS * GLA_DV
GLA_KEY_WIDTH = GLA_HEADS * GLA_DK
IN_SIZES = (DN_KEY_WIDTH, DN_KEY_WIDTH, DN_WIDTH,
            DN_WIDTH,
            DN_HEADS, DN_HEADS,
            GLA_KEY_WIDTH, GLA_KEY_WIDTH, GLA_WIDTH,
            GLA_WIDTH,
            GLA_GATE_RANK)
D_IN_PROJ = 3 * 512 + 512 + 4 + 4 + 256 + 256 + 512 + 512 + 16
DEEPNORM_ALPHA = (2.0 * DEPTH) ** 0.25
DEEPNORM_BETA = (8.0 * DEPTH) ** -0.25
NORM_EPS = 1e-6


def _split(a, sizes):
    out, off = [], 0
    for s in sizes:
        out.append(a[..., off:off + s])
        off += s
    return out

def _to_chunks(a, chunk):
    b, t = a.shape[:2]
    a = a.reshape((b, t // chunk, chunk) + a.shape[2:])
    return jnp.moveaxis(a, 3, 1)

def _from_scan(o):
    n, b, h, c, d = o.shape
    return jnp.transpose(o, (1, 0, 3, 2, 4)).reshape(b, n * c, h, d)

def causal_short_conv(x, w):
    k, c = w.shape
    return lax.conv_general_dilated(
        x, w[:, None, :].astype(x.dtype), window_strides=(1,),
        padding=[(k - 1, 0)], dimension_numbers=("NWC", "WIO", "NWC"),
        feature_group_count=c)

def l2norm(x):
    xf = x.astype(jnp.float32)
    return xf * lax.rsqrt(jnp.sum(xf * xf, axis=-1, keepdims=True) + NORM_EPS)

def head_rms_norm(o, g):
    of = o.astype(jnp.float32)
    of = of * lax.rsqrt(jnp.mean(of * of, axis=-1, keepdims=True) + NORM_EPS)
    return of * g.astype(jnp.float32)

def layer_norm(x, g, b):
    xf = x.astype(jnp.float32)
    mu = jnp.mean(xf, axis=-1, keepdims=True)
    var = jnp.mean(jnp.square(xf - mu), axis=-1, keepdims=True)
    y = (xf - mu) * lax.rsqrt(var + NORM_EPS) * g.astype(jnp.float32) + b.astype(jnp.float32)
    return y.astype(x.dtype)

def gated_delta_rule_chunked(q, k, v, g, beta):
    f32 = jnp.float32
    q, k, v, g, beta = (a.astype(f32) for a in (q, k, v, g, beta))
    b_, t, h, dk = q.shape
    dv = v.shape[-1]
    c = DN_CHUNK
    qc, kc, vc = (_to_chunks(a, c) for a in (q, k, v))
    gc, bc = _to_chunks(g, c), _to_chunks(beta, c)
    G = jnp.cumsum(gc, axis=-1)
    pos = jnp.arange(c)
    causal = pos[:, None] >= pos[None, :]
    strict = pos[:, None] > pos[None, :]
    diff = G[..., :, None] - G[..., None, :]
    decay = jnp.where(causal, jnp.exp(jnp.where(causal, diff, 0.0)), 0.0)
    k_beta = kc * bc[..., None]
    kk = jnp.einsum("bhnid,bhnjd->bhnij", k_beta, kc)
    lower = jnp.eye(c, dtype=f32) + jnp.where(strict, kk * decay, 0.0)
    rhs = jnp.concatenate([vc * bc[..., None], k_beta * jnp.exp(G)[..., None]], axis=-1)
    uw = lax.linalg.triangular_solve(lower, rhs, left_side=True, lower=True)
    u, w = uw[..., :dv], uw[..., dv:]
    attn = jnp.einsum("bhnid,bhnjd->bhnij", qc, kc) * decay
    xs = tuple(jnp.moveaxis(a, 2, 0) for a in (qc, kc, u, w, G, attn))
    s0 = jnp.zeros((b_, h, dk, dv), f32)

    def step(S, inp):
        q_n, k_n, u_n, w_n, g_n, a_n = inp
        v_new = u_n - jnp.einsum("bhid,bhde->bhie", w_n, S)
        o_n = (jnp.einsum("bhid,bhde->bhie", q_n * jnp.exp(g_n)[..., None], S)
               + jnp.einsum("bhij,bhje->bhie", a_n, v_new))
        g_last = g_n[..., -1]
        k_dec = k_n * jnp.exp(g_last[..., None] - g_n)[..., None]
        S = S * jnp.exp(g_last)[..., None, None] + jnp.einsum("bhid,bhie->bhde", k_dec, v_new)
        return S, o_n

    _, o = lax.scan(step, s0, xs)
    return _from_scan(o)

def gla_chunked(q, k, v, gk):
    f32 = jnp.float32
    q, k, v, gk = (a.astype(f32) for a in (q, k, v, gk))
    b_, t, h, dk = q.shape
    dv = v.shape[-1]
    c = GLA_CHUNK
    qc, kc, vc, gc = (_to_chunks(a, c) for a in (q, k, v, gk))
    Bc = jnp.cumsum(gc, axis=-2)
    pos = jnp.arange(c)
    causal = (pos[:, None] >= pos[None, :])[..., None]
    diff = Bc[..., :, None, :] - Bc[..., None, :, :]
    dec = jnp.where(causal, jnp.exp(jnp.where(causal, diff, 0.0)), 0.0)
    attn = jnp.einsum("bhnid,bhnjd,bhnijd->bhnij", qc, kc, dec)
    xs = tuple(jnp.moveaxis(a, 2, 0) for a in (qc, kc, vc, Bc, attn))
    s0 = jnp.zeros((b_, h, dk, dv), f32)

    def step(S, inp):
        q_n, k_n, v_n, b_n, a_n = inp
        o_n = (jnp.einsum("bhid,bhde->bhie", q_n * jnp.exp(b_n), S)
               + jnp.einsum("bhij,bhje->bhie", a_n, v_n))
        b_last = b_n[..., -1:, :]
        k_dec = k_n * jnp.exp(b_last - b_n)
        S = S * jnp.exp(b_last[..., 0, :])[..., None] + jnp.einsum("bhid,bhie->bhde", k_dec, v_n)
        return S, o_n

    _, o = lax.scan(step, s0, xs)
    return _from_scan(o)

def hybrid_layer(x, w_in, conv_w, dn_a_log, dn_dt_bias, gla_gate_w2, gla_gate_b,
                 dn_norm_g, gla_norm_g, w_out, ln_g, ln_b):
    bsz, t, _ = x.shape
    proj = jnp.einsum("btd,de->bte", x, w_in)
    (dn_q, dn_k, dn_v, dn_z, dn_b, dn_a,
     g_q, g_k, g_v, g_z, g_r) = _split(proj, IN_SIZES)

    dn_qkv = jax.nn.silu(causal_short_conv(jnp.concatenate([dn_q, dn_k, dn_v], axis=-1), conv_w))
    cq, ck, cv = _split(dn_qkv, (DN_KEY_WIDTH, DN_KEY_WIDTH, DN_WIDTH))
    q = l2norm(cq.reshape(bsz, t, DN_HEADS, DN_DK)) * (DN_DK ** -0.5)
    k = l2norm(ck.reshape(bsz, t, DN_HEADS, DN_DK))
    v = cv.reshape(bsz, t, DN_HEADS, DN_DV)
    beta = jax.nn.sigmoid(dn_b.astype(jnp.float32))
    g = -jnp.exp(dn_a_log.astype(jnp.float32)) * jax.nn.softplus(
        dn_a.astype(jnp.float32) + dn_dt_bias.astype(jnp.float32))
    o_dn = gated_delta_rule_chunked(q, k, v, g, beta)
    o_dn = head_rms_norm(o_dn, dn_norm_g) * jax.nn.silu(
        dn_z.reshape(bsz, t, DN_HEADS, DN_DV).astype(jnp.float32))

    gq = g_q.reshape(bsz, t, GLA_HEADS, GLA_DK) * (GLA_DK ** -0.5)
    gk = g_k.reshape(bsz, t, GLA_HEADS, GLA_DK)
    gv = g_v.reshape(bsz, t, GLA_HEADS, GLA_DV)
    gate_logits = jnp.einsum("btr,re->bte", g_r, gla_gate_w2) + gla_gate_b
    log_f = (jax.nn.log_sigmoid(gate_logits.astype(jnp.float32)) / GLA_TAU).reshape(
        bsz, t, GLA_HEADS, GLA_DK)
    o_gla = gla_chunked(gq, gk, gv, log_f)
    o_gla = head_rms_norm(o_gla, gla_norm_g) * jax.nn.silu(
        g_z.reshape(bsz, t, GLA_HEADS, GLA_DV).astype(jnp.float32))

    o = jnp.concatenate([o_dn.reshape(bsz, t, DN_WIDTH),
                         o_gla.reshape(bsz, t, GLA_WIDTH)], axis=-1).astype(x.dtype)
    y = jnp.einsum("bte,ed->btd", o, w_out)
    return layer_norm(DEEPNORM_ALPHA * x + y, ln_g, ln_b)

def first_inputs(seed: int = 0) -> dict:
    key = jax.random.key(seed)
    ks = jax.random.split(key, 12)
    f32 = jnp.float32
    x = jax.random.normal(ks[0], (BATCH, SEQ, D_MODEL), f32)
    col_scale = jnp.concatenate([
        jnp.ones((2 * DN_KEY_WIDTH,), f32),
        jnp.full((DN_WIDTH,), DEEPNORM_BETA, f32),
        jnp.ones((DN_WIDTH + 2 * DN_HEADS + 2 * GLA_KEY_WIDTH,), f32),
        jnp.full((GLA_WIDTH,), DEEPNORM_BETA, f32),
        jnp.ones((GLA_WIDTH + GLA_GATE_RANK,), f32)])
    w_in = jax.random.normal(ks[1], (DEPTH, D_MODEL, D_IN_PROJ), f32) * (D_MODEL ** -0.5) * col_scale
    conv_w = jax.random.normal(ks[2], (DEPTH, DN_CONV, DN_KEY_WIDTH * 2 + DN_WIDTH), f32) * (DN_CONV ** -0.5)
    dn_a_log = jnp.log(jax.random.uniform(ks[3], (DEPTH, DN_HEADS), f32, 1.0, 16.0))
    dt = jnp.exp(jax.random.uniform(ks[4], (DEPTH, DN_HEADS), f32, math.log(1e-3), math.log(1e-1)))
    dn_dt_bias = dt + jnp.log(-jnp.expm1(-dt))
    gla_gate_w2 = jax.random.normal(ks[5], (DEPTH, GLA_GATE_RANK, GLA_KEY_WIDTH), f32) * (GLA_GATE_RANK ** -0.5)
    gla_gate_b = 0.1 * jax.random.normal(ks[6], (DEPTH, GLA_KEY_WIDTH), f32)
    dn_norm_g = 1.0 + 0.02 * jax.random.normal(ks[7], (DEPTH, DN_DV), f32)
    gla_norm_g = 1.0 + 0.02 * jax.random.normal(ks[8], (DEPTH, GLA_DV), f32)
    w_out = jax.random.normal(ks[9], (DEPTH, D_MIX, D_MODEL), f32) * (D_MIX ** -0.5) * DEEPNORM_BETA
    ln_g = 1.0 + 0.02 * jax.random.normal(ks[10], (DEPTH, D_MODEL), f32)
    ln_b = 0.02 * jax.random.normal(ks[11], (DEPTH, D_MODEL), f32)
    return {"x": x, "w_in": w_in, "conv_w": conv_w, "dn_a_log": dn_a_log,
            "dn_dt_bias": dn_dt_bias, "gla_gate_w2": gla_gate_w2, "gla_gate_b": gla_gate_b,
            "dn_norm_g": dn_norm_g, "gla_norm_g": gla_norm_g, "w_out": w_out,
            "ln_g": ln_g, "ln_b": ln_b}

def first_block(x, w_in, conv_w, dn_a_log, dn_dt_bias, gla_gate_w2, gla_gate_b,
              dn_norm_g, gla_norm_g, w_out, ln_g, ln_b):
    h = x
    for l in range(DEPTH):
        h = hybrid_layer(h, w_in[l], conv_w[l], dn_a_log[l], dn_dt_bias[l],
                         gla_gate_w2[l], gla_gate_b[l], dn_norm_g[l], gla_norm_g[l],
                         w_out[l], ln_g[l], ln_b[l])
    return h


N_MIXERS = 3
BLOCK = 128
EPS = 1e-6
NEG = -1e30

SB_HEADS = 16
SB_HEAD_DIM = 64

DIL_GROUPS = ((128, 1), (512, 4), (2048, 16))
DIL_HEADS = 8
DIL_HEAD_DIM = 64
N_BUCKETS = 32
BUCKET_MAX_DIST = 2048

MLA_HEADS = 16
MLA_Q_RANK = 384
MLA_KV_RANK = 256
MLA_NOPE = 64
MLA_ROPE = 32
MLA_V = 64
ROPE_THETA = 10000.0

D_FF = 2816
CONV_W = 3


def rms_norm(x, g):
    xf = x.astype(jnp.float32)
    y = xf * lax.rsqrt(jnp.mean(xf * xf, axis=-1, keepdims=True) + EPS)
    return (y * g.astype(jnp.float32)).astype(x.dtype)

def t5_bucket(dist):
    dist = jnp.maximum(dist, 0)
    max_exact = N_BUCKETS // 2
    d = jnp.maximum(dist.astype(jnp.float32), 1.0)
    large = max_exact + (jnp.log(d / max_exact) / math.log(BUCKET_MAX_DIST / max_exact)
                         * (N_BUCKETS - max_exact)).astype(jnp.int32)
    large = jnp.minimum(large, N_BUCKETS - 1)
    return jnp.where(dist < max_exact, dist, large)

def stick_breaking_attention(xn, w_qkv, w_o):
    B, S, _ = xn.shape
    H, dh = SB_HEADS, SB_HEAD_DIM
    qkv = (xn @ w_qkv).reshape(B, S, 3, H, dh)
    q, k, v = qkv[:, :, 0], qkv[:, :, 1], qkv[:, :, 2]
    nb = S // BLOCK
    qb = q.reshape(B, nb, BLOCK, H, dh).transpose(1, 0, 3, 2, 4)
    kt = k.transpose(0, 2, 1, 3)
    vt = v.transpose(0, 2, 1, 3)
    key_pos = jnp.arange(S)
    scale = dh ** -0.5

    def one_block(args):
        q_blk, n = args
        z = jnp.einsum('bhqd,bhkd->bhqk', q_blk, kt).astype(jnp.float32) * scale
        q_pos = n * BLOCK + jnp.arange(BLOCK)
        mask = key_pos[None, :] < q_pos[:, None]
        log_not = jnp.where(mask, jax.nn.log_sigmoid(-z), 0.0)
        between = lax.cumsum(log_not, axis=3, reverse=True) - log_not
        a = jnp.where(mask, jnp.exp(jax.nn.log_sigmoid(z) + between), 0.0)
        return jnp.einsum('bhqk,bhkd->bhqd', a.astype(vt.dtype), vt)

    o = lax.map(one_block, (qb, jnp.arange(nb)))
    o = o.transpose(1, 0, 3, 2, 4).reshape(B, S, H * dh)
    return o @ w_o

def strided_window_attention(q, k, v, dilation, n_back, bias_g):
    B, S, Hg, dh = q.shape
    r, W = dilation, n_back
    L = S // r

    def to_sub(a):
        return a.reshape(B, L, r, Hg, dh).transpose(0, 2, 3, 1, 4)

    qs, ks, vs = to_sub(q), to_sub(k), to_sub(v)
    Lp = -(-L // W) * W
    nb = Lp // W
    pad = Lp - L
    qs = jnp.pad(qs, ((0, 0), (0, 0), (0, 0), (0, pad), (0, 0)))
    kp = jnp.pad(ks, ((0, 0), (0, 0), (0, 0), (W, pad), (0, 0)))
    vp = jnp.pad(vs, ((0, 0), (0, 0), (0, 0), (W, pad), (0, 0)))
    q_blk = qs.reshape(B, r, Hg, nb, W, dh)
    k_blk = jnp.concatenate([kp[:, :, :, :Lp].reshape(B, r, Hg, nb, W, dh),
                             kp[:, :, :, W:].reshape(B, r, Hg, nb, W, dh)], axis=4)
    v_blk = jnp.concatenate([vp[:, :, :, :Lp].reshape(B, r, Hg, nb, W, dh),
                             vp[:, :, :, W:].reshape(B, r, Hg, nb, W, dh)], axis=4)
    i = jnp.arange(W)[:, None]
    j = jnp.arange(2 * W)[None, :]
    m = i + W - j
    key_abs = jnp.arange(nb)[:, None, None] * W - W + j[None]
    mask = (m >= 0)[None] & (m <= n_back)[None] & (key_abs >= 0)
    bias = bias_g[t5_bucket(m * r)].astype(jnp.float32).transpose(2, 0, 1)
    s = jnp.einsum('brhnqd,brhnkd->brhnqk', q_blk, k_blk).astype(jnp.float32) * (dh ** -0.5)
    s = jnp.where(mask[None, None, None], s + bias[None, None, :, None], NEG)
    lse = jax.nn.logsumexp(s, axis=-1)
    p = jnp.exp(s - lse[..., None])
    o = jnp.einsum('brhnqk,brhnkd->brhnqd', p.astype(v_blk.dtype), v_blk)
    o = o.reshape(B, r, Hg, Lp, dh)[:, :, :, :L].transpose(0, 3, 1, 2, 4).reshape(B, S, Hg, dh)
    lse = lse.reshape(B, r, Hg, Lp)[:, :, :, :L].transpose(0, 3, 1, 2).reshape(B, S, Hg)
    return o, lse

def dilated_attention(xn, w_qkv, w_o, rel_bias):
    B, S, _ = xn.shape
    G, Hg, dh = len(DIL_GROUPS), DIL_HEADS, DIL_HEAD_DIM
    qkv = (xn @ w_qkv).reshape(B, S, 3, G, Hg, dh)
    outs, lses = [], []
    for g, (window, dilation) in enumerate(DIL_GROUPS):
        o, lse = strided_window_attention(qkv[:, :, 0, g], qkv[:, :, 1, g], qkv[:, :, 2, g],
                                          dilation, window // dilation,
                                          rel_bias[:, g * Hg:(g + 1) * Hg])
        outs.append(o)
        lses.append(lse)
    outs = jnp.stack(outs)
    wts = jax.nn.softmax(jnp.stack(lses), axis=0)
    o = jnp.einsum('gbshd,gbsh->bshd', outs, wts.astype(outs.dtype)).reshape(B, S, Hg * dh)
    return o @ w_o

def apply_rope(x, positions):
    half = x.shape[-1] // 2
    freqs = ROPE_THETA ** (-jnp.arange(half, dtype=jnp.float32) / half)
    ang = positions.astype(jnp.float32)[:, :, None, None] * freqs
    cos, sin = jnp.cos(ang).astype(x.dtype), jnp.sin(ang).astype(x.dtype)
    x1, x2 = x[..., :half], x[..., half:]
    return jnp.concatenate([x1 * cos - x2 * sin, x2 * cos + x1 * sin], axis=-1)

def causal_softmax_blocks(q, k, v, scale):
    B, S, H, dq = q.shape
    nb = S // BLOCK
    qb = q.reshape(B, nb, BLOCK, H, dq).transpose(1, 0, 3, 2, 4)
    kt = k.transpose(0, 2, 1, 3)
    vt = v.transpose(0, 2, 1, 3)
    key_pos = jnp.arange(S)

    def one_block(args):
        q_blk, n = args
        s = jnp.einsum('bhqd,bhkd->bhqk', q_blk, kt).astype(jnp.float32) * scale
        q_pos = n * BLOCK + jnp.arange(BLOCK)
        s = jnp.where(key_pos[None, :] <= q_pos[:, None], s, NEG)
        p = jax.nn.softmax(s, axis=-1)
        return jnp.einsum('bhqk,bhkd->bhqd', p.astype(vt.dtype), vt)

    o = lax.map(one_block, (qb, jnp.arange(nb)))
    return o.transpose(1, 0, 3, 2, 4).reshape(B, S, H, v.shape[-1])

def latent_attention(xn, positions, w_in, q_norm, w_qb, kv_norm, w_kvb, w_o):
    B, S, _ = xn.shape
    H = MLA_HEADS
    h = xn @ w_in
    c_q = h[..., :MLA_Q_RANK]
    c_kv = h[..., MLA_Q_RANK:MLA_Q_RANK + MLA_KV_RANK]
    k_rope = h[..., MLA_Q_RANK + MLA_KV_RANK:][:, :, None, :]
    q = (rms_norm(c_q, q_norm) @ w_qb).reshape(B, S, H, MLA_NOPE + MLA_ROPE)
    kv = (rms_norm(c_kv, kv_norm) @ w_kvb).reshape(B, S, H, MLA_NOPE + MLA_V)
    q_rope = apply_rope(q[..., MLA_NOPE:], positions)
    k_rope = apply_rope(k_rope, positions)
    q_full = jnp.concatenate([q[..., :MLA_NOPE], q_rope], axis=-1)
    k_full = jnp.concatenate([kv[..., :MLA_NOPE],
                              jnp.broadcast_to(k_rope, (B, S, H, MLA_ROPE))], axis=-1)
    o = causal_softmax_blocks(q_full, k_full, kv[..., MLA_NOPE:], (MLA_NOPE + MLA_ROPE) ** -0.5)
    return o.reshape(B, S, H * MLA_V) @ w_o

def conv_ffn(xn, w_up, conv_w, conv_b, w_down):
    h = xn @ w_up
    C = h.shape[-1]
    h = lax.conv_general_dilated(h, conv_w[:, None, :], window_strides=(1,),
                                 padding=[(CONV_W - 1, 0)],
                                 dimension_numbers=('NWC', 'WIO', 'NWC'),
                                 feature_group_count=C) + conv_b
    g, u = h[..., :D_FF], h[..., D_FF:]
    return (jax.nn.silu(g) * u) @ w_down

def second_inputs(seed: int = 0) -> dict:
    key = jax.random.key(seed)
    ks = iter(jax.random.split(key, 32))
    n_a = len(range(0, DEPTH, N_MIXERS))
    n_b = len(range(1, DEPTH, N_MIXERS))
    n_c = len(range(2, DEPTH, N_MIXERS))
    G = len(DIL_GROUPS)

    def w(shape, fan_in):
        return jax.random.normal(next(ks), shape, jnp.float32) * fan_in ** -0.5

    def gain(shape):
        return 1.0 + 0.05 * jax.random.normal(next(ks), shape, jnp.float32)

    return {
        'x': jax.random.normal(next(ks), (BATCH, SEQ, D_MODEL), jnp.float32),
        'positions': jnp.broadcast_to(jnp.arange(SEQ, dtype=jnp.int32), (BATCH, SEQ)),
        'rel_bias': 0.5 * jax.random.normal(next(ks), (N_BUCKETS, G * DIL_HEADS), jnp.float32),
        'norm_gains': gain((DEPTH, 4, D_MODEL)),
        'sb_w_qkv': w((n_a, D_MODEL, 3 * SB_HEADS * SB_HEAD_DIM), D_MODEL),
        'sb_w_o': w((n_a, SB_HEADS * SB_HEAD_DIM, D_MODEL), SB_HEADS * SB_HEAD_DIM),
        'dil_w_qkv': w((n_b, D_MODEL, 3 * G * DIL_HEADS * DIL_HEAD_DIM), D_MODEL),
        'dil_w_o': w((n_b, DIL_HEADS * DIL_HEAD_DIM, D_MODEL), DIL_HEADS * DIL_HEAD_DIM),
        'mla_w_in': w((n_c, D_MODEL, MLA_Q_RANK + MLA_KV_RANK + MLA_ROPE), D_MODEL),
        'mla_q_norm': gain((n_c, MLA_Q_RANK)),
        'mla_w_qb': w((n_c, MLA_Q_RANK, MLA_HEADS * (MLA_NOPE + MLA_ROPE)), MLA_Q_RANK),
        'mla_kv_norm': gain((n_c, MLA_KV_RANK)),
        'mla_w_kvb': w((n_c, MLA_KV_RANK, MLA_HEADS * (MLA_NOPE + MLA_V)), MLA_KV_RANK),
        'mla_w_o': w((n_c, MLA_HEADS * MLA_V, D_MODEL), MLA_HEADS * MLA_V),
        'ffn_w_up': w((DEPTH, D_MODEL, 2 * D_FF), D_MODEL),
        'ffn_conv_w': w((DEPTH, CONV_W, 2 * D_FF), CONV_W),
        'ffn_conv_b': 0.02 * jax.random.normal(next(ks), (DEPTH, 2 * D_FF), jnp.float32),
        'ffn_w_down': w((DEPTH, D_FF, D_MODEL), D_FF),
    }

def second_block(x, positions, rel_bias, norm_gains, sb_w_qkv, sb_w_o, dil_w_qkv, dil_w_o,
              mla_w_in, mla_q_norm, mla_w_qb, mla_kv_norm, mla_w_kvb, mla_w_o,
              ffn_w_up, ffn_conv_w, ffn_conv_b, ffn_w_down):
    for i in range(DEPTH):
        kind, j = i % N_MIXERS, i // N_MIXERS
        hn = rms_norm(x, norm_gains[i, 0])
        if kind == 0:
            m = stick_breaking_attention(hn, sb_w_qkv[j], sb_w_o[j])
        elif kind == 1:
            m = dilated_attention(hn, dil_w_qkv[j], dil_w_o[j], rel_bias)
        else:
            m = latent_attention(hn, positions, mla_w_in[j], mla_q_norm[j], mla_w_qb[j],
                                 mla_kv_norm[j], mla_w_kvb[j], mla_w_o[j])
        x = x + rms_norm(m, norm_gains[i, 1])
        f = conv_ffn(rms_norm(x, norm_gains[i, 2]), ffn_w_up[i], ffn_conv_w[i],
                     ffn_conv_b[i], ffn_w_down[i])
        x = x + rms_norm(f, norm_gains[i, 3])
    return x


def setup_inputs(seed=0):
    out = dict(first_inputs(seed))
    for name, value in second_inputs(seed + 1).items():
        if name != "x":
            out[name + "_2"] = value
    return out


def reference(
    x, w_in, conv_w, dn_a_log, dn_dt_bias, gla_gate_w2, gla_gate_b, dn_norm_g, gla_norm_g,
    w_out, ln_g, ln_b, positions_2, rel_bias_2, norm_gains_2, sb_w_qkv_2, sb_w_o_2, dil_w_qkv_2,
    dil_w_o_2, mla_w_in_2, mla_q_norm_2, mla_w_qb_2, mla_kv_norm_2, mla_w_kvb_2, mla_w_o_2,
    ffn_w_up_2, ffn_conv_w_2, ffn_conv_b_2, ffn_w_down_2,
):
    x = first_block(
        x, w_in, conv_w, dn_a_log, dn_dt_bias, gla_gate_w2, gla_gate_b, dn_norm_g, gla_norm_g,
        w_out, ln_g, ln_b,
    )
    return second_block(
        x, positions_2, rel_bias_2, norm_gains_2, sb_w_qkv_2, sb_w_o_2, dil_w_qkv_2, dil_w_o_2,
        mla_w_in_2, mla_q_norm_2, mla_w_qb_2, mla_kv_norm_2, mla_w_kvb_2, mla_w_o_2, ffn_w_up_2,
        ffn_conv_w_2, ffn_conv_b_2, ffn_w_down_2,
    )


_drawn_inputs = setup_inputs


def setup_inputs(seed=0):
    import zlib

    import numpy as np

    out = dict(_drawn_inputs(seed))
    spreads = {}
    factors = {'gla_gate_b': 3.691, 'dn_norm_g': 7.785, 'gla_norm_g': 8.0}
    for name, (base, spread) in spreads.items():
        noise = np.random.default_rng([zlib.crc32(name.encode()), seed]).standard_normal(out[name].shape)
        drawn = base * np.exp(spread * noise) if base else spread * noise
        out[name] = __import__('jax').numpy.asarray(drawn.astype(out[name].dtype))
    for name, factor in factors.items():
        out[name] = (out[name] * factor).astype(out[name].dtype)
    return out
```

```python
import math
from collections import Counter, namedtuple
from contextlib import ExitStack, contextmanager

import numpy as np
import concourse.bass as bass
from concourse import mybir

F32 = mybir.dt.float32
F32R = mybir.dt.float32r
I32 = mybir.dt.int32
ALU = mybir.AluOpType
ACT = mybir.ActivationFunctionType
AX_X = mybir.AxisListType.X

P = 128
T = 512
D = 1024
KD = D // P
TT = T // P
LAYERS = 2
CHUNK = 2048
NORM_EPS = 1e-6

HEADS = 4
QKV = 12
GLA_SCALE = 64 ** -0.5
GLA_TAU = 16.0
ALPHA = (2.0 * LAYERS) ** 0.25
PROJ_CHUNKS = 14
OUT_CHUNKS = 4
HYBRID_CHUNKS = PROJ_CHUNKS + OUT_CHUNKS

SB_HEADS = 16
SB_CHUNKS = 12
DIL_HEADS = 8
DIL_GROUPS = 3
DIL_RATES = (1, 4, 16)
ORDER = (1, 4, 4)
DIL_CHUNKS = 18
DIL_OUT_CHUNKS = 2
N_BUCKETS = 32
BUCKET_MAX_DIST = 2048
NEG = -1e30
FF = 2816
KF = FF // P
DOWN_CHUNKS = 16
DOWN_BLOCKS = KF // 2

AT_STICK = LAYERS * HYBRID_CHUNKS
AT_STICK_OUT = AT_STICK + SB_CHUNKS
UP_CHUNKS = 2 * KF * P // (2 * P)
AT_DILATED = AT_STICK_OUT + OUT_CHUNKS + UP_CHUNKS
AT_DILATED_OUT = AT_DILATED + DIL_CHUNKS
AT_UP = (AT_STICK_OUT + OUT_CHUNKS, AT_DILATED_OUT + DIL_OUT_CHUNKS)

C_TAP, C_GB, C_DNG, C_GLG, C_LNG, C_LNB, C_ALOG, C_DTB, C_WBA, C_WGR = np.cumsum(
    [0, 4 * QKV, 2, 1, 1, KD, KD, HEADS, HEADS, KD * 8]).tolist()
N_LAYER = C_WGR + KD * 16
C_GAIN, C_FTAP, C_FBIAS = np.cumsum([0, 2 * 4 * KD, 2 * 3 * 2 * KF]).tolist()
N_SECOND = C_FBIAS + 2 * 2 * KF
LEVELS = (1, 2, 4, 8, 16, 32, 64)
K_IDENT, K_ONES, K_INCL, K_STRICT, K_NEGTRI, K_NEGONES, K_FLIP, K_LEVEL = [P * n for n in range(8)]
K_RESET = K_LEVEL + P * len(LEVELS)
K_EPS = K_RESET + T
K_QLN = K_EPS + 1
K_ONE = K_EPS + 2
N_CONST = K_EPS + 3


def level_mask(s):
    j, i = np.meshgrid(np.arange(P), np.arange(P), indexing="ij")
    return ((j // (2 * s) == i // (2 * s)) & (i % (2 * s) >= s) & (j % (2 * s) < s)).astype(np.float32)


def constants():
    c = np.zeros((P, N_CONST), np.float32)
    j, i = np.meshgrid(np.arange(P), np.arange(P), indexing="ij")
    c[:, K_IDENT:K_IDENT + P] = i == j
    c[:, K_ONES:K_ONES + P] = 1
    c[:, K_INCL:K_INCL + P] = j <= i
    c[:, K_STRICT:K_STRICT + P] = j < i
    c[:, K_NEGTRI:K_NEGTRI + P] = -(j >= i).astype(np.float32)
    c[:, K_NEGONES:K_NEGONES + P] = -1
    c[:, K_FLIP:K_FLIP + P] = i + j == P - 1
    for n, s in enumerate(LEVELS):
        c[:, K_LEVEL + P * n:K_LEVEL + P * (n + 1)] = level_mask(s)
    c[:, K_RESET:K_RESET + T] = np.arange(T) % P != 0
    c[:, K_EPS] = NORM_EPS
    c[:, K_QLN] = -0.5 * math.log(P)
    c[:, K_ONE] = 1
    return c


def named(**things):
    return namedtuple("Named", things)(**things)


class Shared:
    pass


NAMES = Counter()


def sbuf(nc, name, shape, dtype):
    NAMES[name] += 1
    return nc.sbuf_tensor(f"{name}_{NAMES[name]}", shape, dtype)


@contextmanager
def phase(nc, *names):
    with ExitStack() as stack:
        sems = {n: stack.enter_context(nc.semaphore(n)) for n in names}
        yield named(**sems)
        with nc.Block() as block:
            @block.sync
            def _(sp):
                for s in sems.values():
                    sp.sem_clear(s)


def groups(eng, first, end, total, body):
    if first == 0:
        body(0)
        first = 1
    last = end == total and total > 1
    end -= last
    if end - first == 1:
        body(first)
    elif end > first:
        with eng.Fori(first, end) as i:
            body(i)
    if last:
        body(total - 1)


def static(i):
    return isinstance(i, int)


class Stream:

    def __init__(self, k, weights, base, chunks, cols, pieces, inputs, source):
        self.raw, self.whi, self.wlo = k.raw, k.whi, k.wlo
        self.landed = k.landed
        self.weights, self.base, self.chunks, self.cols = weights, base, chunks, cols
        self.pieces = pieces
        self.inputs, self.source = inputs, source
        self.ahi, self.alo = k.ahi, k.alo
        self.k = k

    def load(self, sp, s):
        def body(i):
            for u in range(2):
                c = 2 * i + u
                sp.wait_ge(s.split, c - 1)
                sp.dma_start(self.raw[:, u, 0:self.cols], self.weights[self.base + c]).then_inc(self.landed[u], 16)
        n = self.chunks // 2
        if n == 2:
            body(1)
        elif n > 2:
            with sp.Fori(1, n) as i:
                body(i)

    def input_high(self, act, s):
        for k in range(self.inputs):
            act.copy(self.ahi[:, k], self.source[:, k]).then_inc(s.in_hi, 1)

    def high(self, act, s, c, u):
        act.wait_ge(self.landed[u], 8 * (c - u) + 16)
        if not (static(c) and c < 2):
            act.wait_ge(s.made, self.pieces * (c - 1))
        act.copy(self.whi[:, u, 0:self.cols], self.raw[:, u, 0:self.cols]).then_inc(s.high, 1)

    def input_low(self, dve, s):
        for k in range(self.inputs):
            dve.wait_ge(s.in_hi, k + 1)
            dve.tensor_tensor(self.alo[:, k], self.source[:, k], self.ahi[:, k].bitcast(F32),
                              ALU.subtract).then_inc(s.in_lo, 1)

    def low(self, dve, s, c, u):
        dve.wait_ge(s.high, c + 1)
        dve.tensor_tensor(self.wlo[:, u, 0:self.cols], self.raw[:, u, 0:self.cols],
                          self.whi[:, u, 0:self.cols].bitcast(F32), ALU.subtract).then_inc(s.split, 1)

    def block(self, u, b):
        return self.whi[:, u, b * P:(b + 1) * P], self.wlo[:, u, b * P:(b + 1) * P]

    def feature_tile(self, pe, out, u, block0, blocks, k0, start, stop):
        for b in range(blocks):
            hi, lo = self.block(u, block0 + b)
            k = k0 + b
            pe.matmul(out, hi, self.ahi[:, k], start=start and b == 0, stop=False)
            pe.matmul(out, hi, self.alo[:, k], start=False, stop=False)
            mm = pe.matmul(out, lo, self.ahi[:, k], start=False, stop=stop and b == blocks - 1)
        return mm

    def token_tile(self, pe, out, u, t, tokens=None):
        w = [x[:, u, :].rearrange("p (k n) -> p k n", n=2 * P) for x in (self.whi, self.wlo)]
        for k in range(KD):
            a = [tokens(x[:, k], t) if tokens else x[:, k, t * P:(t + 1) * P] for x in (self.ahi, self.alo)]
            pe.matmul(out, a[0], w[0][:, k], start=k == 0, stop=False)
            pe.matmul(out, a[1], w[0][:, k], start=False, stop=False)
            mm = pe.matmul(out, a[0], w[1][:, k], start=False, stop=k == KD - 1)
        return mm

    def products(self, pe, s, i, ps, kind, freed=None, per_tile=1, tokens=None):
        for u in range(2):
            pe.wait_ge(s.split, 2 * i + u + 1)
            for n in range(2):
                tile = 4 * i + 2 * u + n
                if not (static(i) and i == 0):
                    pe.wait_ge(freed or s.freed, per_tile * (tile - 3))
                out = ps[:, 2 * u + n]
                if kind == "feature":
                    self.feature_tile(pe, out, u, KD * n, KD, 0, True, True).then_inc(s.made, 1)
                else:
                    self.token_tile(pe, out[:, 0:2 * P], u, 2 * n, tokens)
                    self.token_tile(pe, out[:, 2 * P:], u, 2 * n + 1, tokens).then_inc(s.made, 1)


GEMM = ("split", "in_hi", "in_lo", "high", "made", "freed")


@contextmanager
def operands(nc, k, inputs, cols=CHUNK):
    with ExitStack() as stack:
        k.whi = stack.enter_context(sbuf(nc, "weights_high", [P, 2, cols], F32R))
        k.wlo = stack.enter_context(sbuf(nc, "weights_low", [P, 2, cols], F32R))
        k.ahi = stack.enter_context(sbuf(nc, "inputs_high", [P, inputs, T], F32R))
        k.alo = stack.enter_context(sbuf(nc, "inputs_low", [P, inputs, T], F32R))
        yield


def prefetch(nc, k, weights, index, cols):
    with nc.Block() as block:
        @block.sync
        def _(sp):
            for u in range(2):
                sp.sem_clear(k.landed[u])
            for u in range(2):
                sp.dma_start(k.raw[:, u, 0:cols], weights[index + u]).then_inc(k.landed[u], 16)



def hybrid_projections(nc, k, layer, h):
    ps, par = k.ps, h.par
    taps = par[:, C_TAP:C_TAP + 4 * QKV].rearrange("p (w c a) -> p w c a", w=4, a=1)
    n_groups = PROJ_CHUNKS // 2
    with operands(nc, k, KD), ExitStack() as stack, \
            phase(nc, *GEMM, "tap", "conv", "small", "small_out") as s:
        y = stack.enter_context(sbuf(nc, "conv", [P, 4, T], F32))
        st = Stream(k, k.w_stream, layer * HYBRID_CHUNKS, PROJ_CHUNKS, CHUNK, 2, KD, k.x)
        with nc.Block() as block:
            @block.sync
            def _(sp):
                st.load(sp, s)

            @block.tensor
            def _(pe):
                pe.wait_ge(s.in_lo, KD)
                groups(pe, 0, 6, n_groups, lambda i: st.products(pe, s, i, ps, "feature"))
                st.products(pe, s, 6, ps, "token")
                for t in range(TT):
                    for kk in range(KD):
                        pe.matmul(ps[:, 4, t * 8:t * 8 + 8], k.x[:, kk, t * P:(t + 1) * P],
                                  par[:, C_WBA + kk * 8:C_WBA + kk * 8 + 8], start=kk == 0, stop=kk == KD - 1)
                for kk in range(KD):
                    mm = pe.matmul(ps[0:16, 5], par[:, C_WGR + kk * 16:C_WGR + kk * 16 + 16], k.x[:, kk],
                                   start=kk == 0, stop=kk == KD - 1)
                mm.then_inc(s.small, 1)

            @block.scalar
            def _(act):
                st.input_high(act, s)
                st.high(act, s, 0, 0)

                def convolved(i):
                    for u in range(2):
                        st.high(act, s, 2 * i + u + 1, 1 - u)
                        for n in range(2):
                            b = 2 * u + n
                            tile = 4 * i + b
                            act.wait_ge(s.made, tile + 1)
                            if not (static(i) and i == 0):
                                act.wait_ge(s.freed, tile - 3)
                            act.mul(y[:, b], ps[:, b], taps[:, 3, tile]).then_inc(s.tap, 1)
                        for n in range(2):
                            b = 2 * u + n
                            tile = 4 * i + b
                            act.wait_ge(s.conv, 3 * tile + 3)
                            act.activation(h.qkv[:, tile], y[:, b], ACT.Silu).then_inc(s.freed, 1)

                def gated(i):
                    for u in range(2):
                        st.high(act, s, 2 * i + u + 1, 1 - u)
                        for n in range(2):
                            tile = 4 * i + 2 * u + n
                            act.wait_ge(s.made, tile + 1)
                            act.activation(h.z[:, tile - QKV], ps[:, 2 * u + n], ACT.Silu).then_inc(s.freed, 1)

                def gla_qk(i):
                    for u in range(2):
                        st.high(act, s, 2 * i + u + 1, 1 - u)
                        for n in range(2):
                            act.wait_ge(s.made, 4 * i + 2 * u + n + 1)
                            act.mul(h.gqk[:, 2 * u + n], ps[:, 2 * u + n],
                                    GLA_SCALE if u == 0 else 1.0).then_inc(s.freed, 1)

                def gla_v(i):
                    for u in range(2):
                        if u == 0:
                            st.high(act, s, 2 * i + 1, 1)
                        for n in range(2):
                            act.wait_ge(s.made, 4 * i + 2 * u + n + 1)
                            act.copy(h.gv[:, 2 * n:2 * n + 2, u * 2 * P:(u + 1) * 2 * P],
                                     ps[:, 2 * u + n].rearrange("p (t n) -> p t n", t=2)).then_inc(s.freed, 1)
                groups(act, 0, 3, n_groups, convolved)
                groups(act, 3, 5, n_groups, gated)
                gla_qk(5)
                gla_v(6)
                act.wait_ge(s.small, 1)
                act.copy(h.ba[:], ps[:, 4, 0:TT * 8]).then_inc(s.small_out, 1)
                act.copy(h.gr[0:16, :], ps[0:16, 5]).then_inc(s.small_out, 1)

            @block.vector
            def _(dve):
                st.input_low(dve, s)
                st.low(dve, s, 0, 0)

                def convolved(i):
                    for u in range(2):
                        st.low(dve, s, 2 * i + u + 1, 1 - u)
                        for n in range(2):
                            b = 2 * u + n
                            tile = 4 * i + b
                            dve.wait_ge(s.tap, tile + 1)
                            for back in (1, 2, 3):
                                if back > 1:
                                    dve.wait_ge(s.conv, 3 * tile + back - 1)
                                ins = dve.scalar_tensor_tensor(
                                    y[:, b, back:], ps[:, b, 0:T - back], taps[:, 3 - back, tile],
                                    y[:, b, back:], ALU.mult, ALU.add)
                                ins.then_inc(s.conv, 1)

                def others(i):
                    for u in range(2):
                        st.low(dve, s, 2 * i + u + 1, 1 - u)
                groups(dve, 0, 3, n_groups, convolved)
                groups(dve, 3, 6, n_groups, others)
                st.low(dve, s, 2 * n_groups - 1, 1)


def delta_gates(nc, k, h, a):
    ps, par, con = k.ps, h.par, k.con
    ones, ident, incl = con[:, K_ONES:K_ONES + P], con[:, K_IDENT:K_IDENT + P], con[:, K_INCL:K_INCL + P]
    strict = con[:, K_STRICT:K_STRICT + P]
    q, kk, v = h.qkv[:, 0:4], h.qkv[:, 4:8], h.qkv[:, 8:12]
    with ExitStack() as stack, phase(
            nc, "square", "square_sum", "inv_ln", "inv_norm", "normed", "gate_act", "gate_dve", "g_ready", "gcol_sum",
            "gcol", "spread", "row", "row_exp", "diff", "row_read", "decay", "masked", "kb", "scaled", "turned", "turned_read",
            "last_arg", "last_exp", "pair", "pair_read") as s:
        def sb(name, shape):
            return stack.enter_context(sbuf(nc, name, shape, F32))
        sq = sb("squares", [P, 2, T])
        inv = sb("inverse_norm", [P, 2, T])
        gt = sb("gate_steps", [P, 8, 16])
        beta = sb("beta", [P, TT, HEADS])
        g = sb("log_decay", [P, TT, HEADS])
        gcol = sb("g_column", [P, TT, HEADS])
        spread = sb("spread", [P, 2, TT, P])
        erow = sb("exp_g_row", [P, HEADS, T])
        decay = sb("decay", [P, TT, HEADS, P])
        kb = sb("k_beta", [P, HEADS, T])
        last = sb("to_last", [P, 2, HEADS, TT])
        ba = h.ba[:].rearrange("p (t c) -> p t c", t=TT)

        def b16(n):
            return gt[:, n].rearrange("p (t h) -> p t h", t=TT)

        with nc.Block() as block:
            @block.scalar
            def _(act):
                act.activation(b16(0), ba[:, :, 0:HEADS], ACT.Exp, scale=-1.0).then_inc(s.gate_act, 1)
                act.activation(gt[:, 7, 0:HEADS], par[:, C_ALOG:C_ALOG + HEADS], ACT.Exp).then_inc(s.gate_act, 1)
                act.wait_ge(s.gate_dve, 1)
                act.activation(b16(2), b16(1), ACT.Abs).then_inc(s.gate_act, 1)
                act.wait_ge(s.gate_act, 3)
                act.activation(b16(3), b16(2), ACT.Exp, scale=-1.0).then_inc(s.gate_act, 1)
                act.wait_ge(s.gate_act, 4)
                act.activation(b16(4), b16(3), ACT.Ln, bias=con[:, K_ONE:K_ONE + 1]).then_inc(s.gate_act, 1)
                for j in range(9):
                    if j < 8:
                        if j >= 2:
                            act.wait_ge(s.square_sum, j - 1)
                        act.activation(sq[:, j % 2], h.qkv[:, j], ACT.Square).then_inc(s.square, 1)
                    if j >= 1:
                        n = j - 1
                        act.wait_ge(s.square_sum, n + 1)
                        if n >= 2:
                            act.wait_ge(s.normed, n - 1)
                        act.activation(inv[:, n % 2], ps[:, 4 + n % 2], ACT.Ln,
                                       bias=con[:, K_EPS:K_EPS + 1]).then_inc(s.inv_ln, 1)
                        act.wait_ge(s.inv_ln, n + 1)
                        if n < HEADS:
                            act.activation(inv[:, n % 2], inv[:, n % 2], ACT.Exp, scale=-0.5,
                                           bias=con[:, K_QLN:K_QLN + 1]).then_inc(s.inv_norm, 1)
                        else:
                            act.activation(inv[:, n % 2], inv[:, n % 2], ACT.Exp, scale=-0.5).then_inc(s.inv_norm, 1)
                for n in range(HEADS):
                    act.wait_ge(s.row, 2 * n + 1)
                    act.activation(erow[:, n], ps[:, (2 * n) % 4], ACT.Exp).then_inc(s.row_exp, 1)
                    act.wait_ge(s.diff, 4 * n + 4)
                    act.activation(decay[:, :, n], decay[:, :, n], ACT.Exp).then_inc(s.decay, 1)
                act.wait_ge(s.last_arg, HEADS)
                act.activation(last[:, 1], last[:, 0], ACT.Exp).then_inc(s.last_exp, 1)

            @block.vector
            def _(dve):
                dtb = par[:, C_DTB:C_DTB + HEADS].unsqueeze(1).to_broadcast([P, TT, HEADS])
                dve.tensor_tensor(b16(1), ba[:, :, HEADS:], dtb, ALU.add).then_inc(s.gate_dve, 1)
                dve.wait_ge(s.gate_act, 1)
                dve.tensor_scalar(b16(5), b16(0), 1.0, None, ALU.add).then_inc(s.gate_dve, 1)
                dve.wait_ge(s.gate_dve, 2)
                dve.reciprocal(beta[:], b16(5)).then_inc(s.gate_dve, 1)
                dve.wait_ge(s.gate_act, 5)
                dve.scalar_tensor_tensor(b16(6), b16(1), 0.0, b16(4), ALU.max, ALU.add).then_inc(s.gate_dve, 1)
                dve.wait_ge(s.gate_dve, 4)
                rate = gt[:, 7, 0:HEADS].unsqueeze(1).to_broadcast([P, TT, HEADS])
                dve.scalar_tensor_tensor(g[:], b16(6), -1.0, rate, ALU.mult, ALU.mult).then_inc(s.g_ready, 1)
                dve.wait_ge(s.gcol_sum, 1)
                dve.tensor_copy(gcol[:], ps[:, 6, 0:16].rearrange("p (t h) -> p t h", t=TT)).then_inc(s.gcol, 1)
                for j in range(8):
                    dve.wait_ge(s.inv_norm, j + 1)
                    dve.tensor_tensor(h.qkv[:, j], h.qkv[:, j], inv[:, j % 2], ALU.mult).then_inc(s.normed, 1)
                dve.wait_ge(s.gcol, 1)
                for n in range(HEADS):
                    row = ps[:, (2 * n) % 4].rearrange("p (t i) -> p t i", t=TT)
                    dve.wait_ge(s.row_exp, n + 1)
                    for t in range(TT):
                        dve.tensor_scalar(decay[:, t, n], row[:, t], gcol[:, t, n:n + 1], 0.0,
                                          ALU.subtract, ALU.min).then_inc(s.diff, 1)
                    dve.tensor_tensor(last[:, 0, n], row[:, :, P - 1], gcol[:, :, n], ALU.subtract).then_inc(s.last_arg, 1)
                    dve.wait_ge(s.row, 2 * n + 2)
                    dve.wait_ge(s.normed, 4 + n + 1)
                    dve.tensor_tensor(kb[:, n], kk[:, n], ps[:, (2 * n + 1) % 4], ALU.mult).then_inc(s.kb, 1)
                for n in range(2 * HEADS):
                    hd = n % HEADS
                    dve.wait_ge(s.turned, n + 1)
                    if n == HEADS:
                        dve.wait_ge(s.last_exp, 1)
                    src = ps[:, 6 + n % 2].rearrange("p (t e) -> p t e", t=TT)
                    col = beta[:, :, hd] if n < HEADS else last[:, 1, hd]
                    dst = a.vb if n < HEADS else a.kdec
                    dve.tensor_tensor(dst[:, :, hd], src, col.unsqueeze(2).to_broadcast([P, TT, P]),
                                      ALU.mult).then_inc(s.turned_read, 1)
                for n in range(2 * TT):
                    t = n % TT
                    dve.wait_ge(s.pair, n + 1)
                    if n % TT == 0:
                        dve.wait_ge(s.masked, 2 if n == 0 else 1)
                    dst = a.at if n < TT else a.attn
                    dve.tensor_tensor(dst[:, t], ps[:, n % 2].rearrange("p (h i) -> p h i", h=HEADS),
                                      (decay if n < TT else a.inv_t)[:, t], ALU.mult).then_inc(s.pair_read, 1)

            @block.gpsimd
            def _(pool):
                pool.wait_ge(s.gate_dve, 3)
                pool.wait_ge(s.g_ready, 1)
                for n in range(2 * HEADS):
                    if n >= 2:
                        pool.wait_ge(s.row, n - 1)
                    base, col = (incl, g) if n % 2 == 0 else (ident, beta)
                    pool.tensor_tensor(spread[:, n % 2], base.unsqueeze(1).to_broadcast([P, TT, P]),
                                       col[:, :, n // 2].unsqueeze(2).to_broadcast([P, TT, P]),
                                       ALU.mult).then_inc(s.spread, 1)
                for n in range(HEADS):
                    pool.wait_ge(s.kb, n + 1)
                    pool.wait_ge(s.row_exp, n + 1)
                    pool.tensor_tensor(a.kbg[:, n], kb[:, n], erow[:, n], ALU.mult).then_inc(s.scaled, 1)
                    pool.wait_ge(s.normed, n + 1)
                    pool.tensor_tensor(a.qg[:, n], q[:, n], erow[:, n], ALU.mult).then_inc(s.scaled, 1)
                    pool.tensor_copy(a.elast[:, n], erow[:, n].rearrange("p (t i) -> p t i", t=TT)[:, :, P - 1]) \
                        .then_inc(s.scaled, 1)
                pool.wait_ge(s.decay, HEADS)
                flat = decay[:].rearrange("p t h i -> p (t h) i")
                pool.tensor_tensor(a.inv_t[:].rearrange("p t h i -> p (t h) i"), flat,
                                   incl.unsqueeze(1).to_broadcast([P, 16, P]), ALU.mult).then_inc(s.masked, 1)
                pool.wait_ge(s.masked, 1)
                pool.tensor_tensor(flat, flat, strict.unsqueeze(1).to_broadcast([P, 16, P]), ALU.mult) \
                    .then_inc(s.masked, 1)

            @block.tensor
            def _(pe):
                pe.wait_ge(s.g_ready, 1)
                pe.matmul(ps[:, 6, 0:16], incl, g[:].rearrange("p t h -> p (t h)"), start=True, stop=True) \
                    .then_inc(s.gcol_sum, 1)
                for j in range(8):
                    pe.wait_ge(s.square, j + 1)
                    if j >= 2:
                        pe.wait_ge(s.inv_ln, j - 1)
                    pe.matmul(ps[:, 4 + j % 2], ones, sq[:, j % 2], start=True, stop=True).then_inc(s.square_sum, 1)
                for n in range(2 * HEADS):
                    pe.wait_ge(s.spread, n + 1)
                    if n >= 4:
                        pe.wait_ge(s.kb, (n - 4) // 2 + 1)
                        pe.wait_ge(s.last_arg, (n - 4) // 2 + 1)
                    pe.matmul(ps[:, n % 4], ones, spread[:, n % 2].rearrange("p t i -> p (t i)"),
                              start=True, stop=True).then_inc(s.row, 1)
                pe.wait_ge(s.gcol, 1)
                for n in range(2 * HEADS):
                    src = v if n < HEADS else kk
                    if n >= 2:
                        pe.wait_ge(s.turned_read, n - 1)
                    if n >= HEADS:
                        pe.wait_ge(s.normed, n + 1)
                    for t in range(TT):
                        mm = pe.transpose(ps[:, 6 + n % 2, t * P:(t + 1) * P],
                                          src[:, n % HEADS, t * P:(t + 1) * P], ident)
                    mm.then_inc(s.turned, 1)
                pe.wait_ge(s.kb, HEADS)
                for n in range(2 * TT):
                    cols = slice((n % TT) * P, (n % TT + 1) * P)
                    if n >= 2:
                        pe.wait_ge(s.pair_read, n - 1)
                    for hd in range(HEADS):
                        mm = pe.matmul(ps[:, n % 2, hd * P:(hd + 1) * P], kk[:, hd, cols],
                                       (kb if n < TT else q)[:, hd, cols], start=True, stop=True)
                    mm.then_inc(s.pair, 1)


def delta_solve(nc, k, a):
    ps, con = k.ps, k.con
    ident = con[:, K_IDENT:K_IDENT + P]
    with ExitStack() as stack, phase(nc, "coupling", "first", "first_inv", "left", "left_copy", "both", "inv", "inv_t") as s:
        x = stack.enter_context(sbuf(nc, "inverse", [P, TT, HEADS, P], F32))
        ct = stack.enter_context(sbuf(nc, "coupling", [P, TT, HEADS, P], F32))
        cx = stack.enter_context(sbuf(nc, "coupled", [P, TT, HEADS, P], F32))
        xt = a.inv_t
        n_levels = len(LEVELS)

        def bank(n):
            return ps[:, n].rearrange("p (h i) -> p h i", h=HEADS)

        def identity():
            return ident.unsqueeze(1).to_broadcast([P, HEADS, P])

        with nc.Block() as block:
            @block.gpsimd
            def _(pool):
                def level(n):
                    mask = con[:, K_LEVEL + P * n:K_LEVEL + P * (n + 1)].unsqueeze(1).to_broadcast([P, HEADS, P])
                    for t in range(TT):
                        if n:
                            pool.wait_ge(s.left, 4 * (n - 1) + t + 1)
                            pool.wait_ge(s.inv_t, t + 1)
                        pool.tensor_tensor(ct[:, t], a.at[:, t], mask, ALU.mult).then_inc(s.coupling, 1)
                for n in range(n_levels):
                    level(n)

            @block.tensor
            def _(pe):
                for t in range(TT):
                    pe.wait_ge(s.coupling, t + 1)
                    for hd in range(HEADS):
                        mm = pe.matmul(ps[:, t, hd * P:(hd + 1) * P], ct[:, t, hd], ident, start=True, stop=True)
                    mm.then_inc(s.left, 1)
                with pe.Fori(1, n_levels) as n:
                    for t in range(TT):
                        pe.wait_ge(s.coupling, 4 * n + t + 1)
                        pe.wait_ge(s.inv, 4 * (n - 1) + t + 1)
                        for hd in range(HEADS):
                            mm = pe.matmul(ps[:, t, hd * P:(hd + 1) * P], ct[:, t, hd], x[:, t, hd],
                                           start=True, stop=True)
                        mm.then_inc(s.left, 1)
                    for t in range(TT):
                        pe.wait_ge(s.left_copy, 4 * (n - 1) + t + 1)
                        pe.wait_ge(s.inv, 4 * n + t - 1)
                        pe.wait_ge(s.inv_t, 4 * n + t - 1)
                        for hd in range(HEADS):
                            pe.matmul(ps[:, 4 + t % 2, hd * P:(hd + 1) * P], xt[:, t, hd], cx[:, t, hd],
                                      start=True, stop=True)
                        for hd in range(HEADS):
                            mm = pe.matmul(ps[:, 6 + t % 2, hd * P:(hd + 1) * P], cx[:, t, hd], xt[:, t, hd],
                                           start=True, stop=True)
                        mm.then_inc(s.both, 1)

            @block.scalar
            def _(act):
                with act.Fori(1, n_levels) as n:
                    for t in range(TT):
                        act.wait_ge(s.left, 4 * n + t + 1)
                        act.copy(cx[:, t], bank(t)).then_inc(s.left_copy, 1)

            @block.vector
            def _(dve):
                for t in range(TT):
                    dve.wait_ge(s.left, t + 1)
                    dve.tensor_tensor(x[:, t], identity(), bank(t), ALU.subtract).then_inc(s.inv, 1)
                    dve.tensor_tensor(xt[:, t], identity(), ct[:, t], ALU.subtract).then_inc(s.inv_t, 1)
                with dve.Fori(1, n_levels) as n:
                    for t in range(TT):
                        dve.wait_ge(s.both, 4 * (n - 1) + t + 1)
                        dve.tensor_tensor(x[:, t], x[:, t], bank(4 + t % 2), ALU.subtract).then_inc(s.inv, 1)
                        dve.tensor_tensor(xt[:, t], xt[:, t], bank(6 + t % 2), ALU.subtract).then_inc(s.inv_t, 1)


def delta_scan(nc, k, h, a):
    ps = k.ps
    with ExitStack() as stack, phase(nc, "zero", "carried", "rest", "solved", "values", "out", "out_copy", "added", "state") as s:
        st = stack.enter_context(sbuf(nc, "state", [P, HEADS, P], F32))
        z = stack.enter_context(sbuf(nc, "rest", [P, HEADS, P], F32))
        vn = stack.enter_context(sbuf(nc, "new_values", [P, HEADS, P], F32))

        def bank(n):
            return ps[:, n].rearrange("p (h i) -> p h i", h=HEADS)

        with nc.Block() as block:
            @block.tensor
            def _(pe):
                pe.wait_ge(s.zero, 1)
                for t in range(TT):
                    cols = slice(t * P, (t + 1) * P)
                    if t >= 1:
                        pe.wait_ge(s.state, 4 * t)
                    for hd in range(HEADS):
                        mm = pe.matmul(bank(0)[:, hd], a.kbg[:, hd, cols], st[:, hd], start=True, stop=True)
                    mm.then_inc(s.carried, 1)
                    pe.wait_ge(s.rest, t + 1)
                    for hd in range(HEADS):
                        mm = pe.matmul(bank(1)[:, hd], a.inv_t[:, t, hd], z[:, hd], start=True, stop=True)
                    mm.then_inc(s.solved, 1)
                    pe.wait_ge(s.values, t + 1)
                    for hd in range(HEADS):
                        mm = pe.matmul(bank(2)[:, hd], a.kdec[:, t, hd], vn[:, hd], start=True, stop=True)
                    mm.then_inc(s.added, 1)
                    if t >= 1:
                        pe.wait_ge(s.out_copy, t)
                    for hd in range(HEADS):
                        pe.matmul(bank(3)[:, hd], st[:, hd], a.qg[:, hd, cols], start=True, stop=False)
                        mm = pe.matmul(bank(3)[:, hd], vn[:, hd], a.attn[:, t, hd], start=False, stop=True)
                    mm.then_inc(s.out, 1)

            @block.vector
            def _(dve):
                dve.memset(st[:], 0.0).then_inc(s.zero, 1)
                for t in range(TT):
                    dve.wait_ge(s.carried, t + 1)
                    dve.tensor_tensor(z[:], a.vb[:, t], bank(0), ALU.subtract).then_inc(s.rest, 1)
                    dve.wait_ge(s.added, t + 1)
                    dve.wait_ge(s.out, t + 1)
                    for hd in range(HEADS):
                        dve.scalar_tensor_tensor(st[:, hd], st[:, hd], a.elast[:, hd, t:t + 1], bank(2)[:, hd],
                                                 ALU.mult, ALU.add).then_inc(s.state, 1)

            @block.scalar
            def _(act):
                for t in range(TT):
                    act.wait_ge(s.solved, t + 1)
                    if t >= 1:
                        act.wait_ge(s.out, t)
                    act.copy(vn[:], bank(1)).then_inc(s.values, 1)
                    act.wait_ge(s.out, t + 1)
                    act.copy(h.qkv[:, 0:HEADS, t * P:(t + 1) * P], bank(3)).then_inc(s.out_copy, 1)


def gla_prepare(nc, k, h, a):
    ps, con, par = k.ps, k.con, h.par
    ident = con[:, K_IDENT:K_IDENT + P]
    reset = con[:, K_RESET:K_RESET + T]
    one = con[:, K_ONE:K_ONE + 1]
    n_levels = len(LEVELS)
    with ExitStack() as stack, phase(
            nc, "logits", "act_step", "log_f", "sums", "filled", "slot_filled", "apart", "falls", "scaled", "pair", "taken",
            "end_arg", "end_exp", "k_end", "turned", "turned_read") as s:
        def sb(name, shape):
            return stack.enter_context(sbuf(nc, name, shape, F32))
        lx = sb("gate_logits", [P, 2, T])
        la = sb("gate_steps", [P, 2, T])
        bsum = sb("b_sums", [P, 2, T])
        fall = sb("falls", [P, 2, 2, T])
        qs = sb("q_level", [P, 2, 2, T])
        ks = sb("k_level", [P, 2, 2, T])
        kend = sb("k_to_end", [P, 2, T])
        q, kk = h.gqk[:, 0:2], h.gqk[:, 2:4]
        cq = [x.rearrange("p f (t i) -> p (f t) i", i=P) for x in (bsum[:], kend[:])]

        def halves(x, size):
            v = x.rearrange("p f (b i) -> p (f b) i", i=2 * size)
            return v[:, :, 0:size], v[:, :, size:]

        def bank(n):
            return ps[:, n].rearrange("p (h i) -> p h i", h=HEADS)

        with nc.Block() as block:
            @block.tensor
            def _(pe):
                for f in range(2):
                    mm = pe.matmul(ps[:, f], h.w2[0:16, f * P:(f + 1) * P], h.gr[0:16, :], start=True, stop=True)
                mm.then_inc(s.logits, 1)
                for n in range(n_levels + 1):
                    if n:
                        pe.wait_ge(s.scaled, 2 * n)
                    for t in range(TT):
                        b = 2 + 2 * ((4 * n + t) % 3)
                        if 4 * n + t >= 3:
                            pe.wait_ge(s.taken, 4 * n + t - 2)
                        cols = slice(t * P, (t + 1) * P)
                        for hd in range(HEADS):
                            rows = slice(64 * (hd % 2), 64 * (hd % 2) + 64)
                            ka = ks[rows, (n - 1) % 2, hd // 2, cols] if n else kk[rows, hd // 2, cols]
                            qa = qs[rows, (n - 1) % 2, hd // 2, cols] if n else q[rows, hd // 2, cols]
                            mm = pe.matmul(bank(b + hd % 2)[:, hd // 2], ka, qa, start=True, stop=True)
                        mm.then_inc(s.pair, 1)
                pe.wait_ge(s.k_end, 1)
                for f in range(2):
                    for t in range(TT):
                        mm = pe.transpose(ps[:, f, t * P:(t + 1) * P], kend[:, f, t * P:(t + 1) * P], ident)
                    mm.then_inc(s.turned, 1)

            @block.scalar
            def _(act):
                act.wait_ge(s.logits, 1)
                for f in range(2):
                    act.activation(lx[:, f], ps[:, f], ACT.Identity, bias=par[:, C_GB + f:C_GB + f + 1]) \
                        .then_inc(s.act_step, 1)
                act.wait_ge(s.act_step, 2)
                act.activation(la[:], lx[:], ACT.Abs).then_inc(s.act_step, 1)
                act.wait_ge(s.act_step, 3)
                act.activation(la[:], la[:], ACT.Exp, scale=-1.0).then_inc(s.act_step, 1)
                act.wait_ge(s.act_step, 4)
                act.activation(la[:], la[:], ACT.Ln, bias=one).then_inc(s.act_step, 1)
                for n in range(n_levels):
                    act.wait_ge(s.apart, 2 * n + 2)
                    act.activation(fall[:, n % 2], fall[:, n % 2], ACT.Exp).then_inc(s.falls, 1)
                act.wait_ge(s.sums, 2)
                act.activation(a.q_sum[:], bsum[:], ACT.Exp).then_inc(s.end_exp, 1)
                act.wait_ge(s.end_arg, 1)
                act.activation(kend[:], kend[:], ACT.Exp).then_inc(s.end_exp, 1)
                act.activation(a.f_last[:], cq[0][:, :, P - 1].rearrange("p (f t) -> p f t", f=2), ACT.Exp) \
                    .then_inc(s.end_exp, 1)
                for f in range(2):
                    act.wait_ge(s.turned, f + 1)
                    act.copy(a.k_end[:, :, f], ps[:, f].rearrange("p (t d) -> p t d", t=TT)).then_inc(s.turned_read, 1)

            @block.vector
            def _(dve):
                dve.memset(a.scores[:], 0.0).then_inc(s.filled, 1)
                dve.wait_ge(s.act_step, 5)
                dve.scalar_tensor_tensor(lx[:], lx[:], 0.0, la[:], ALU.min, ALU.subtract).then_inc(s.log_f, 1)
                dve.wait_ge(s.log_f, 1)
                dve.tensor_scalar(lx[:], lx[:], 1.0 / GLA_TAU, None, ALU.mult).then_inc(s.log_f, 1)
                dve.wait_ge(s.log_f, 2)
                for f in range(2):
                    dve.tensor_tensor_scan(bsum[:, f], reset, lx[:, f], 0.0, ALU.mult, ALU.add).then_inc(s.sums, 1)
                dve.wait_ge(s.sums, 2)
                dve.wait_ge(s.filled, 1)

                def take(n):
                    mask = (con[:, K_LEVEL + P * (n - 1):K_LEVEL + P * n] if n else ident).bitcast(I32)
                    for t in range(TT):
                        dve.wait_ge(s.pair, 4 * n + t + 1)
                        if n:
                            dve.wait_ge(s.taken, 4 * (n - 1) + t + 1)
                        b = 2 + 2 * ((4 * n + t) % 3)
                        dve.copy_predicated(a.scores[:, t].rearrange("p (y f) i -> p y f i", y=2),
                                            mask.unsqueeze(1).unsqueeze(1).to_broadcast([P, 2, 2, P]),
                                            ps[:, b:b + 2, 0:2 * P].rearrange("p y (f i) -> p y f i", f=2)) \
                            .then_inc(s.taken, 1)
                for n, size in enumerate(LEVELS):
                    low, up = halves(bsum[:], size)
                    fl, fu = halves(fall[:, n % 2], size)
                    middle = low[:, :, size - 1:size].to_broadcast([P, 2 * T // (2 * size), size])
                    if n >= 2:
                        dve.wait_ge(s.scaled, 2 * n - 2)
                    dve.tensor_tensor(fl, middle, low, ALU.subtract).then_inc(s.apart, 1)
                    dve.tensor_tensor(fu, up, middle, ALU.subtract).then_inc(s.apart, 1)
                    take(n)
                take(n_levels)
                dve.tensor_tensor(cq[1], cq[0][:, :, P - 1:P].to_broadcast([P, 8, P]), cq[0],
                                  ALU.subtract).then_inc(s.end_arg, 1)
                dve.wait_ge(s.end_exp, 2)
                dve.tensor_tensor(kend[:], kend[:], kk, ALU.mult).then_inc(s.k_end, 1)
                dve.tensor_tensor(a.q_sum[:], a.q_sum[:], q, ALU.mult).then_inc(s.end_arg, 1)

            @block.gpsimd
            def _(pool):
                for n, size in enumerate(LEVELS):
                    slot = n % 2
                    pool.wait_ge(s.falls, n + 1)
                    if n >= 2:
                        pool.wait_ge(s.pair, 4 * n)
                    else:
                        pool.tensor_copy(qs[:, slot], q).then_inc(s.slot_filled, 1)
                        pool.tensor_copy(ks[:, slot], kk).then_inc(s.slot_filled, 1)
                        pool.wait_ge(s.slot_filled, 2 * (n + 1))
                    _, qu = halves(q, size)
                    kl, _ = halves(kk, size)
                    fl, fu = halves(fall[:, slot], size)
                    pool.tensor_tensor(halves(qs[:, slot], size)[1], qu, fu, ALU.mult).then_inc(s.scaled, 1)
                    pool.tensor_tensor(halves(ks[:, slot], size)[0], kl, fl, ALU.mult).then_inc(s.scaled, 1)


def gla_scan(nc, k, h, a):
    ps = k.ps
    with ExitStack() as stack, phase(nc, "zero", "out", "out_copy", "added", "state") as s:
        st = stack.enter_context(sbuf(nc, "gla_state", [P, HEADS, P], F32))

        def bank(n):
            return ps[:, n].rearrange("p (h i) -> p h i", h=HEADS)

        with nc.Block() as block:
            @block.tensor
            def _(pe):
                pe.wait_ge(s.zero, 1)
                for t in range(TT):
                    cols = slice(t * P, (t + 1) * P)
                    b = 2 * (t % 2)
                    for hd in range(HEADS):
                        mm = pe.matmul(bank(b)[:, hd], a.k_end[:, t, hd // 2], h.gv[:, t, hd * P:(hd + 1) * P],
                                       start=True, stop=True)
                    mm.then_inc(s.added, 1)
                    if t >= 1:
                        pe.wait_ge(s.state, HEADS * t)
                    if t >= 2:
                        pe.wait_ge(s.out_copy, t - 1)
                    for hd in range(HEADS):
                        pe.matmul(bank(b + 1)[:, hd], st[:, hd], a.q_sum[:, hd // 2, cols], start=True, stop=False)
                        mm = pe.matmul(bank(b + 1)[:, hd], h.gv[:, t, hd * P:(hd + 1) * P],
                                       a.scores[:, t, 2 * (hd % 2) + hd // 2], start=False, stop=True)
                    mm.then_inc(s.out, 1)

            @block.vector
            def _(dve):
                dve.memset(st[:], 0.0).then_inc(s.zero, 1)
                for t in range(TT):
                    dve.wait_ge(s.added, t + 1)
                    dve.wait_ge(s.out, t + 1)
                    for hd in range(HEADS):
                        rows = slice(64 * (hd % 2), 64 * (hd % 2) + 64)
                        dve.scalar_tensor_tensor(st[rows, hd], st[rows, hd], a.f_last[rows, hd // 2, t:t + 1],
                                                 bank(2 * (t % 2))[rows, hd], ALU.mult, ALU.add).then_inc(s.state, 1)

            @block.scalar
            def _(act):
                for t in range(TT):
                    act.wait_ge(s.out, t + 1)
                    act.copy(h.qkv[:, HEADS:2 * HEADS, t * P:(t + 1) * P], bank(2 * (t % 2) + 1)).then_inc(s.out_copy, 1)


def head_norms(nc, k, h):
    ps, con, par = k.ps, k.con, h.par
    ones, eps = con[:, K_ONES:K_ONES + P], con[:, K_EPS:K_EPS + 1]
    with ExitStack() as stack, phase(nc, "square", "square_sum", "inv_ln", "inv_norm", "gained", "normed") as s:
        sq = stack.enter_context(sbuf(nc, "squares", [P, 2, T], F32))
        inv = stack.enter_context(sbuf(nc, "inverse_norm", [P, 2, T], F32))
        with nc.Block() as block:
            @block.scalar
            def _(act):
                for j in range(2 * HEADS + 1):
                    if j < 2 * HEADS:
                        if j >= 2:
                            act.wait_ge(s.square_sum, j - 1)
                        act.activation(sq[:, j % 2], h.qkv[:, j], ACT.Square).then_inc(s.square, 1)
                    if j >= 1:
                        n = j - 1
                        act.wait_ge(s.square_sum, n + 1)
                        if n >= 2:
                            act.wait_ge(s.gained, n - 1)
                        act.activation(inv[:, n % 2], ps[:, n % 2], ACT.Ln, bias=eps, scale=1.0 / P).then_inc(s.inv_ln, 1)
                        act.wait_ge(s.inv_ln, n + 1)
                        act.activation(inv[:, n % 2], inv[:, n % 2], ACT.Exp, scale=-0.5).then_inc(s.inv_norm, 1)

            @block.tensor
            def _(pe):
                for j in range(2 * HEADS):
                    pe.wait_ge(s.square, j + 1)
                    if j >= 2:
                        pe.wait_ge(s.inv_ln, j - 1)
                    pe.matmul(ps[:, j % 2], ones, sq[:, j % 2], start=True, stop=True).then_inc(s.square_sum, 1)

            @block.vector
            def _(dve):
                for j in range(2 * HEADS):
                    gain = C_DNG if j < HEADS else C_GLG
                    dve.wait_ge(s.inv_norm, j + 1)
                    dve.scalar_tensor_tensor(h.qkv[:, j], h.qkv[:, j], par[:, gain:gain + 1], inv[:, j % 2],
                                             ALU.mult, ALU.mult).then_inc(s.gained, 1)

            @block.gpsimd
            def _(pool):
                for j in range(2 * HEADS):
                    pool.wait_ge(s.gained, j + 1)
                    pool.tensor_tensor(h.qkv[:, j], h.qkv[:, j], h.z[:, j], ALU.mult).then_inc(s.normed, 1)


def output_product(nc, k, weights, base, source, inputs, chunks, out, alpha=None):
    ps = k.ps
    wide = inputs == KD
    n_groups = chunks // 2
    per = 2 if wide else 4
    with operands(nc, k, inputs), phase(nc, *GEMM) as s:
        st = Stream(k, weights, base, chunks, CHUNK, per, inputs, source)
        with nc.Block() as block:
            @block.sync
            def _(sp):
                st.load(sp, s)

            @block.scalar
            def _(act):
                st.input_high(act, s)
                for c in range(chunks):
                    st.high(act, s, c, c % 2)

            @block.vector
            def _(dve):
                st.input_low(dve, s)
                st.low(dve, s, 0, 0)
                for c in range(chunks):
                    if c + 1 < chunks:
                        st.low(dve, s, c + 1, (c + 1) % 2)
                    for n in range(per):
                        tile = per * c + n
                        dve.wait_ge(s.made, tile + 1)
                        src = ps[:, tile % 4]
                        if alpha is None:
                            dve.tensor_copy(out[:, tile], src).then_inc(s.freed, 1)
                        else:
                            dve.scalar_tensor_tensor(out[:, tile], out[:, tile], alpha, src,
                                                     ALU.mult, ALU.add).then_inc(s.freed, 1)

            @block.tensor
            def _(pe):
                pe.wait_ge(s.in_lo, inputs)
                for c in range(chunks):
                    pe.wait_ge(s.split, c + 1)
                    for n in range(per):
                        tile = per * c + n
                        if tile >= 4:
                            pe.wait_ge(s.freed, tile - 3)
                        st.feature_tile(pe, ps[:, tile % 4], c % 2, inputs * n, inputs, 0, True, True).then_inc(s.made, 1)


def layer_norm(nc, k, h):
    ps, con, par, x = k.ps, k.con, h.par, k.x
    ones, eps = con[:, K_ONES:K_ONES + P], con[:, K_EPS:K_EPS + 1]
    with ExitStack() as stack, phase(nc, "total", "mean", "centred", "square", "square_sum", "inv_ln", "inv_norm",
                                     "scaled", "done") as s:
        sq = stack.enter_context(sbuf(nc, "squares", [P, 2, T], F32))
        mean = stack.enter_context(sbuf(nc, "mean", [P, T], F32))
        inv = stack.enter_context(sbuf(nc, "inverse_deviation", [P, T], F32))
        with nc.Block() as block:
            @block.tensor
            def _(pe):
                for j in range(KD):
                    mm = pe.matmul(ps[:, 0], ones, x[:, j], start=j == 0, stop=j == KD - 1)
                mm.then_inc(s.total, 1)
                for j in range(KD):
                    pe.wait_ge(s.square, j + 1)
                    pe.matmul(ps[:, 1], ones, sq[:, j % 2], start=j == 0, stop=j == KD - 1).then_inc(s.square_sum, 1)

            @block.scalar
            def _(act):
                act.wait_ge(s.total, 1)
                act.mul(mean[:], ps[:, 0], 1.0 / D).then_inc(s.mean, 1)
                for j in range(KD):
                    act.wait_ge(s.centred, j + 1)
                    if j >= 2:
                        act.wait_ge(s.square_sum, j - 1)
                    act.activation(sq[:, j % 2], x[:, j], ACT.Square).then_inc(s.square, 1)
                act.wait_ge(s.square_sum, KD)
                act.activation(inv[:], ps[:, 1], ACT.Ln, bias=eps, scale=1.0 / D).then_inc(s.inv_ln, 1)
                act.wait_ge(s.inv_ln, 1)
                act.activation(inv[:], inv[:], ACT.Exp, scale=-0.5).then_inc(s.inv_norm, 1)
                for j in range(KD):
                    act.wait_ge(s.scaled, j + 1)
                    act.activation(x[:, j], x[:, j], ACT.Identity, scale=par[:, C_LNG + j:C_LNG + j + 1],
                                   bias=par[:, C_LNB + j:C_LNB + j + 1]).then_inc(s.done, 1)

            @block.vector
            def _(dve):
                dve.wait_ge(s.mean, 1)
                for j in range(KD):
                    dve.tensor_tensor(x[:, j], x[:, j], mean[:], ALU.subtract).then_inc(s.centred, 1)
                dve.wait_ge(s.inv_norm, 1)
                for j in range(KD):
                    dve.tensor_tensor(x[:, j], x[:, j], inv[:], ALU.mult).then_inc(s.scaled, 1)


def hybrid_layer(nc, k, layer):
    with ExitStack() as stack:
        def sb(name, shape):
            return stack.enter_context(sbuf(nc, name, shape, F32))
        h = named(
            par=sb("layer_parameters", [P, N_LAYER]), w2=sb("gate_w2_sb", [16, 2 * P]),
            qkv=sb("qkv", [P, QKV, T]), z=sb("gates_z", [P, 2 * HEADS, T]), gqk=sb("gla_qk", [P, 4, T]),
            gv=sb("gla_v", [P, TT, T]), ba=sb("beta_decay_logits", [P, TT * 8]), gr=sb("gate_rank", [16, T]))
        with phase(nc, "params") as s, nc.Block() as block:
            @block.sync
            def _(sp):
                sp.dma_start(h.par[:], k.layer_params[layer]).then_inc(s.params, 16)
                sp.dma_start(h.w2[:], k.gate_w2[layer]).then_inc(s.params, 16)
                sp.wait_ge(s.params, 32)
        hybrid_projections(nc, k, layer, h)
        prefetch(nc, k, k.w_stream, layer * HYBRID_CHUNKS + PROJ_CHUNKS, CHUNK)
        with ExitStack() as inner:
            def sb2(name, shape):
                return inner.enter_context(sbuf(nc, name, shape, F32))
            a = named(
                kbg=sb2("k_beta_g", [P, HEADS, T]), qg=sb2("q_g", [P, HEADS, T]), at=sb2("a_transposed", [P, TT, HEADS, P]),
                attn=sb2("attention", [P, TT, HEADS, P]), vb=sb2("v_beta", [P, TT, HEADS, P]),
                kdec=sb2("k_decayed", [P, TT, HEADS, P]), inv_t=sb2("inverse_transposed", [P, TT, HEADS, P]),
                elast=sb2("chunk_decay", [P, HEADS, TT]))
            delta_gates(nc, k, h, a)
            delta_solve(nc, k, a)
            delta_scan(nc, k, h, a)
        with ExitStack() as inner:
            def sb3(name, shape):
                return inner.enter_context(sbuf(nc, name, shape, F32))
            a = named(scores=sb3("gla_scores", [P, TT, HEADS, P]), q_sum=sb3("q_sum", [P, 2, T]),
                                f_last=sb3("f_last", [P, 2, TT]), k_end=sb3("k_end", [P, TT, 2, P]))
            gla_prepare(nc, k, h, a)
            gla_scan(nc, k, h, a)
        head_norms(nc, k, h)
        output_product(nc, k, k.w_stream, layer * HYBRID_CHUNKS + PROJ_CHUNKS, h.qkv, KD, OUT_CHUNKS, k.x, ALPHA)
        layer_norm(nc, k, h)
        prefetch(nc, k, k.w_stream, (layer + 1) * HYBRID_CHUNKS, CHUNK)



def t5_buckets(dist):
    exact = N_BUCKETS // 2
    d = np.maximum(dist, 1).astype(np.float32)
    large = exact + (np.log(d / np.float32(exact)) / np.float32(math.log(BUCKET_MAX_DIST / exact))
                     * np.float32(N_BUCKETS - exact)).astype(np.int32)
    return np.where(dist < exact, dist, np.minimum(large, N_BUCKETS - 1))


def bucket_onehots():
    out = np.zeros((N_BUCKETS + 1, DIL_GROUPS, 384), np.float32)
    for g, rate in enumerate(DIL_RATES):
        c = np.arange(384) - (P - 1)
        m = P - c if g == 0 else -c
        ok = (m >= 0) & (m <= (P if g == 0 else P - 1)) & (m * ORDER[g] % rate == 0)
        b = t5_buckets(np.where(ok, m, 0) * ORDER[g])
        out[b, g, np.arange(384)] = ok
        out[N_BUCKETS, g] = np.where(ok, 0, NEG)
    return out


def rms_norm(nc, k, source, gain, out=None, residual=False):
    ps, con, x = k.ps, k.con, k.x
    ones, eps = con[:, K_ONES:K_ONES + P], con[:, K_EPS:K_EPS + 1]
    with ExitStack() as stack, phase(nc, "square", "square_sum", "inv_ln", "inv_norm", "scaled", "done") as s:
        sq = stack.enter_context(sbuf(nc, "squares", [P, 2, T], F32))
        inv = stack.enter_context(sbuf(nc, "inverse_rms", [P, T], F32))
        scaled = source if residual else out
        with nc.Block() as block:
            @block.tensor
            def _(pe):
                for j in range(KD):
                    pe.wait_ge(s.square, j + 1)
                    pe.matmul(ps[:, 0], ones, sq[:, j % 2], start=j == 0, stop=j == KD - 1).then_inc(s.square_sum, 1)

            @block.scalar
            def _(act):
                for j in range(KD):
                    if j >= 2:
                        act.wait_ge(s.square_sum, j - 1)
                    act.activation(sq[:, j % 2], source[:, j], ACT.Square).then_inc(s.square, 1)
                act.wait_ge(s.square_sum, KD)
                act.activation(inv[:], ps[:, 0], ACT.Ln, bias=eps, scale=1.0 / D).then_inc(s.inv_ln, 1)
                act.wait_ge(s.inv_ln, 1)
                act.activation(inv[:], inv[:], ACT.Exp, scale=-0.5).then_inc(s.inv_norm, 1)

            @block.vector
            def _(dve):
                dve.wait_ge(s.inv_norm, 1)
                for j in range(KD):
                    g = k.second[:, C_GAIN + gain * KD + j:C_GAIN + gain * KD + j + 1]
                    if residual:
                        dve.scalar_tensor_tensor(source[:, j], source[:, j], g, inv[:], ALU.mult, ALU.mult) \
                            .then_inc(s.scaled, 1)
                        if j:
                            dve.wait_ge(s.scaled, j)
                            dve.tensor_tensor(x[:, j - 1], x[:, j - 1], source[:, j - 1], ALU.add).then_inc(s.done, 1)
                    else:
                        dve.scalar_tensor_tensor(out[:, j], source[:, j], g, inv[:], ALU.mult, ALU.mult) \
                            .then_inc(s.done, 1)
                if residual:
                    dve.wait_ge(s.scaled, KD)
                    dve.tensor_tensor(x[:, KD - 1], x[:, KD - 1], source[:, KD - 1], ALU.add).then_inc(s.done, 1)


def stick_projections(nc, k, source, qk, v):
    n_groups = SB_CHUNKS // 2
    with operands(nc, k, KD), phase(nc, *GEMM) as s:
        st = Stream(k, k.w_stream, AT_STICK, SB_CHUNKS, CHUNK, 2, KD, source)
        ps = k.ps
        with nc.Block() as block:
            @block.sync
            def _(sp):
                st.load(sp, s)

            @block.tensor
            def _(pe):
                pe.wait_ge(s.in_lo, KD)
                groups(pe, 0, 4, n_groups, lambda i: st.products(pe, s, i, ps, "feature"))
                groups(pe, 4, 6, n_groups, lambda i: st.products(pe, s, i, ps, "token"))

            @block.scalar
            def _(act):
                st.input_high(act, s)
                st.high(act, s, 0, 0)

                def features(scale):
                    def body(i):
                        for u in range(2):
                            st.high(act, s, 2 * i + u + 1, 1 - u)
                            for n in range(2):
                                tile = 4 * i + 2 * u + n
                                act.wait_ge(s.made, tile + 1)
                                act.mul(qk[:, tile], ps[:, 2 * u + n], scale).then_inc(s.freed, 1)
                    return body

                def values(i):
                    for u in range(2):
                        if not (static(i) and i == n_groups - 1 and u == 1):
                            st.high(act, s, 2 * i + u + 1, 1 - u)
                        for n in range(2):
                            act.wait_ge(s.made, 4 * i + 2 * u + n + 1)
                            act.copy(v[:, 2 * n:2 * n + 2, bass.ds((2 * i + u - 8) * 2 * P, 2 * P)],
                                     ps[:, 2 * u + n].rearrange("p (t n) -> p t n", t=2)).then_inc(s.freed, 1)
                groups(act, 0, 2, n_groups, features(64 ** -0.5))
                groups(act, 2, 4, n_groups, features(1.0))
                groups(act, 4, 6, n_groups, values)

            @block.vector
            def _(dve):
                st.input_low(dve, s)
                st.low(dve, s, 0, 0)

                def body(i):
                    for u in range(2):
                        if not (static(i) and i == n_groups - 1 and u == 1):
                            st.low(dve, s, 2 * i + u + 1, 1 - u)
                groups(dve, 0, n_groups, n_groups, body)


def stick_attention(nc, k, qk, v, out):
    ps, con = k.ps, k.con
    negtri, negones = con[:, K_NEGTRI:K_NEGTRI + P], con[:, K_NEGONES:K_NEGONES + P]
    pairs = SB_HEADS // 2
    units = [(p, jt) for p in range(pairs) for jt in reversed(range(TT))]
    n_units = len(units)
    with ExitStack() as stack, phase(nc, "z", "capped", "exp", "log", "softplus", "masked", "later", "sums", "weights",
                                     "kept", "out", "out_copy") as s:
        zc = stack.enter_context(sbuf(nc, "z_capped", [P, 2, 2, T], F32))
        softp = stack.enter_context(sbuf(nc, "softplus", [P, 2, 2, T], F32))
        later = stack.enter_context(sbuf(nc, "later_keys", [P, 2, 2, T], F32))
        w = stack.enter_context(sbuf(nc, "weights", [P, 2, 2, T], F32))

        def zbank(u):
            return ps[:, 2 * (u % 3):2 * (u % 3) + 2]

        def made_later(u):
            return (TT - 1) * (u // TT) + min(u % TT, TT - 1)

        with nc.Block() as block:
            @block.tensor
            def _(pe):
                def scores(u):
                    p, jt = units[u]
                    if u >= 3:
                        pe.wait_ge(s.weights, u - 2)
                    for y in range(2):
                        rows = slice(64 * y, 64 * y + 64)
                        mm = pe.matmul(zbank(u)[:, y, jt * P:], qk[rows, 8 + p, jt * P:(jt + 1) * P],
                                       qk[rows, p, jt * P:], start=True, stop=False, skip_group_check=True)
                    mm.then_inc(s.z, 1)

                def sums(u):
                    p, jt = units[u]
                    pe.wait_ge(s.softplus, u + 1)
                    pe.wait_ge(s.masked, u + 1)
                    if jt < TT - 1:
                        pe.wait_ge(s.later, 2 * made_later(u))
                    for y in range(2):
                        if jt < TT - 1:
                            pe.matmul(zbank(u)[:, y, (jt + 1) * P:], negones, later[:, u % 2, y, (jt + 1) * P:],
                                      start=False, stop=False, skip_group_check=True)
                        mm = pe.matmul(zbank(u)[:, y, jt * P:], negtri, softp[:, u % 2, y, jt * P:],
                                       start=False, stop=True, skip_group_check=True)
                    mm.then_inc(s.sums, 1)

                def values(u):
                    p, jt = units[u]
                    pe.wait_ge(s.kept, u + 1)
                    if jt == TT - 1 and p >= 2:
                        pe.wait_ge(s.out_copy, p - 1)
                    for y in range(2):
                        hd = 2 * p + y
                        mm = pe.matmul(ps[64 * y:64 * y + 64, 6 + p % 2, jt * P:], v[:, jt, hd * 64:hd * 64 + 64],
                                       w[:, u % 2, y, jt * P:], start=jt == TT - 1, stop=jt == 0,
                                       skip_group_check=True)
                    mm.then_inc(s.out, 1)
                for u in range(n_units + 2):
                    if u < n_units:
                        scores(u)
                    if 1 <= u <= n_units:
                        sums(u - 1)
                    if u >= 2:
                        values(u - 2)

            @block.vector
            def _(dve):
                def cap(u):
                    jt = units[u][1]
                    dve.wait_ge(s.z, u + 1)
                    if u >= 2:
                        dve.wait_ge(s.log, u - 1)
                        dve.wait_ge(s.softplus, u - 1)
                    dve.tensor_scalar(zc[:, u % 2, :, jt * P:], zbank(u)[:, :, jt * P:], 40.0, None, ALU.min) \
                        .then_inc(s.capped, 1)

                def softplus(u):
                    jt = units[u][1]
                    dve.wait_ge(s.log, u + 1)
                    if u >= 2:
                        dve.wait_ge(s.sums, u - 1)
                        dve.wait_ge(s.later, 2 * made_later(u - 1))
                    dve.tensor_tensor(softp[:, u % 2, :, jt * P:], zbank(u)[:, :, jt * P:], zc[:, u % 2, :, jt * P:],
                                      ALU.max).then_inc(s.softplus, 1)

                def copy_out(p):
                    dve.wait_ge(s.out, TT * (p + 1))
                    dve.tensor_copy(out[:, p], ps[:, 6 + p % 2]).then_inc(s.out_copy, 1)
                for u in range(n_units + 1):
                    if u < n_units:
                        cap(u)
                    if u >= 1:
                        softplus(u - 1)
                    if u >= 6 and (u - 6) % TT == 0:
                        copy_out((u - 6) // TT)
                copy_out(pairs - 1)

            @block.scalar
            def _(act):
                def logs(u):
                    jt = units[u][1]
                    z = zc[:, u % 2, :, jt * P:]
                    act.wait_ge(s.capped, u + 1)
                    act.activation(z, z, ACT.Exp).then_inc(s.exp, 1)
                    act.wait_ge(s.exp, u + 1)
                    act.activation(z, z, ACT.Ln, bias=con[:, K_ONE:K_ONE + 1]).then_inc(s.log, 1)

                def weights(u):
                    jt = units[u][1]
                    act.wait_ge(s.sums, u + 1)
                    if u >= 2:
                        act.wait_ge(s.out, u - 1)
                    act.activation(w[:, u % 2, :, jt * P:], zbank(u)[:, :, jt * P:], ACT.Exp).then_inc(s.weights, 1)
                for u in range(n_units + 1):
                    if u < n_units:
                        logs(u)
                    if u >= 1:
                        weights(u - 1)

            @block.gpsimd
            def _(pool):
                def keep(x, jt):
                    d = x[:, :, jt * P:(jt + 1) * P]
                    return pool.affine_select(out=d, in_=d, compare_op=ALU.is_gt, fill=0.0, base=0,
                                              pattern=[[0, 2], [1, P]], channel_multiplier=-1)
                for u in range(n_units + 1):
                    if u < n_units:
                        jt = units[u][1]
                        pool.wait_ge(s.softplus, u + 1)
                        keep(softp[:, u % 2], jt).then_inc(s.masked, 1)
                        pool.wait_ge(s.masked, u + 1)
                        if u >= 1:
                            pool.wait_ge(s.sums, u)
                        new, old = later[:, (u + 1) % 2], later[:, u % 2]
                        if jt == TT - 1:
                            pool.tensor_copy(new[:, :, jt * P:], softp[:, u % 2, :, jt * P:]).then_inc(s.later, 2)
                        elif jt > 0:
                            pool.wait_ge(s.later, 2 * made_later(u))
                            pool.tensor_copy(new[:, :, jt * P:(jt + 1) * P], softp[:, u % 2, :, jt * P:(jt + 1) * P]) \
                                .then_inc(s.later, 1)
                            pool.tensor_tensor(new[:, :, (jt + 1) * P:], old[:, :, (jt + 1) * P:],
                                               softp[:, u % 2, :, (jt + 1) * P:], ALU.add).then_inc(s.later, 1)
                    if u >= 1:
                        pool.wait_ge(s.weights, u)
                        keep(w[:, (u - 1) % 2], units[u - 1][1]).then_inc(s.kept, 1)


def ffn_up(nc, k, source, layer, h):
    ps = k.ps
    n_groups = UP_CHUNKS // 2
    taps = k.second[:, C_FTAP:C_FTAP + 2 * 3 * 2 * KF].rearrange("p (l w y c a) -> p l w y c a", l=2, w=3, y=2, a=1)
    bias = k.second[:, C_FBIAS:C_FBIAS + 2 * 2 * KF].rearrange("p (l y c a) -> p l y c a", l=2, y=2, a=1)
    with operands(nc, k, KD), ExitStack() as stack, phase(nc, *GEMM, "tap", "conv", "silu") as s:
        y = stack.enter_context(sbuf(nc, "conv", [P, 4, T], F32))
        st = Stream(k, k.w_stream, AT_UP[layer], UP_CHUNKS, CHUNK, 2, KD, source)
        with nc.Block() as block:
            @block.sync
            def _(sp):
                st.load(sp, s)

            @block.tensor
            def _(pe):
                pe.wait_ge(s.in_lo, KD)
                groups(pe, 0, n_groups, n_groups, lambda i: st.products(pe, s, i, ps, "feature", s.conv, 2))

            @block.scalar
            def _(act):
                st.input_high(act, s)
                st.high(act, s, 0, 0)

                def body(i):
                    for u in range(2):
                        if not (static(i) and i == n_groups - 1 and u == 1):
                            st.high(act, s, 2 * i + u + 1, 1 - u)
                        for n in range(2):
                            b = 2 * u + n
                            act.wait_ge(s.made, 4 * i + b + 1)
                            if not (static(i) and i == 0):
                                act.wait_ge(s.freed, 2 * i - 1 + n)
                            act.activation(y[:, b], ps[:, b], ACT.Identity, scale=taps[:, layer, 2, u, 2 * i + n],
                                           bias=bias[:, layer, u, 2 * i + n]).then_inc(s.tap, 1)
                        for n in range(2):
                            if u == 0:
                                act.wait_ge(s.conv, 2 * (4 * i + n) + 2)
                                act.activation(y[:, n], y[:, n], ACT.Silu).then_inc(s.silu, 1)
                groups(act, 0, n_groups, n_groups, body)

            @block.vector
            def _(dve):
                st.input_low(dve, s)
                st.low(dve, s, 0, 0)

                def body(i):
                    for u in range(2):
                        if not (static(i) and i == n_groups - 1 and u == 1):
                            st.low(dve, s, 2 * i + u + 1, 1 - u)
                        for n in range(2):
                            b = 2 * u + n
                            dve.wait_ge(s.tap, 4 * i + b + 1)
                            for back in (1, 2):
                                if back == 2:
                                    dve.wait_ge(s.conv, 2 * (4 * i + b) + 1)
                                dve.scalar_tensor_tensor(y[:, b, back:], ps[:, b, 0:T - back],
                                                         taps[:, layer, 2 - back, u, 2 * i + n], y[:, b, back:],
                                                         ALU.mult, ALU.add).then_inc(s.conv, 1)
                    dve.wait_ge(s.silu, 2 * i + 2)
                    dve.wait_ge(s.conv, 8 * i + 8)
                    for n in range(2):
                        dve.tensor_tensor(h[:, 2 * i + n], y[:, n], y[:, 2 + n], ALU.mult).then_inc(s.freed, 1)
                groups(dve, 0, n_groups, n_groups, body)


def ffn_down(nc, k, layer, h):
    ps = k.ps
    n_groups = DOWN_CHUNKS // 4
    cols = DOWN_BLOCKS * P
    with operands(nc, k, KF, cols), phase(nc, *GEMM) as s:
        st = Stream(k, k.w_down, layer * DOWN_CHUNKS, DOWN_CHUNKS, cols, 1, KF, h)
        with nc.Block() as block:
            @block.sync
            def _(sp):
                st.load(sp, s)

            @block.tensor
            def _(pe):
                def body(i):
                    for n in range(2):
                        if not (static(i) and i == 0):
                            pe.wait_ge(s.freed, 2 * i + n - 1)
                        for half in range(2):
                            pe.wait_ge(s.split, 4 * i + 2 * n + half + 1)
                            if static(i) and i == 0 and n == 0:
                                pe.wait_ge(s.in_lo, DOWN_BLOCKS * (half + 1))
                            st.feature_tile(pe, ps[:, n], half, 0, DOWN_BLOCKS, DOWN_BLOCKS * half,
                                            half == 0, half == 1).then_inc(s.made, 1)
                groups(pe, 0, n_groups, n_groups, body)

            @block.scalar
            def _(act):
                st.input_high(act, s)
                n_pairs = DOWN_CHUNKS // 2

                def body(i):
                    for u in range(2):
                        st.high(act, s, 2 * i + u, u)
                body(0)
                with act.Fori(1, n_pairs) as i:
                    body(i)

            @block.vector
            def _(dve):
                st.input_low(dve, s)
                st.low(dve, s, 0, 0)

                def body(i):
                    for n in range(2):
                        for half in range(2):
                            c = 4 * i + 2 * n + half + 1
                            if not (static(i) and i == n_groups - 1 and n == 1 and half == 1):
                                st.low(dve, s, c, 1 - half)
                        dve.wait_ge(s.made, 2 * (2 * i + n) + 2)
                        dve.tensor_copy(h[:, 2 * i + n], ps[:, n]).then_inc(s.freed, 1)
                groups(dve, 0, n_groups, n_groups, body)


def bias_tables(nc, k, rel_bias, bucket_onehot, tables):
    scratch = nc.dram_tensor("bias_rows", (DIL_GROUPS, DIL_HEADS, 384), F32, kind="Internal").ap()
    ps = k.ps
    flip = k.con[:, K_FLIP:K_FLIP + P]
    parts = [(g, n) for g in range(DIL_GROUPS) for n in range(4 if g == 0 else 2)]
    with ExitStack() as stack, phase(nc, "loaded", "ones", "rows", "copied", "written", "read", "flipped", "table") as s:
        rb = stack.enter_context(sbuf(nc, "bias_by_bucket", [N_BUCKETS + 1, DIL_GROUPS * DIL_HEADS], F32))
        onehot = stack.enter_context(sbuf(nc, "bucket_onehot", [N_BUCKETS + 1, DIL_GROUPS, 384], F32))
        rows = stack.enter_context(sbuf(nc, "bias_rows_sb", [DIL_HEADS, DIL_GROUPS, 384], F32))
        backward = [stack.enter_context(sbuf(nc, "table_backward", t.shape, F32)) for t in tables]

        def columns_of(x, n):
            return x[:].rearrange("p h j -> p (h j)")[:, n * T:(n + 1) * T]

        with nc.Block() as block:
            @block.sync
            def _(sp):
                sp.dma_start(rb[0:N_BUCKETS], rel_bias).then_inc(s.loaded, 16)
                sp.dma_start(onehot[:], bucket_onehot).then_inc(s.loaded, 16)
                sp.wait_ge(s.copied, DIL_GROUPS)
                sp.dma_start(scratch.rearrange("g h c -> h g c"), rows[:]).then_inc(s.written, 16)
                sp.wait_ge(s.written, 16)
                for g in range(DIL_GROUPS):
                    width = 2 * P if g == 0 else P
                    shifted = bass.AP(scratch.tensor, g * DIL_HEADS * 384, [[1, P], [384, DIL_HEADS], [1, width]])
                    sp.dma_start(backward[g][:], shifted).then_inc(s.read, 16)

            @block.vector
            def _(dve):
                dve.memset(rb[N_BUCKETS:N_BUCKETS + 1], 1.0).then_inc(s.ones, 1)
                for g in range(DIL_GROUPS):
                    dve.wait_ge(s.rows, g + 1)
                    dve.tensor_copy(rows[:, g], ps[0:DIL_HEADS, g, 0:384]).then_inc(s.copied, 1)
                for m, (g, n) in enumerate(parts):
                    dve.wait_ge(s.flipped, m + 1)
                    dve.tensor_copy(columns_of(tables[g], n), ps[:, m]).then_inc(s.table, 1)

            @block.tensor
            def _(pe):
                pe.wait_ge(s.loaded, 32)
                pe.wait_ge(s.ones, 1)
                for g in range(DIL_GROUPS):
                    pe.matmul(ps[0:DIL_HEADS, g, 0:384], rb[:, g * DIL_HEADS:(g + 1) * DIL_HEADS], onehot[:, g],
                              start=True, stop=True).then_inc(s.rows, 1)
                pe.wait_ge(s.read, 16 * DIL_GROUPS)
                for m, (g, n) in enumerate(parts):
                    pe.matmul(ps[:, m], flip, columns_of(backward[g], n), start=True, stop=True).then_inc(s.flipped, 1)


def by_class(x, rate):
    return x.rearrange("p (l c) -> p c l", c=rate)


def dilated_projections(nc, k, source, q, kk, v):
    n_groups = DIL_CHUNKS // 2
    with operands(nc, k, KD), phase(nc, *GEMM) as s:
        st = Stream(k, k.w_stream, AT_DILATED, DIL_CHUNKS, CHUNK, 2, KD, source)
        ps = k.ps

        def ordered_tokens(x, g, t):
            rate = ORDER[g]
            if rate == 1:
                return x[:, t * P:(t + 1) * P]
            return by_class(x, rate)[:, t]

        with nc.Block() as block:
            @block.sync
            def _(sp):
                st.load(sp, s)

            @block.tensor
            def _(pe):
                pe.wait_ge(s.in_lo, KD)
                groups(pe, 0, 6, n_groups, lambda i: st.products(pe, s, i, ps, "feature"))
                for g in range(DIL_GROUPS):
                    st.products(pe, s, 6 + g, ps, "token", tokens=lambda x, t, g=g: ordered_tokens(x, g, t))

            @block.scalar
            def _(act):
                st.input_high(act, s)
                st.high(act, s, 0, 0)
                for i in range(n_groups):
                    for u in range(2):
                        if 2 * i + u + 1 < DIL_CHUNKS:
                            st.high(act, s, 2 * i + u + 1, 1 - u)
                        for n in range(2):
                            tile = 4 * i + 2 * u + n
                            src = ps[:, 2 * u + n]
                            act.wait_ge(s.made, tile + 1)
                            if tile < 24:
                                dst = (q if tile < 12 else kk)[:, tile % 12]
                                rate = ORDER[tile % 12 // 4]
                                if rate > 1:
                                    dst, src = dst.rearrange("p (c l) -> p c l", c=rate), by_class(src, rate)
                                act.mul(dst, src, 64 ** -0.5 if tile < 12 else 1.0).then_inc(s.freed, 1)
                            else:
                                act.copy(v[:, 2 * n:2 * n + 2, i - 6, u * 2 * P:(u + 1) * 2 * P],
                                         src.rearrange("p (t n) -> p t n", t=2)).then_inc(s.freed, 1)

            @block.vector
            def _(dve):
                st.input_low(dve, s)
                st.low(dve, s, 0, 0)

                def body(i):
                    for u in range(2):
                        if not (static(i) and i == n_groups - 1 and u == 1):
                            st.low(dve, s, 2 * i + u + 1, 1 - u)
                groups(dve, 0, n_groups, n_groups, body)


def dilated_scores(nc, k, q, kk, v, tables, num, top, total):
    ps, con = k.ps, k.con
    ident = con[:, K_IDENT:K_IDENT + P]
    units = [(0, 0, 0, 8, 1)] + [(0, t, h0, 4, 2) for t in range(1, TT) for h0 in (0, 4)] \
        + [(g, t, 0, 8, 1) for g in (1, 2) for t in range(TT)]
    n_units = len(units)
    tiles = [n for n, (g, t, h0, heads, _) in enumerate(units) if h0 + heads == DIL_HEADS]
    with ExitStack() as stack, phase(nc, "scores", "half", "biased", "exp", "turned", "turned_read", "out", "out_copy") as s:
        sc = stack.enter_context(sbuf(nc, "scores", [P, 2, 2 * T], F32))
        pt = stack.enter_context(sbuf(nc, "weights_turned", [P, 2, 8, P], F32))

        def exps(n):
            return sum(u[3] for u in units[:n])

        def tile_of(n):
            return sum(1 for m in tiles if m < n)

        with nc.Block() as block:
            @block.tensor
            def _(pe):
                def scores(n):
                    g, t, h0, heads, keys = units[n]
                    b = 2 * (n % 2)
                    if n >= 2:
                        pe.wait_ge(s.biased, n - 1)
                    for hd in range(h0, h0 + heads):
                        rows = slice(64 * (hd % 2), 64 * (hd % 2) + 64)
                        at = (hd - h0) // 2 * keys * P
                        f = 4 * g + hd // 2
                        mm = pe.matmul(ps[:, b + hd % 2, at:at + keys * P], q[rows, f, t * P:(t + 1) * P],
                                       kk[rows, f, (t + 1 - keys) * P:(t + 1) * P], start=True, stop=True)
                    mm.then_inc(s.scores, 1)

                def turn(n):
                    pe.wait_ge(s.exp, exps(n + 1))
                    if n >= 1:
                        pe.wait_ge(s.turned_read, 2 * n)
                    for m in range(8):
                        mm = pe.transpose(ps[:, 4 + m // 4, m % 4 * P:(m % 4 + 1) * P],
                                          sc[:, n % 2, m * P:(m + 1) * P], ident)
                        if m % 4 == 3:
                            mm.then_inc(s.turned, 1)

                def values(n):
                    g, t, h0, heads, keys = units[n]
                    out = 6 + tile_of(n) % 2
                    pe.wait_ge(s.turned_read, 2 * n + 2)
                    if tile_of(n) >= 2:
                        pe.wait_ge(s.out_copy, tile_of(n) - 1)
                    for hd in range(h0, h0 + heads):
                        for kt in range(keys):
                            m = (hd % 2) * 4 + (hd - h0) // 2 * keys + kt
                            mm = pe.matmul(ps[:, out, hd * 64:hd * 64 + 64], pt[:, n % 2, m],
                                           v[:, t + 1 - keys + kt, g, hd * 64:hd * 64 + 64],
                                           start=kt == 0, stop=kt == keys - 1)
                    mm.then_inc(s.out, 1)
                for n in range(n_units + 2):
                    if n < n_units:
                        scores(n)
                    if 1 <= n <= n_units:
                        turn(n - 1)
                    if n >= 2:
                        values(n - 2)

            @block.vector
            def _(dve):
                def bias(n):
                    g, t, h0, heads, keys = units[n]
                    b = 2 * (n % 2)
                    w = keys * P
                    hh = heads // 2
                    tab = tables[g][:, h0:h0 + heads, :]
                    if g == 0 and keys == 1:
                        tab = tab[:, :, P:]
                    dst = sc[:, n % 2].rearrange("p (y h w) -> p y h w", y=2, h=hh)
                    dve.wait_ge(s.scores, n + 1)
                    if n >= 2:
                        dve.wait_ge(s.turned, 2 * (n - 1))
                    for y in range(2):
                        dve.tensor_tensor(dst[:, y], ps[:, b + y].rearrange("p (h w) -> p h w", h=hh),
                                          tab.rearrange("p (h y) w -> p y h w", y=2)[:, y], ALU.add).then_inc(s.half, 1)
                    dve.wait_ge(s.half, 2 * n + 2)
                    dve.tensor_reduce(top[:, TT * g + t, h0:h0 + heads].rearrange("p (h y) -> p y h", y=2), dst, AX_X,
                                      ALU.max, negate=True).then_inc(s.biased, 1)

                def turned(n):
                    for half in range(2):
                        dve.wait_ge(s.turned, 2 * n + half + 1)
                        if n >= 2:
                            dve.wait_ge(s.out, n - 1)
                        dve.tensor_copy(pt[:, n % 2, 4 * half:4 * half + 4],
                                        ps[:, 4 + half].rearrange("p (m i) -> p m i", m=4)).then_inc(s.turned_read, 1)
                for n in range(n_units + 1):
                    if n < n_units:
                        bias(n)
                    if n >= 1:
                        turned(n - 1)

            @block.scalar
            def _(act):
                def exps(n):
                    g, t, h0, heads, keys = units[n]
                    act.wait_ge(s.biased, n + 1)
                    for hd in range(h0, h0 + heads):
                        at = hd % 2 * T + (hd - h0) // 2 * keys * P
                        x = sc[:, n % 2, at:at + keys * P]
                        act.activation(x, x, ACT.Exp, bias=top[:, TT * g + t, hd:hd + 1],
                                       accum_out=total[:, TT * g + t, hd:hd + 1]).then_inc(s.exp, 1)

                def copy_out(n):
                    g, t = units[n][0:2]
                    act.wait_ge(s.out, n + 1)
                    act.copy(num[:, TT * g + t], ps[:, 6 + tile_of(n) % 2]).then_inc(s.out_copy, 1)
                for n in range(n_units + 3):
                    if n < n_units:
                        exps(n)
                    if n - 3 in tiles:
                        copy_out(n - 3)


def dilated_merge(nc, k, num, top, total, out):
    ps, con = k.ps, k.con
    ident = con[:, K_IDENT:K_IDENT + P]
    G = DIL_GROUPS
    with ExitStack() as stack, phase(nc, "turned", "rows", "step", "exp", "weight", "columns", "column", "scaled",
                                     "features", "merged") as s:
        rows = stack.enter_context(sbuf(nc, "top_and_total", [DIL_HEADS, 2, G, T], F32))
        low = stack.enter_context(sbuf(nc, "least_negative", [DIL_HEADS, T], F32))
        den = stack.enter_context(sbuf(nc, "denominator", [DIL_HEADS, G, T], F32))
        col = stack.enter_context(sbuf(nc, "weight_columns", [P, G * TT, DIL_HEADS], F32))
        tops, totals = rows[:, 0], rows[:, 1]

        with nc.Block() as block:
            @block.tensor
            def _(pe):
                for g in range(G):
                    for n, src in enumerate((top, total)):
                        for t in range(TT):
                            mm = pe.transpose(ps[0:DIL_HEADS, 2 * g + n, t * P:(t + 1) * P], src[:, TT * g + t], ident)
                        mm.then_inc(s.turned, 1)
                pe.wait_ge(s.weight, G)
                for g in range(G):
                    for t in range(TT):
                        rate = ORDER[g]
                        if rate == 1:
                            src = tops[:, g, t * P:(t + 1) * P]
                        else:
                            src = by_class(tops[:, g], rate)[:, t]
                        n = TT * g + t
                        mm = pe.transpose(ps[:, 6, n * DIL_HEADS:(n + 1) * DIL_HEADS], src,
                                          ident[0:DIL_HEADS, 0:DIL_HEADS])
                mm.then_inc(s.columns, 1)
                for n in range(G * TT):
                    pe.wait_ge(s.scaled, n + 1)
                    if n >= 4:
                        pe.wait_ge(s.merged, n - 3)
                    for f in range(TT):
                        mm = pe.transpose(ps[:, n % 4, f * P:(f + 1) * P], num[:, n, f * P:(f + 1) * P], ident)
                    mm.then_inc(s.features, 1)

            @block.scalar
            def _(act):
                for g in range(G):
                    rate = ORDER[g]
                    for n in range(2):
                        act.wait_ge(s.turned, 2 * g + n + 1)
                        src = ps[0:DIL_HEADS, 2 * g + n]
                        dst = rows[:, n, g]
                        if rate > 1:
                            src, dst = src.rearrange("p (c l) -> p c l", c=rate), by_class(dst, rate)
                        act.copy(dst, src).then_inc(s.rows, 1)
                act.wait_ge(s.step, 5)
                act.activation(tops, tops, ACT.Exp, scale=-1.0).then_inc(s.exp, 1)

            @block.vector
            def _(dve):
                steps = [0]

                def step(ins):
                    steps[0] += 1
                    ins.then_inc(s.step, 1)
                    dve.wait_ge(s.step, steps[0])
                dve.wait_ge(s.rows, 2 * G)
                step(dve.tensor_tensor(low[:], tops[:, 0], tops[:, 1], ALU.min))
                step(dve.tensor_tensor(low[:], low[:], tops[:, 2], ALU.min))
                for g in range(G):
                    step(dve.tensor_tensor(tops[:, g], tops[:, g], low[:], ALU.subtract))
                dve.wait_ge(s.exp, 1)
                step(dve.tensor_tensor(den[:], tops, totals, ALU.mult))
                step(dve.tensor_tensor(low[:], den[:, 0], den[:, 1], ALU.add))
                step(dve.tensor_tensor(low[:], low[:], den[:, 2], ALU.add))
                step(dve.reciprocal(low[:], low[:]))
                for g in range(G):
                    dve.tensor_tensor(tops[:, g], tops[:, g], low[:], ALU.mult).then_inc(s.weight, 1)
                dve.wait_ge(s.columns, 1)
                dve.tensor_copy(col[:].rearrange("p n h -> p (n h)"), ps[:, 6, 0:G * TT * DIL_HEADS]).then_inc(s.column, 1)
                for n in range(G * TT):
                    g, t = n // TT, n % TT
                    rate = ORDER[g]
                    dve.wait_ge(s.features, n + 1)
                    src = ps[:, n % 4].rearrange("p (f i) -> p f i", f=TT)
                    if rate == 1:
                        dve.tensor_copy(out[:, :, t * P:(t + 1) * P], src).then_inc(s.merged, 1)
                        continue
                    dve.wait_ge(s.merged, TT * g)
                    dst = out[:].rearrange("p f (l c) -> p c f l", c=rate)[:, t]
                    dve.tensor_tensor(dst, dst, src, ALU.add).then_inc(s.merged, 1)

            @block.gpsimd
            def _(pool):
                pool.wait_ge(s.column, 1)
                for n in range(G * TT):
                    x = num[:, n].rearrange("p (h e) -> p h e", h=DIL_HEADS)
                    pool.tensor_tensor(x, x, col[:, n].unsqueeze(2).to_broadcast([P, DIL_HEADS, 64]), ALU.mult) \
                        .then_inc(s.scaled, 1)


def second_block(nc, k, second_params, rel_bias, bucket_onehot):
    with ExitStack() as stack:
        def sb(name, shape, where=stack):
            return where.enter_context(sbuf(nc, name, shape, F32))
        k.second = sb("second_parameters", [P, N_SECOND])
        with phase(nc, "params") as s, nc.Block() as block:
            @block.sync
            def _(sp):
                sp.dma_start(k.second[:], second_params).then_inc(s.params, 16)
                sp.wait_ge(s.params, 16)

        def mixer_out(layer, source, inputs, chunks, base, next_base):
            with ExitStack() as inner:
                m = sb("mixed", [P, KD, T], inner)
                output_product(nc, k, k.w_stream, base, source, inputs, chunks, m)
                prefetch(nc, k, k.w_stream, next_base, CHUNK)
                rms_norm(nc, k, m, 4 * layer + 1, residual=True)

        def feed_forward(layer, next_base):
            with ExitStack() as inner:
                h = sb("hidden", [P, KF, T], inner)
                with ExitStack() as up:
                    xn = sb("normed", [P, KD, T], up)
                    rms_norm(nc, k, k.x, 4 * layer + 2, out=xn)
                    ffn_up(nc, k, xn, layer, h)
                prefetch(nc, k, k.w_down, layer * DOWN_CHUNKS, DOWN_BLOCKS * P)
                ffn_down(nc, k, layer, h)
                if next_base is not None:
                    prefetch(nc, k, k.w_stream, next_base, CHUNK)
                rms_norm(nc, k, h, 4 * layer + 3, residual=True)

        with ExitStack() as mixer:
            v = sb("stick_v", [P, TT, D], mixer)
            o = sb("stick_out", [P, KD, T], mixer)
            qk = sb("stick_qk", [P, 2 * KD, T], mixer)
            with ExitStack() as inner:
                xn = sb("normed", [P, KD, T], inner)
                rms_norm(nc, k, k.x, 0, out=xn)
                stick_projections(nc, k, xn, qk, v)
            prefetch(nc, k, k.w_stream, AT_STICK_OUT, CHUNK)
            stick_attention(nc, k, qk, v, o)
            mixer_out(0, o, KD, OUT_CHUNKS, AT_STICK_OUT, AT_UP[0])
        feed_forward(0, AT_DILATED)
        with ExitStack() as mixer:
            num = sb("numerators", [P, DIL_GROUPS * TT, T], mixer)
            top = sb("negative_maxima", [P, DIL_GROUPS * TT, DIL_HEADS], mixer)
            total = sb("totals", [P, DIL_GROUPS * TT, DIL_HEADS], mixer)
            with ExitStack() as inner:
                q = sb("dilated_q", [P, 4 * DIL_GROUPS, T], inner)
                kk = sb("dilated_k", [P, 4 * DIL_GROUPS, T], inner)
                v = sb("dilated_v", [P, TT, DIL_GROUPS, T], inner)
                rms_norm(nc, k, k.x, 4, out=num[:, 0:KD])
                dilated_projections(nc, k, num, q, kk, v)
                prefetch(nc, k, k.w_stream, AT_DILATED_OUT, CHUNK)
                with ExitStack() as tab:
                    tables = [sb(f"bias_{g}", [P, DIL_HEADS, 2 * P if g == 0 else P], tab)
                              for g in range(DIL_GROUPS)]
                    bias_tables(nc, k, rel_bias, bucket_onehot, tables)
                    dilated_scores(nc, k, q, kk, v, tables, num, top, total)
            o = sb("dilated_out", [P, TT, T], mixer)
            dilated_merge(nc, k, num, top, total, o)
            mixer_out(1, o, TT, DIL_OUT_CHUNKS, AT_DILATED_OUT, AT_UP[1])
        feed_forward(1, None)



def program(nc, x_t, w_stream, w_down, layer_params, gate_w2, second_params, rel_bias, bucket_onehot, consts, out_t):
    NAMES.clear()
    with ExitStack() as stack:
        def sb(name, shape):
            return stack.enter_context(sbuf(nc, name, shape, F32))
        k = Shared()
        k.w_stream, k.w_down, k.layer_params, k.gate_w2 = w_stream, w_down, layer_params, gate_w2
        k.con, k.x, k.raw = sb("constants", [P, N_CONST]), sb("residual", [P, KD, T]), sb("weights_raw", [P, 2, CHUNK])
        k.ps = stack.enter_context(nc.psum_tensor("psum", [P, 8, T], F32))
        k.landed = [stack.enter_context(nc.semaphore(f"weights_landed_{u}")) for u in range(2)]
        with phase(nc, "loaded") as s, nc.Block() as block:
            @block.sync
            def _(sp):
                sp.dma_start(k.con[:], consts).then_inc(s.loaded, 16)
                sp.dma_start(k.x[:], x_t).then_inc(s.loaded, 16)
                sp.wait_ge(s.loaded, 32)
        prefetch(nc, k, w_stream, 0, CHUNK)
        with nc.Fori(0, LAYERS) as layer:
            hybrid_layer(nc, k, layer)
        second_block(nc, k, second_params, rel_bias, bucket_onehot)
        with phase(nc, "stored") as s, nc.Block() as block:
            @block.sync
            def _(sp):
                sp.dma_start(out_t, k.x[:]).then_inc(s.stored, 16)
                sp.wait_ge(s.stored, 16)
                for u in range(2):
                    sp.wait_ge(k.landed[u], 16)


def feature_chunks(w):
    kt, n = w.shape[0] // P, w.shape[1]
    per = CHUNK // (kt * P)
    return w.reshape(kt, P, n // (per * P), per, P).transpose(2, 1, 3, 0, 4).reshape(-1, P, CHUNK)


def token_chunks(w):
    return w.reshape(KD, P, -1, 2 * P).transpose(2, 1, 0, 3).reshape(-1, P, CHUNK)


def columns(v):
    v = v.reshape(-1, v.shape[-1] // P, P)
    return v.transpose(2, 0, 1).reshape(P, -1)


def interleaved(a, b):
    return np.stack([a, b], 1).reshape(-1, *a.shape[1:])


def layout(x, w_in, conv_w, dn_a_log, dn_dt_bias, gla_gate_w2, gla_gate_b, dn_norm_g, gla_norm_g, w_out, ln_g, ln_b,
           rel_bias_2, norm_gains_2, sb_w_qkv_2, sb_w_o_2, dil_w_qkv_2, dil_w_o_2, ffn_w_up_2, ffn_conv_w_2,
           ffn_conv_b_2, ffn_w_down_2, **unused):
    at = np.cumsum([0, 1536, 512, 8, 512, 512, 512, 16])
    stream, params = [], []
    for n in range(LAYERS):
        w = w_in[n]
        qkv, z, ba, gqk, gv, gz, gr = (w[:, a:b] for a, b in zip(at[:-1], at[1:]))
        stream += [feature_chunks(m) for m in (qkv, z, gz, gqk)] + [token_chunks(gv), feature_chunks(w_out[n])]
        params.append(np.concatenate([
            columns(conv_w[n]), columns(gla_gate_b[n]), columns(dn_norm_g[n]), columns(gla_norm_g[n]), columns(ln_g[n]),
            columns(ln_b[n]), np.broadcast_to(dn_a_log[n], (P, HEADS)), np.broadcast_to(dn_dt_bias[n], (P, HEADS)),
            ba.reshape(KD, P, 8).transpose(1, 0, 2).reshape(P, -1),
            gr.reshape(KD, P, 16).transpose(1, 0, 2).reshape(P, -1)], 1))
    up = [interleaved(feature_chunks(w[:, :FF]), feature_chunks(w[:, FF:])) for w in ffn_w_up_2]
    stream += [feature_chunks(sb_w_qkv_2[0][:, :2 * D]), token_chunks(sb_w_qkv_2[0][:, 2 * D:]),
               feature_chunks(sb_w_o_2[0]), up[0],
               feature_chunks(dil_w_qkv_2[0][:, :3072]), token_chunks(dil_w_qkv_2[0][:, 3072:]),
               feature_chunks(dil_w_o_2[0]), up[1]]
    down = ffn_w_down_2.reshape(LAYERS, 2, DOWN_BLOCKS, P, KD, P).transpose(0, 4, 1, 3, 2, 5) \
        .reshape(LAYERS * DOWN_CHUNKS, P, DOWN_BLOCKS * P)
    second = np.concatenate([columns(norm_gains_2), columns(ffn_conv_w_2), columns(ffn_conv_b_2)], 1)
    return {
        "x_t": x[0].reshape(T, KD, P).transpose(2, 1, 0), "w_stream": np.concatenate(stream), "w_down": down,
        "layer_params": np.stack(params), "gate_w2": gla_gate_w2, "second_params": second, "rel_bias": rel_bias_2,
        "bucket_onehot": bucket_onehots(), "consts": constants(),
    }


def kernel(**inputs):
    from concourse import bacc
    from concourse.bass_utils import run_bass_kernel_spmd

    arrays = {n: np.ascontiguousarray(a) for n, a in layout(**inputs).items()}
    nc = bacc.Bacc("TRN2", target_bir_lowering=False, num_devices=1)
    args = [nc.dram_tensor(n, a.shape, mybir.dt.from_np(a.dtype), kind="ExternalInput").ap() for n, a in arrays.items()]
    args.append(nc.dram_tensor("out_t", (P, KD, T), F32, kind="ExternalOutput").ap())
    program(nc, *args)
    got = run_bass_kernel_spmd(nc, [arrays], core_ids=[0]).results[0]["out_t"]
    return np.ascontiguousarray(got.transpose(2, 1, 0)).reshape(1, T, D)
```

```python
import math
from collections import Counter, namedtuple
from contextlib import ExitStack, contextmanager

import numpy as np
import concourse.bass as bass
from concourse import mybir

F32 = mybir.dt.float32
F32R = mybir.dt.float32r
I32 = mybir.dt.int32
ALU = mybir.AluOpType
ACT = mybir.ActivationFunctionType
AX_X = mybir.AxisListType.X

P = 128
T = 512
D = 1024
KD = D // P
TT = T // P
LAYERS = 2
CHUNK = 2048
NORM_EPS = 1e-6

HEADS = 4
QKV = 12
GLA_SCALE = 64 ** -0.5
GLA_TAU = 16.0
ALPHA = (2.0 * LAYERS) ** 0.25
PROJ_CHUNKS = 14
OUT_CHUNKS = 4
HYBRID_CHUNKS = PROJ_CHUNKS + OUT_CHUNKS

SB_HEADS = 16
SB_CHUNKS = 12
DIL_HEADS = 8
DIL_GROUPS = 3
DIL_RATES = (1, 4, 16)
ORDER = (1, 4, 4)
DIL_CHUNKS = 18
DIL_OUT_CHUNKS = 2
N_BUCKETS = 32
BUCKET_MAX_DIST = 2048
NEG = -1e30
FF = 2816
KF = FF // P
DOWN_CHUNKS = 16
DOWN_BLOCKS = KF // 2

AT_STICK = LAYERS * HYBRID_CHUNKS
AT_STICK_OUT = AT_STICK + SB_CHUNKS
UP_CHUNKS = 2 * KF * P // (2 * P)
AT_DILATED = AT_STICK_OUT + OUT_CHUNKS + UP_CHUNKS
AT_DILATED_OUT = AT_DILATED + DIL_CHUNKS
AT_UP = (AT_STICK_OUT + OUT_CHUNKS, AT_DILATED_OUT + DIL_OUT_CHUNKS)

C_TAP, C_GB, C_DNG, C_GLG, C_LNG, C_LNB, C_ALOG, C_DTB, C_WBA, C_WGR = np.cumsum(
    [0, 4 * QKV, 2, 1, 1, KD, KD, HEADS, HEADS, KD * 8]).tolist()
N_LAYER = C_WGR + KD * 16
C_GAIN, C_FTAP, C_FBIAS = np.cumsum([0, 2 * 4 * KD, 2 * 3 * 2 * KF]).tolist()
N_SECOND = C_FBIAS + 2 * 2 * KF
LEVELS = (1, 2, 4, 8, 16, 32, 64)
K_IDENT, K_ONES, K_INCL, K_NEGTRI, K_NEGONES, K_FLIP, K_LEVEL = [P * n for n in range(7)]
K_RESET = K_LEVEL + 2 * P * len(LEVELS)
K_EPS = K_RESET + T
K_QLN = K_EPS + 1
K_ONE = K_EPS + 2
N_CONST = K_EPS + 3


def level_mask(s):
    j, i = np.meshgrid(np.arange(P), np.arange(P), indexing="ij")
    return ((j // (2 * s) == i // (2 * s)) & (i % (2 * s) >= s) & (j % (2 * s) < s)).astype(np.float32)


def level_mask_of(table, n, copies=1):
    return table[:, K_LEVEL + 2 * P * n:K_LEVEL + 2 * P * n + copies * P]


def constants():
    c = np.zeros((P, N_CONST), np.float32)
    j, i = np.meshgrid(np.arange(P), np.arange(P), indexing="ij")
    c[:, K_IDENT:K_IDENT + P] = i == j
    c[:, K_ONES:K_ONES + P] = 1
    c[:, K_INCL:K_INCL + P] = j <= i
    c[:, K_NEGTRI:K_NEGTRI + P] = -(j >= i).astype(np.float32)
    c[:, K_NEGONES:K_NEGONES + P] = -1
    c[:, K_FLIP:K_FLIP + P] = i + j == P - 1
    for n, s in enumerate(LEVELS):
        level_mask_of(c, n, 2)[:] = np.tile(level_mask(s), 2)
    c[:, K_RESET:K_RESET + T] = np.arange(T) % P != 0
    c[:, K_EPS] = NORM_EPS
    c[:, K_QLN] = -0.5 * math.log(P)
    c[:, K_ONE] = 1
    return c


def named(**things):
    return namedtuple("Named", things)(**things)


class Shared:
    pass


def exp_and_log(act):
    act.preload_act_table_set("natural_log_exp_and_others")


NAMES = Counter()


def sbuf(nc, name, shape, dtype):
    NAMES[name] += 1
    return nc.sbuf_tensor(f"{name}_{NAMES[name]}", shape, dtype)


@contextmanager
def phase(nc, *names):
    with ExitStack() as stack:
        sems = {n: stack.enter_context(nc.semaphore(n)) for n in names}
        yield named(**sems)
        with nc.Block() as block:
            @block.sync
            def _(sp):
                for s in sems.values():
                    sp.sem_clear(s)


def groups(eng, first, end, total, body):
    if first == 0:
        body(0)
        first = 1
    last = end == total and total > 1
    end -= last
    if end - first == 1:
        body(first)
    elif end > first:
        with eng.Fori(first, end) as i:
            body(i)
    if last:
        body(total - 1)


def static(i):
    return isinstance(i, int)


class Stream:

    def __init__(self, k, weights, base, chunks, cols, pieces, inputs, source):
        self.raw, self.whi, self.wlo = k.raw, k.whi, k.wlo
        self.landed = k.landed
        self.weights, self.base, self.chunks, self.cols = weights, base, chunks, cols
        self.pieces = pieces
        self.inputs, self.source = inputs, source
        self.ahi, self.alo = k.ahi, k.alo
        self.k = k

    def load(self, sp, s):
        def body(i):
            for u in range(2):
                c = 2 * i + u
                sp.wait_ge(s.split, c - 1)
                sp.dma_start(self.raw[:, u, 0:self.cols], self.weights[self.base + c]).then_inc(self.landed[u], 16)
        n = self.chunks // 2
        if n == 2:
            body(1)
        elif n > 2:
            with sp.Fori(1, n) as i:
                body(i)

    def input_high(self, act, s, first=0, end=None):
        for k in range(first, end or self.inputs):
            act.copy(self.ahi[:, k], self.source[:, k]).then_inc(s.in_hi, 1)

    def high(self, act, s, c, u):
        act.wait_ge(self.landed[u], 8 * (c - u) + 16)
        if not (static(c) and c < 2):
            act.wait_ge(s.made, self.pieces * (c - 1))
        act.copy(self.whi[:, u, 0:self.cols], self.raw[:, u, 0:self.cols]).then_inc(s.high, 1)

    def input_low(self, dve, s, first=0, end=None):
        for k in range(first, end or self.inputs):
            dve.wait_ge(s.in_hi, k + 1)
            dve.tensor_tensor(self.alo[:, k], self.source[:, k], self.ahi[:, k].bitcast(F32),
                              ALU.subtract).then_inc(s.in_lo, 1)

    def low(self, dve, s, c, u):
        dve.wait_ge(s.high, c + 1)
        dve.tensor_tensor(self.wlo[:, u, 0:self.cols], self.raw[:, u, 0:self.cols],
                          self.whi[:, u, 0:self.cols].bitcast(F32), ALU.subtract).then_inc(s.split, 1)

    def block(self, u, b):
        return self.whi[:, u, b * P:(b + 1) * P], self.wlo[:, u, b * P:(b + 1) * P]

    def feature_tile(self, pe, out, u, block0, blocks, k0, start, stop, split=None):
        for b in range(blocks):
            hi, lo = self.block(u, block0 + b)
            k = k0 + b
            if split is not None:
                pe.wait_ge(split, k + 1)
            pe.matmul(out, hi, self.ahi[:, k], start=start and b == 0, stop=False)
            pe.matmul(out, hi, self.alo[:, k], start=False, stop=False)
            mm = pe.matmul(out, lo, self.ahi[:, k], start=False, stop=stop and b == blocks - 1)
        return mm

    def token_tile(self, pe, out, u, t, tokens=None):
        w = [x[:, u, :].rearrange("p (k n) -> p k n", n=2 * P) for x in (self.whi, self.wlo)]
        for k in range(KD):
            a = [tokens(x[:, k], t) if tokens else x[:, k, t * P:(t + 1) * P] for x in (self.ahi, self.alo)]
            pe.matmul(out, a[0], w[0][:, k], start=k == 0, stop=False)
            pe.matmul(out, a[1], w[0][:, k], start=False, stop=False)
            mm = pe.matmul(out, a[0], w[1][:, k], start=False, stop=k == KD - 1)
        return mm

    def products(self, pe, s, i, ps, kind, freed=None, per_tile=1, tokens=None):
        for u in range(2):
            pe.wait_ge(s.split, 2 * i + u + 1)
            for n in range(2):
                tile = 4 * i + 2 * u + n
                if not (static(i) and i == 0):
                    pe.wait_ge(freed or s.freed, per_tile * (tile - 3))
                out = ps[:, 2 * u + n]
                if kind == "feature":
                    self.feature_tile(pe, out, u, KD * n, KD, 0, True, True,
                                      s.in_lo if static(i) and tile == 0 else None).then_inc(s.made, 1)
                else:
                    self.token_tile(pe, out[:, 0:2 * P], u, 2 * n, tokens)
                    self.token_tile(pe, out[:, 2 * P:], u, 2 * n + 1, tokens).then_inc(s.made, 1)


GEMM = ("split", "in_hi", "in_lo", "high", "made", "freed")


@contextmanager
def operands(nc, k, inputs, cols=CHUNK):
    with ExitStack() as stack:
        k.whi = stack.enter_context(sbuf(nc, "weights_high", [P, 2, cols], F32R))
        k.wlo = stack.enter_context(sbuf(nc, "weights_low", [P, 2, cols], F32R))
        k.ahi = stack.enter_context(sbuf(nc, "inputs_high", [P, inputs, T], F32R))
        k.alo = stack.enter_context(sbuf(nc, "inputs_low", [P, inputs, T], F32R))
        yield


def prefetch(nc, k, weights, index, cols):
    with nc.Block() as block:
        @block.sync
        def _(sp):
            for u in range(2):
                sp.sem_clear(k.landed[u])
            for u in range(2):
                sp.dma_start(k.raw[:, u, 0:cols], weights[index + u]).then_inc(k.landed[u], 16)



def hybrid_projections(nc, k, layer, h):
    ps, par = k.ps, h.par
    taps = par[:, C_TAP:C_TAP + 4 * QKV].rearrange("p (w c a) -> p w c a", w=4, a=1)
    n_groups = PROJ_CHUNKS // 2
    with operands(nc, k, KD), ExitStack() as stack, \
            phase(nc, *GEMM, "tap", "conv", "small", "small_out") as s:
        y = stack.enter_context(sbuf(nc, "conv", [P, 4, T], F32))
        st = Stream(k, k.w_stream, layer * HYBRID_CHUNKS, PROJ_CHUNKS, CHUNK, 2, KD, k.x)
        with nc.Block() as block:
            @block.sync
            def _(sp):
                st.load(sp, s)

            @block.tensor
            def _(pe):
                groups(pe, 0, 6, n_groups, lambda i: st.products(pe, s, i, ps, "feature"))
                st.products(pe, s, 6, ps, "token")
                for t in range(TT):
                    for kk in range(KD):
                        pe.matmul(ps[:, 4, t * 8:t * 8 + 8], k.x[:, kk, t * P:(t + 1) * P],
                                  par[:, C_WBA + kk * 8:C_WBA + kk * 8 + 8], start=kk == 0, stop=kk == KD - 1)
                for kk in range(KD):
                    mm = pe.matmul(ps[0:16, 5], par[:, C_WGR + kk * 16:C_WGR + kk * 16 + 16], k.x[:, kk],
                                   start=kk == 0, stop=kk == KD - 1)
                mm.then_inc(s.small, 1)

            @block.scalar
            def _(act):
                st.high(act, s, 0, 0)
                st.input_high(act, s)

                def convolved(i):
                    for u in range(2):
                        st.high(act, s, 2 * i + u + 1, 1 - u)
                        for n in range(2):
                            b = 2 * u + n
                            tile = 4 * i + b
                            act.wait_ge(s.made, tile + 1)
                            if not (static(i) and i == 0):
                                act.wait_ge(s.freed, tile - 3)
                            act.mul(y[:, b], ps[:, b], taps[:, 3, tile]).then_inc(s.tap, 1)
                        for n in range(2):
                            b = 2 * u + n
                            tile = 4 * i + b
                            act.wait_ge(s.conv, 3 * tile + 3)
                            act.activation(h.qkv[:, tile], y[:, b], ACT.Silu).then_inc(s.freed, 1)

                def gated(i):
                    for u in range(2):
                        st.high(act, s, 2 * i + u + 1, 1 - u)
                        for n in range(2):
                            tile = 4 * i + 2 * u + n
                            act.wait_ge(s.made, tile + 1)
                            act.activation(h.z[:, tile - QKV], ps[:, 2 * u + n], ACT.Silu).then_inc(s.freed, 1)

                def gla_qk(i):
                    for u in range(2):
                        st.high(act, s, 2 * i + u + 1, 1 - u)
                        for n in range(2):
                            act.wait_ge(s.made, 4 * i + 2 * u + n + 1)
                            act.mul(h.gqk[:, 2 * u + n], ps[:, 2 * u + n],
                                    GLA_SCALE if u == 0 else 1.0).then_inc(s.freed, 1)

                def gla_v(i):
                    for u in range(2):
                        if u == 0:
                            st.high(act, s, 2 * i + 1, 1)
                        for n in range(2):
                            act.wait_ge(s.made, 4 * i + 2 * u + n + 1)
                            act.copy(h.gv[:, 2 * n:2 * n + 2, u * 2 * P:(u + 1) * 2 * P],
                                     ps[:, 2 * u + n].rearrange("p (t n) -> p t n", t=2)).then_inc(s.freed, 1)
                groups(act, 0, 3, n_groups, convolved)
                groups(act, 3, 5, n_groups, gated)
                gla_qk(5)
                gla_v(6)
                act.wait_ge(s.small, 1)
                act.copy(h.ba[:], ps[:, 4, 0:TT * 8]).then_inc(s.small_out, 1)
                act.copy(h.gr[0:16, :], ps[0:16, 5]).then_inc(s.small_out, 1)

            @block.vector
            def _(dve):
                st.low(dve, s, 0, 0)
                st.input_low(dve, s)

                def convolved(i):
                    for u in range(2):
                        st.low(dve, s, 2 * i + u + 1, 1 - u)
                        for n in range(2):
                            b = 2 * u + n
                            tile = 4 * i + b
                            dve.wait_ge(s.tap, tile + 1)
                            for back in (1, 2, 3):
                                if back > 1:
                                    dve.wait_ge(s.conv, 3 * tile + back - 1)
                                ins = dve.scalar_tensor_tensor(
                                    y[:, b, back:], ps[:, b, 0:T - back], taps[:, 3 - back, tile],
                                    y[:, b, back:], ALU.mult, ALU.add)
                                ins.then_inc(s.conv, 1)

                def others(i):
                    for u in range(2):
                        st.low(dve, s, 2 * i + u + 1, 1 - u)
                groups(dve, 0, 3, n_groups, convolved)
                groups(dve, 3, 6, n_groups, others)
                st.low(dve, s, 2 * n_groups - 1, 1)


def delta_gates(nc, k, h, a):
    ps, par, con = k.ps, h.par, k.con
    ones, ident, incl = con[:, K_ONES:K_ONES + P], con[:, K_IDENT:K_IDENT + P], con[:, K_INCL:K_INCL + P]
    q, kk, v = h.qkv[:, 0:4], h.qkv[:, 4:8], h.qkv[:, 8:12]
    with ExitStack() as stack, phase(
            nc, "square", "square_sum", "inv_ln", "inv_norm", "normed", "gate_act", "gate_dve", "g_ready", "gcol_sum",
            "gcol", "spread", "row", "row_exp", "diff", "row_read", "decay", "masked", "kb", "scaled", "turned", "turned_read",
            "last_arg", "last_exp", "pair", "pair_read") as s:
        def sb(name, shape):
            return stack.enter_context(sbuf(nc, name, shape, F32))
        sq = sb("squares", [P, 2, T])
        inv = sb("inverse_norm", [P, 2, T])
        gt = sb("gate_steps", [P, 8, 16])
        beta = sb("beta", [P, TT, HEADS])
        g = sb("log_decay", [P, TT, HEADS])
        gcol = sb("g_column", [P, TT, HEADS])
        spread = sb("spread", [P, 2, TT, P])
        erow = sb("exp_g_row", [P, HEADS, T])
        decay = sb("decay", [P, TT, HEADS, P])
        kb = sb("k_beta", [P, HEADS, T])
        last = sb("to_last", [P, 2, HEADS, TT])
        ba = h.ba[:].rearrange("p (t c) -> p t c", t=TT)

        def b16(n):
            return gt[:, n].rearrange("p (t h) -> p t h", t=TT)

        with nc.Block() as block:
            @block.scalar
            def _(act):
                exp_and_log(act)
                act.activation(b16(0), ba[:, :, 0:HEADS], ACT.Exp, scale=-1.0).then_inc(s.gate_act, 1)
                act.activation(gt[:, 7, 0:HEADS], par[:, C_ALOG:C_ALOG + HEADS], ACT.Exp).then_inc(s.gate_act, 1)
                act.wait_ge(s.gate_dve, 1)
                act.activation(b16(2), b16(1), ACT.Abs).then_inc(s.gate_act, 1)
                act.wait_ge(s.gate_act, 3)
                act.activation(b16(3), b16(2), ACT.Exp, scale=-1.0).then_inc(s.gate_act, 1)
                act.wait_ge(s.gate_act, 4)
                act.activation(b16(4), b16(3), ACT.Ln, bias=con[:, K_ONE:K_ONE + 1]).then_inc(s.gate_act, 1)
                for j in range(9):
                    if j < 8:
                        if j >= 2:
                            act.wait_ge(s.square_sum, j - 1)
                        act.activation(sq[:, j % 2], h.qkv[:, j], ACT.Square).then_inc(s.square, 1)
                    if j >= 1:
                        n = j - 1
                        act.wait_ge(s.square_sum, n + 1)
                        if n >= 2:
                            act.wait_ge(s.normed, n - 1)
                        act.activation(inv[:, n % 2], ps[:, 4 + n % 2], ACT.Ln,
                                       bias=con[:, K_EPS:K_EPS + 1]).then_inc(s.inv_ln, 1)
                        act.wait_ge(s.inv_ln, n + 1)
                        if n < HEADS:
                            act.activation(inv[:, n % 2], inv[:, n % 2], ACT.Exp, scale=-0.5,
                                           bias=con[:, K_QLN:K_QLN + 1]).then_inc(s.inv_norm, 1)
                        else:
                            act.activation(inv[:, n % 2], inv[:, n % 2], ACT.Exp, scale=-0.5).then_inc(s.inv_norm, 1)
                for n in range(HEADS):
                    act.wait_ge(s.row, 2 * n + 1)
                    act.activation(erow[:, n], ps[:, (2 * n) % 4], ACT.Exp).then_inc(s.row_exp, 1)
                    act.wait_ge(s.diff, 4 * n + 4)
                    act.activation(decay[:, :, n], decay[:, :, n], ACT.Exp).then_inc(s.decay, 1)
                act.wait_ge(s.last_arg, HEADS)
                act.activation(last[:, 1], last[:, 0], ACT.Exp).then_inc(s.last_exp, 1)

            @block.vector
            def _(dve):
                dtb = par[:, C_DTB:C_DTB + HEADS].unsqueeze(1).to_broadcast([P, TT, HEADS])
                dve.tensor_tensor(b16(1), ba[:, :, HEADS:], dtb, ALU.add).then_inc(s.gate_dve, 1)
                dve.wait_ge(s.gate_act, 1)
                dve.tensor_scalar(b16(5), b16(0), 1.0, None, ALU.add).then_inc(s.gate_dve, 1)
                dve.wait_ge(s.gate_dve, 2)
                dve.reciprocal(beta[:], b16(5)).then_inc(s.gate_dve, 1)
                dve.wait_ge(s.gate_act, 5)
                dve.scalar_tensor_tensor(b16(6), b16(1), 0.0, b16(4), ALU.max, ALU.add).then_inc(s.gate_dve, 1)
                dve.wait_ge(s.gate_dve, 4)
                rate = gt[:, 7, 0:HEADS].unsqueeze(1).to_broadcast([P, TT, HEADS])
                dve.scalar_tensor_tensor(g[:], b16(6), -1.0, rate, ALU.mult, ALU.mult).then_inc(s.g_ready, 1)
                dve.wait_ge(s.gcol_sum, 1)
                dve.tensor_copy(gcol[:], ps[:, 6, 0:16].rearrange("p (t h) -> p t h", t=TT)).then_inc(s.gcol, 1)
                for j in range(8):
                    dve.wait_ge(s.inv_norm, j + 1)
                    dve.tensor_tensor(h.qkv[:, j], h.qkv[:, j], inv[:, j % 2], ALU.mult).then_inc(s.normed, 1)
                dve.wait_ge(s.gcol, 1)
                for n in range(HEADS):
                    row = ps[:, (2 * n) % 4].rearrange("p (t i) -> p t i", t=TT)
                    dve.wait_ge(s.row_exp, n + 1)
                    for t in range(TT):
                        dve.tensor_scalar(decay[:, t, n], row[:, t], gcol[:, t, n:n + 1], 0.0,
                                          ALU.subtract, ALU.min).then_inc(s.diff, 1)
                    dve.tensor_tensor(last[:, 0, n], row[:, :, P - 1], gcol[:, :, n], ALU.subtract).then_inc(s.last_arg, 1)
                    dve.wait_ge(s.row, 2 * n + 2)
                    dve.wait_ge(s.normed, 4 + n + 1)
                    dve.tensor_tensor(kb[:, n], kk[:, n], ps[:, (2 * n + 1) % 4], ALU.mult).then_inc(s.kb, 1)
                    dve.wait_ge(s.kb, n + 1)
                    dve.tensor_tensor(a.kbg[:, n], kb[:, n], erow[:, n], ALU.mult).then_inc(s.scaled, 1)
                for n in range(2 * HEADS):
                    hd = n % HEADS
                    dve.wait_ge(s.turned, n + 1)
                    if n == HEADS:
                        dve.wait_ge(s.last_exp, 1)
                    src = ps[:, 6 + n % 2].rearrange("p (t e) -> p t e", t=TT)
                    col = beta[:, :, hd] if n < HEADS else last[:, 1, hd]
                    dst = a.vb if n < HEADS else a.kdec
                    dve.tensor_tensor(dst[:, :, hd], src, col.unsqueeze(2).to_broadcast([P, TT, P]),
                                      ALU.mult).then_inc(s.turned_read, 1)
                for n in range(2 * TT):
                    t = n % TT
                    dve.wait_ge(s.pair, n + 1)
                    dve.wait_ge(s.masked, HEADS)
                    dst = a.at if n < TT else a.attn
                    dve.tensor_tensor(dst[:, t], ps[:, n % 2].rearrange("p (h i) -> p h i", h=HEADS),
                                      decay[:, t], ALU.mult).then_inc(s.pair_read, 1)

            @block.gpsimd
            def _(pool):
                pool.wait_ge(s.gate_dve, 3)
                pool.wait_ge(s.g_ready, 1)
                for n in range(2 * HEADS):
                    if n >= 2:
                        pool.wait_ge(s.row, n - 1)
                    base, col = (incl, g) if n % 2 == 0 else (ident, beta)
                    pool.tensor_tensor(spread[:, n % 2], base.unsqueeze(1).to_broadcast([P, TT, P]),
                                       col[:, :, n // 2].unsqueeze(2).to_broadcast([P, TT, P]),
                                       ALU.mult).then_inc(s.spread, 1)
                for n in range(HEADS):
                    pool.wait_ge(s.row_exp, n + 1)
                    pool.wait_ge(s.normed, n + 1)
                    pool.tensor_tensor(a.qg[:, n], q[:, n], erow[:, n], ALU.mult).then_inc(s.scaled, 1)
                    pool.tensor_copy(a.elast[:, n], erow[:, n].rearrange("p (t i) -> p t i", t=TT)[:, :, P - 1]) \
                        .then_inc(s.scaled, 1)
                    pool.wait_ge(s.decay, n + 1)
                    pool.affine_select(out=decay[:, :, n], in_=decay[:, :, n], compare_op=ALU.is_ge, fill=0.0, base=0,
                                       pattern=[[0, TT], [1, P]], channel_multiplier=-1).then_inc(s.masked, 1)

            @block.tensor
            def _(pe):
                pe.wait_ge(s.g_ready, 1)
                pe.matmul(ps[:, 6, 0:16], incl, g[:].rearrange("p t h -> p (t h)"), start=True, stop=True) \
                    .then_inc(s.gcol_sum, 1)
                for j in range(8):
                    pe.wait_ge(s.square, j + 1)
                    if j >= 2:
                        pe.wait_ge(s.inv_ln, j - 1)
                    pe.matmul(ps[:, 4 + j % 2], ones, sq[:, j % 2], start=True, stop=True).then_inc(s.square_sum, 1)
                for n in range(2 * HEADS):
                    pe.wait_ge(s.spread, n + 1)
                    if n >= 4:
                        pe.wait_ge(s.kb, (n - 4) // 2 + 1)
                        pe.wait_ge(s.last_arg, (n - 4) // 2 + 1)
                    pe.matmul(ps[:, n % 4], ones, spread[:, n % 2].rearrange("p t i -> p (t i)"),
                              start=True, stop=True).then_inc(s.row, 1)
                pe.wait_ge(s.gcol, 1)
                for n in range(2 * HEADS):
                    src = v if n < HEADS else kk
                    if n >= 2:
                        pe.wait_ge(s.turned_read, n - 1)
                    if n >= HEADS:
                        pe.wait_ge(s.normed, n + 1)
                    for t in range(TT):
                        mm = pe.transpose(ps[:, 6 + n % 2, t * P:(t + 1) * P],
                                          src[:, n % HEADS, t * P:(t + 1) * P], ident)
                    mm.then_inc(s.turned, 1)
                pe.wait_ge(s.kb, HEADS)
                for n in range(2 * TT):
                    cols = slice((n % TT) * P, (n % TT + 1) * P)
                    if n >= 2:
                        pe.wait_ge(s.pair_read, n - 1)
                    for hd in range(HEADS):
                        mm = pe.matmul(ps[:, n % 2, hd * P:(hd + 1) * P], kk[:, hd, cols],
                                       (kb if n < TT else q)[:, hd, cols], start=True, stop=True)
                    mm.then_inc(s.pair, 1)


def solve_and_decay(nc, k, h, a, gla):
    ps, con, par = k.ps, k.con, h.par
    ident = con[:, K_IDENT:K_IDENT + P]
    reset = con[:, K_RESET:K_RESET + T]
    n_levels = len(LEVELS)
    with ExitStack() as stack, phase(
            nc, "coupling", "left", "left_copy", "both", "inv", "inv_t",
            "logits", "act_step", "log_f", "sums", "filled", "slot_filled", "apart", "falls", "scaled", "pair", "taken",
            "end_arg", "end_exp", "k_end", "turned", "turned_read") as s:
        x = stack.enter_context(sbuf(nc, "inverse", [P, TT, HEADS, P], F32))
        ct = stack.enter_context(sbuf(nc, "coupling", [P, TT, HEADS, P], F32))
        cx = stack.enter_context(sbuf(nc, "coupled", [P, TT, HEADS, P], F32))
        bsum = stack.enter_context(sbuf(nc, "b_sums", [P, 2, T], F32))
        xt = a.inv_t
        fall, qs, ks = [h.qkv[:, 4 * n:4 * n + 4].rearrange("p (s f) i -> p s f i", s=2) for n in range(3)]
        kend = h.qkv[:, 0:2]
        lx = gla.k_end[:].rearrange("p t f d -> p (t f d)").rearrange("p (f i) -> p f i", f=2)
        la = gla.q_sum[:]
        q, kk = h.gqk[:, 0:2], h.gqk[:, 2:4]
        cq = [v.rearrange("p f (t i) -> p (f t) i", i=P) for v in (bsum[:], kend)]

        def bank(n):
            return ps[:, n].rearrange("p (h i) -> p h i", h=HEADS)

        def lower(v, n):
            return v.rearrange("p h (b i) -> p (h b) i", i=2 * LEVELS[n])[:, :, 0:LEVELS[n]]

        def upper(v, n):
            return v.rearrange("p h (b i) -> p (h b) i", i=2 * LEVELS[n])[:, :, LEVELS[n]:]

        def pair_bank(n, t):
            return 4 + 2 * ((4 * n + t) % 2)

        with nc.Block() as block:
            @block.tensor
            def _(pe):
                def left(n, t):
                    pe.wait_ge(s.coupling, 4 * n + t + 1)
                    if n:
                        pe.wait_ge(s.inv, 4 * (n - 1) + t + 1)
                    if 4 * n + t in (2, 3, 4, 5):
                        pe.wait_ge(s.inv, 4 * n + t - 1)
                    elif n:
                        pe.wait_ge(s.left_copy, 4 * (n - 1) + t - 1)
                    for hd in range(HEADS):
                        mm = pe.matmul(bank(t % 2)[:, hd], ct[:, t, hd], x[:, t, hd] if n else ident, start=True, stop=True)
                    mm.then_inc(s.left, 1)

                def both(n, t):
                    pe.wait_ge(s.left_copy, 4 * (n - 1) + t + 1)
                    pe.wait_ge(s.inv, min(4 * n + t, 4 * (n_levels - 1)))
                    pe.wait_ge(s.inv_t, 4 * n + t)
                    for hd in range(HEADS):
                        if n < n_levels - 1:
                            pe.matmul(bank(2)[:, hd], xt[:, t, hd], cx[:, t, hd], start=True, stop=True)
                    for hd in range(HEADS):
                        mm = pe.matmul(bank(3)[:, hd], cx[:, t, hd], xt[:, t, hd], start=True, stop=True)
                    mm.then_inc(s.both, 1)

                def pair(n, t):
                    if n:
                        pe.wait_ge(s.scaled, 2 * n)
                    if 4 * n + t >= 2:
                        pe.wait_ge(s.taken, 4 * n + t - 1)
                    if 4 * n + t == 1:
                        pe.wait_ge(s.act_step, 2)
                    cols = slice(t * P, (t + 1) * P)
                    for hd in range(HEADS):
                        rows = slice(64 * (hd % 2), 64 * (hd % 2) + 64)
                        ka, qa = (ks[:, (n - 1) % 2], qs[:, (n - 1) % 2]) if n else (kk, q)
                        mm = pe.matmul(bank(pair_bank(n, t) + hd % 2)[:, hd // 2], ka[rows, hd // 2, cols],
                                       qa[rows, hd // 2, cols], start=True, stop=True)
                    mm.then_inc(s.pair, 1)

                for f in range(2):
                    mm = pe.matmul(ps[:, 6 + f], h.w2[0:16, f * P:(f + 1) * P], h.gr[0:16, :], start=True, stop=True)
                mm.then_inc(s.logits, 1)
                for n in range(n_levels):
                    left(n, 0)
                    left(n, 1)
                    pair(n, 0)
                    left(n, 2)
                    left(n, 3)
                    pair(n, 1)
                    for t in range(TT):
                        if n:
                            both(n, t)
                        if t < 2:
                            pair(n, t + 2)
                for t in range(TT):
                    pair(n_levels, t)
                pe.wait_ge(s.k_end, 1)
                pe.wait_ge(s.taken, 4 * (n_levels + 1))
                for f in range(2):
                    for t in range(TT):
                        mm = pe.transpose(ps[:, 4 + f, t * P:(t + 1) * P], kend[:, f, t * P:(t + 1) * P], ident)
                    mm.then_inc(s.turned, 1)

            @block.scalar
            def _(act):
                act.wait_ge(s.logits, 1)
                for f in range(2):
                    act.activation(lx[:, f], ps[:, 6 + f], ACT.Identity, bias=par[:, C_GB + f:C_GB + f + 1]) \
                        .then_inc(s.act_step, 1)
                act.wait_ge(s.act_step, 2)
                act.activation(la, lx, ACT.Abs).then_inc(s.act_step, 1)
                act.wait_ge(s.act_step, 3)
                act.activation(la, la, ACT.Exp, scale=-1.0).then_inc(s.act_step, 1)
                act.wait_ge(s.act_step, 4)
                act.activation(la, la, ACT.Ln, bias=con[:, K_ONE:K_ONE + 1]).then_inc(s.act_step, 1)

                def falls(n):
                    act.wait_ge(s.apart, 2 * n + 2)
                    act.activation(fall[:, n % 2], fall[:, n % 2], ACT.Exp).then_inc(s.falls, 1)
                falls(0)
                falls(1)
                for n in range(1, n_levels):
                    for t in range(TT):
                        act.wait_ge(s.left, 4 * n + t + 1)
                        act.copy(cx[:, t], bank(t % 2)).then_inc(s.left_copy, 1)
                    if n + 1 < n_levels:
                        falls(n + 1)
                act.activation(gla.q_sum[:], bsum[:], ACT.Exp).then_inc(s.end_exp, 1)
                act.wait_ge(s.end_arg, 1)
                act.activation(kend, kend, ACT.Exp).then_inc(s.end_exp, 1)
                act.activation(gla.f_last[:], cq[0][:, :, P - 1].rearrange("p (f t) -> p f t", f=2), ACT.Exp) \
                    .then_inc(s.end_exp, 1)
                for f in range(2):
                    act.wait_ge(s.turned, f + 1)
                    act.copy(gla.k_end[:, :, f], ps[:, 4 + f].rearrange("p (t d) -> p t d", t=TT)).then_inc(s.turned_read, 1)

            @block.vector
            def _(dve):
                def first(t):
                    identity = ident.unsqueeze(1).to_broadcast([P, HEADS, P])
                    dve.wait_ge(s.left, t + 1)
                    dve.tensor_tensor(x[:, t], identity, bank(t % 2), ALU.subtract).then_inc(s.inv, 1)
                    dve.tensor_tensor(xt[:, t], identity, ct[:, t], ALU.subtract).then_inc(s.inv_t, 1)

                def update(n, t):
                    dve.wait_ge(s.both, 4 * (n - 1) + t + 1)
                    xu = upper(xt[:, t], n)
                    if n < n_levels - 1:
                        xl = lower(x[:, t], n)
                        dve.tensor_tensor(xl, xl, lower(bank(2), n), ALU.subtract).then_inc(s.inv, 1)
                    dve.tensor_tensor(xu, xu, upper(bank(3), n), ALU.subtract).then_inc(s.inv_t, 1)

                def take(n, t):
                    dve.wait_ge(s.pair, 4 * n + t + 1)
                    if n:
                        dve.wait_ge(s.taken, 4 * (n - 1) + t + 1)
                    b = pair_bank(n, t)
                    if n:
                        size = LEVELS[n - 1]
                        dst = gla.scores[:, t].rearrange("p (y f) (b i) -> p y (f b) i", y=2, i=2 * size)[:, :, :, size:]
                        src = ps[:, b:b + 2, 0:2 * P].rearrange("p y (c i) -> p y c i", i=2 * size)[:, :, :, size:]
                        mask = level_mask_of(con, n - 1, 2).bitcast(I32).rearrange("p (c i) -> p c i", i=2 * size)
                        mask = mask[:, :, size:].unsqueeze(1).to_broadcast([P, 2, P // size, size])
                    else:
                        dst = gla.scores[:, t].rearrange("p (y f) i -> p y f i", y=2)
                        src = ps[:, b:b + 2, 0:2 * P].rearrange("p y (f i) -> p y f i", f=2)
                        mask = ident.bitcast(I32).unsqueeze(1).unsqueeze(1).to_broadcast([P, 2, 2, P])
                    dve.copy_predicated(dst, mask, src).then_inc(s.taken, 1)

                def apart(n):
                    size = LEVELS[n]
                    low, up = (half(bsum[:], n) for half in (lower, upper))
                    fl, fu = (half(fall[:, n % 2], n) for half in (lower, upper))
                    middle = low[:, :, size - 1:size].to_broadcast([P, T // size, size])
                    if n >= 2:
                        dve.wait_ge(s.scaled, 2 * n - 2)
                    dve.tensor_tensor(fl, middle, low, ALU.subtract).then_inc(s.apart, 1)
                    dve.tensor_tensor(fu, up, middle, ALU.subtract).then_inc(s.apart, 1)

                dve.memset(gla.scores[:], 0.0).then_inc(s.filled, 1)
                dve.wait_ge(s.filled, 1)
                first(0)
                first(1)
                take(0, 0)
                first(2)
                first(3)
                for t in range(1, TT):
                    take(0, t)
                dve.wait_ge(s.act_step, 5)
                dve.scalar_tensor_tensor(lx, lx, 0.0, la, ALU.min, ALU.subtract).then_inc(s.log_f, 1)
                dve.wait_ge(s.log_f, 1)
                dve.tensor_scalar(lx, lx, 1.0 / GLA_TAU, None, ALU.mult).then_inc(s.log_f, 1)
                dve.wait_ge(s.log_f, 2)
                for f in range(2):
                    dve.tensor_tensor_scan(bsum[:, f], reset, lx[:, f], 0.0, ALU.mult, ALU.add).then_inc(s.sums, 1)
                dve.wait_ge(s.sums, 2)
                apart(0)
                apart(1)
                for n in range(1, n_levels):
                    take(n, 0)
                    take(n, 1)
                    for t in range(TT):
                        update(n, t)
                        if t < 2:
                            take(n, t + 2)
                    if n + 1 < n_levels:
                        apart(n + 1)
                dve.wait_ge(s.scaled, 2 * n_levels)
                dve.tensor_tensor(cq[1], cq[0][:, :, P - 1:P].to_broadcast([P, 8, P]), cq[0],
                                  ALU.subtract).then_inc(s.end_arg, 1)
                dve.wait_ge(s.end_exp, 2)
                dve.tensor_tensor(kend, kend, kk, ALU.mult).then_inc(s.k_end, 1)
                for t in range(TT):
                    take(n_levels, t)
                dve.tensor_tensor(gla.q_sum[:], gla.q_sum[:], q, ALU.mult).then_inc(s.end_arg, 1)

            @block.gpsimd
            def _(pool):
                def couple(n):
                    mask = level_mask_of(con, n).unsqueeze(1).to_broadcast([P, HEADS, P])
                    for t in range(TT):
                        if n:
                            pool.wait_ge(s.left, 4 * (n - 1) + t + 1)
                            pool.wait_ge(s.inv_t, t + 1)
                        pool.tensor_tensor(ct[:, t], a.at[:, t], mask, ALU.mult).then_inc(s.coupling, 1)

                def scale(n):
                    slot = n % 2
                    pool.wait_ge(s.falls, n + 1)
                    if n >= 2:
                        pool.wait_ge(s.pair, 4 * n)
                    pool.tensor_tensor(upper(qs[:, slot], n), upper(q, n), upper(fall[:, slot], n), ALU.mult) \
                        .then_inc(s.scaled, 1)
                    pool.tensor_tensor(lower(ks[:, slot], n), lower(kk, n), lower(fall[:, slot], n), ALU.mult) \
                        .then_inc(s.scaled, 1)
                couple(0)
                for slot in range(2):
                    pool.tensor_copy(qs[:, slot], q).then_inc(s.slot_filled, 1)
                    pool.tensor_copy(ks[:, slot], kk).then_inc(s.slot_filled, 1)
                couple(1)
                pool.wait_ge(s.slot_filled, 4)
                scale(0)
                scale(1)
                for n in range(2, n_levels):
                    couple(n)
                    scale(n)


def scans(nc, k, h, a, gla):
    ps = k.ps
    with ExitStack() as stack, phase(nc, "zero", "carried", "rest", "solved", "values", "out", "out_copy", "added", "state",
                                     "gla_out", "gla_out_copy", "gla_added", "gla_state") as s:
        st = stack.enter_context(sbuf(nc, "state", [P, HEADS, P], F32))
        z = stack.enter_context(sbuf(nc, "rest", [P, HEADS, P], F32))
        vn = stack.enter_context(sbuf(nc, "new_values", [P, HEADS, P], F32))
        gst = stack.enter_context(sbuf(nc, "gla_state", [P, HEADS, P], F32))

        def bank(n):
            return ps[:, n].rearrange("p (h i) -> p h i", h=HEADS)

        with nc.Block() as block:
            @block.tensor
            def _(pe):
                def gla_adds(t):
                    for hd in range(HEADS):
                        mm = pe.matmul(bank(4 + 2 * (t % 2))[:, hd], gla.k_end[:, t, hd // 2],
                                       h.gv[:, t, hd * P:(hd + 1) * P], start=True, stop=True)
                    mm.then_inc(s.gla_added, 1)

                def gla_outputs(t, heads, last):
                    cols = slice(t * P, (t + 1) * P)
                    for hd in heads:
                        out = bank(5 + 2 * (t % 2))[:, hd]
                        pe.matmul(out, gst[:, hd], gla.q_sum[:, hd // 2, cols], start=True, stop=False)
                        mm = pe.matmul(out, h.gv[:, t, hd * P:(hd + 1) * P], gla.scores[:, t, 2 * (hd % 2) + hd // 2],
                                       start=False, stop=True)
                    if last:
                        mm.then_inc(s.gla_out, 1)
                pe.wait_ge(s.zero, 2)
                for t in range(TT):
                    cols = slice(t * P, (t + 1) * P)
                    if t >= 1:
                        pe.wait_ge(s.state, 4 * t)
                    for hd in range(HEADS):
                        mm = pe.matmul(bank(0)[:, hd], a.kbg[:, hd, cols], st[:, hd], start=True, stop=True)
                    mm.then_inc(s.carried, 1)
                    gla_adds(t)
                    pe.wait_ge(s.rest, t + 1)
                    for hd in range(HEADS):
                        mm = pe.matmul(bank(1)[:, hd], a.inv_t[:, t, hd], z[:, hd], start=True, stop=True)
                    mm.then_inc(s.solved, 1)
                    if t >= 1:
                        pe.wait_ge(s.gla_state, HEADS * t)
                    if t >= 2:
                        pe.wait_ge(s.gla_out_copy, t - 1)
                    gla_outputs(t, (0, 1), False)
                    pe.wait_ge(s.values, t + 1)
                    for hd in range(HEADS):
                        mm = pe.matmul(bank(2)[:, hd], a.kdec[:, t, hd], vn[:, hd], start=True, stop=True)
                    mm.then_inc(s.added, 1)
                    if t >= 1:
                        pe.wait_ge(s.out_copy, t)
                    for hd in range(HEADS):
                        pe.matmul(bank(3)[:, hd], st[:, hd], a.qg[:, hd, cols], start=True, stop=False)
                        mm = pe.matmul(bank(3)[:, hd], vn[:, hd], a.attn[:, t, hd], start=False, stop=True)
                    mm.then_inc(s.out, 1)
                    gla_outputs(t, (2, 3), True)

            @block.vector
            def _(dve):
                dve.memset(st[:], 0.0).then_inc(s.zero, 1)
                dve.memset(gst[:], 0.0).then_inc(s.zero, 1)
                for t in range(TT):
                    dve.wait_ge(s.carried, t + 1)
                    dve.tensor_tensor(z[:], a.vb[:, t], bank(0), ALU.subtract).then_inc(s.rest, 1)
                    dve.wait_ge(s.added, t + 1)
                    dve.wait_ge(s.out, t + 1)
                    for hd in range(HEADS):
                        dve.scalar_tensor_tensor(st[:, hd], st[:, hd], a.elast[:, hd, t:t + 1], bank(2)[:, hd],
                                                 ALU.mult, ALU.add).then_inc(s.state, 1)
                    dve.wait_ge(s.gla_added, t + 1)
                    dve.wait_ge(s.gla_out, t + 1)
                    for hd in range(HEADS):
                        rows = slice(64 * (hd % 2), 64 * (hd % 2) + 64)
                        dve.scalar_tensor_tensor(gst[rows, hd], gst[rows, hd], gla.f_last[rows, hd // 2, t:t + 1],
                                                 bank(4 + 2 * (t % 2))[rows, hd], ALU.mult, ALU.add) \
                            .then_inc(s.gla_state, 1)

            @block.scalar
            def _(act):
                for t in range(TT):
                    act.wait_ge(s.solved, t + 1)
                    if t >= 1:
                        act.wait_ge(s.out, t)
                    act.copy(vn[:], bank(1)).then_inc(s.values, 1)
                    act.wait_ge(s.out, t + 1)
                    act.copy(h.qkv[:, 0:HEADS, t * P:(t + 1) * P], bank(3)).then_inc(s.out_copy, 1)
                    act.wait_ge(s.gla_out, t + 1)
                    act.copy(h.qkv[:, HEADS:2 * HEADS, t * P:(t + 1) * P], bank(5 + 2 * (t % 2))) \
                        .then_inc(s.gla_out_copy, 1)


def head_norms(nc, k, h):
    ps, con, par = k.ps, k.con, h.par
    ones, eps = con[:, K_ONES:K_ONES + P], con[:, K_EPS:K_EPS + 1]
    with ExitStack() as stack, phase(nc, "square", "square_sum", "inv_ln", "inv_norm", "gained", "normed") as s:
        sq = stack.enter_context(sbuf(nc, "squares", [P, 2, T], F32))
        inv = stack.enter_context(sbuf(nc, "inverse_norm", [P, 2, T], F32))
        with nc.Block() as block:
            @block.scalar
            def _(act):
                for j in range(2 * HEADS + 1):
                    if j < 2 * HEADS:
                        if j >= 2:
                            act.wait_ge(s.square_sum, j - 1)
                        act.activation(sq[:, j % 2], h.qkv[:, j], ACT.Square).then_inc(s.square, 1)
                    if j >= 1:
                        n = j - 1
                        act.wait_ge(s.square_sum, n + 1)
                        if n >= 2:
                            act.wait_ge(s.gained, n - 1)
                        act.activation(inv[:, n % 2], ps[:, n % 2], ACT.Ln, bias=eps, scale=1.0 / P).then_inc(s.inv_ln, 1)
                        act.wait_ge(s.inv_ln, n + 1)
                        act.activation(inv[:, n % 2], inv[:, n % 2], ACT.Exp, scale=-0.5).then_inc(s.inv_norm, 1)

            @block.tensor
            def _(pe):
                for j in range(2 * HEADS):
                    pe.wait_ge(s.square, j + 1)
                    if j >= 2:
                        pe.wait_ge(s.inv_ln, j - 1)
                    pe.matmul(ps[:, j % 2], ones, sq[:, j % 2], start=True, stop=True).then_inc(s.square_sum, 1)

            @block.vector
            def _(dve):
                for j in range(2 * HEADS):
                    gain = C_DNG if j < HEADS else C_GLG
                    dve.wait_ge(s.inv_norm, j + 1)
                    dve.scalar_tensor_tensor(h.qkv[:, j], h.qkv[:, j], par[:, gain:gain + 1], inv[:, j % 2],
                                             ALU.mult, ALU.mult).then_inc(s.gained, 1)

            @block.gpsimd
            def _(pool):
                for j in range(2 * HEADS):
                    pool.wait_ge(s.gained, j + 1)
                    pool.tensor_tensor(h.qkv[:, j], h.qkv[:, j], h.z[:, j], ALU.mult).then_inc(s.normed, 1)


def square_tile(act, s, sq, source, tile, ready):
    act.wait_ge(ready, tile + 1)
    if tile >= 3:
        act.wait_ge(s.added, max(tile - 3, 1))
    act.activation(sq[:, tile % 3], source[:, tile], ACT.Square).then_inc(s.square, 1)


def add_squares(eng, s, sq, total):
    for tile in range(1, KD):
        eng.wait_ge(s.square, tile + 1)
        if tile > 1:
            eng.wait_ge(s.added, tile - 1)
        eng.tensor_tensor(total[:], total[:] if tile > 1 else sq[:, 0], sq[:, tile % 3], ALU.add).then_inc(s.added, 1)


def output_product(nc, k, weights, base, source, inputs, chunks, out, alpha=None):
    ps = k.ps
    wide = inputs == KD
    n_groups = chunks // 2
    per = 2 if wide else 4
    with operands(nc, k, inputs), ExitStack() as stack, phase(nc, *GEMM, "square", "added") as s:
        sq = stack.enter_context(sbuf(nc, "squares", [P, 3, T], F32)) if alpha is None else None
        st = Stream(k, weights, base, chunks, CHUNK, per, inputs, source)
        with nc.Block() as block:
            @block.sync
            def _(sp):
                st.load(sp, s)

            @block.scalar
            def _(act):
                st.high(act, s, 0, 0)
                st.input_high(act, s)
                for c in range(1, chunks + 2):
                    if c < chunks:
                        st.high(act, s, c, c % 2)
                    if c >= 2 and alpha is None:
                        for tile in range(per * (c - 2), per * (c - 1)):
                            square_tile(act, s, sq, out, tile, s.freed)

            if alpha is None:
                @block.gpsimd
                def _(pool):
                    add_squares(pool, s, sq, k.total)
            else:
                @block.gpsimd
                def _(pool):
                    for tile in range(1, KD):
                        pool.wait_ge(s.freed, tile + 1)
                        if tile > 1:
                            pool.wait_ge(s.added, tile - 1)
                        pool.tensor_tensor(k.total[:], k.total[:] if tile > 1 else out[:, 0], out[:, tile],
                                           ALU.add).then_inc(s.added, 1)

            @block.vector
            def _(dve):
                st.low(dve, s, 0, 0)
                st.input_low(dve, s)
                for c in range(chunks):
                    if c + 1 < chunks:
                        st.low(dve, s, c + 1, (c + 1) % 2)
                    for n in range(per):
                        tile = per * c + n
                        dve.wait_ge(s.made, tile + 1)
                        src = ps[:, tile % 4]
                        if alpha is None:
                            dve.tensor_copy(out[:, tile], src).then_inc(s.freed, 1)
                        else:
                            dve.scalar_tensor_tensor(out[:, tile], out[:, tile], alpha, src,
                                                     ALU.mult, ALU.add).then_inc(s.freed, 1)

            @block.tensor
            def _(pe):
                for c in range(chunks):
                    pe.wait_ge(s.split, c + 1)
                    for n in range(per):
                        tile = per * c + n
                        if tile >= 4:
                            pe.wait_ge(s.freed, tile - 3)
                        st.feature_tile(pe, ps[:, tile % 4], c % 2, inputs * n, inputs, 0, True, True,
                                        s.in_lo if tile == 0 else None).then_inc(s.made, 1)


def layer_norm(nc, k, h):
    ps, con, par, x = k.ps, k.con, h.par, k.x
    ones, eps = con[:, K_ONES:K_ONES + P], con[:, K_EPS:K_EPS + 1]
    with ExitStack() as stack, phase(nc, "total", "mean", "centred", "square", "square_sum", "inv_ln", "inv_norm",
                                     "scaled", "done") as s:
        sq = stack.enter_context(sbuf(nc, "squares", [P, 3, T], F32))
        mean = stack.enter_context(sbuf(nc, "mean", [P, T], F32))
        inv = stack.enter_context(sbuf(nc, "inverse_deviation", [P, T], F32))
        with nc.Block() as block:
            @block.tensor
            def _(pe):
                pe.matmul(ps[:, 0], ones, k.total[:], start=True, stop=True).then_inc(s.total, 1)
                for j in range(KD):
                    pe.wait_ge(s.square, j + 1)
                    pe.matmul(ps[:, 1], ones, sq[:, j % 3], start=j == 0, stop=j == KD - 1).then_inc(s.square_sum, 1)

            @block.scalar
            def _(act):
                act.wait_ge(s.total, 1)
                act.mul(mean[:], ps[:, 0], 1.0 / D).then_inc(s.mean, 1)
                for j in range(KD):
                    act.wait_ge(s.centred, j + 1)
                    if j >= 3:
                        act.wait_ge(s.square_sum, j - 2)
                    act.activation(sq[:, j % 3], x[:, j], ACT.Square).then_inc(s.square, 1)
                act.wait_ge(s.square_sum, KD)
                act.activation(inv[:], ps[:, 1], ACT.Ln, bias=eps, scale=1.0 / D).then_inc(s.inv_ln, 1)
                act.wait_ge(s.inv_ln, 1)
                act.activation(inv[:], inv[:], ACT.Exp, scale=-0.5).then_inc(s.inv_norm, 1)
                for j in range(KD):
                    act.wait_ge(s.scaled, j + 1)
                    act.activation(x[:, j], x[:, j], ACT.Identity, scale=par[:, C_LNG + j:C_LNG + j + 1],
                                   bias=par[:, C_LNB + j:C_LNB + j + 1]).then_inc(s.done, 1)

            @block.vector
            def _(dve):
                dve.wait_ge(s.mean, 1)
                for j in range(KD):
                    dve.tensor_tensor(x[:, j], x[:, j], mean[:], ALU.subtract).then_inc(s.centred, 1)
                dve.wait_ge(s.inv_norm, 1)
                for j in range(KD):
                    dve.tensor_tensor(x[:, j], x[:, j], inv[:], ALU.mult).then_inc(s.scaled, 1)


def hybrid_layer(nc, k, layer):
    with ExitStack() as stack:
        def sb(name, shape):
            return stack.enter_context(sbuf(nc, name, shape, F32))
        h = named(
            par=sb("layer_parameters", [P, N_LAYER]), w2=sb("gate_w2_sb", [16, 2 * P]),
            qkv=sb("qkv", [P, QKV, T]), z=sb("gates_z", [P, 2 * HEADS, T]), gqk=sb("gla_qk", [P, 4, T]),
            gv=sb("gla_v", [P, TT, T]), ba=sb("beta_decay_logits", [P, TT * 8]), gr=sb("gate_rank", [16, T]))
        with phase(nc, "params") as s, nc.Block() as block:
            @block.sync
            def _(sp):
                sp.dma_start(h.par[:], k.layer_params[layer]).then_inc(s.params, 16)
                sp.dma_start(h.w2[:], k.gate_w2[layer]).then_inc(s.params, 16)
                sp.wait_ge(s.params, 32)
        hybrid_projections(nc, k, layer, h)
        prefetch(nc, k, k.w_stream, layer * HYBRID_CHUNKS + PROJ_CHUNKS, CHUNK)
        with ExitStack() as inner:
            def sb2(name, shape):
                return inner.enter_context(sbuf(nc, name, shape, F32))
            a = named(
                kbg=sb2("k_beta_g", [P, HEADS, T]), qg=sb2("q_g", [P, HEADS, T]), at=sb2("a_transposed", [P, TT, HEADS, P]),
                attn=sb2("attention", [P, TT, HEADS, P]), vb=sb2("v_beta", [P, TT, HEADS, P]),
                kdec=sb2("k_decayed", [P, TT, HEADS, P]), inv_t=sb2("inverse_transposed", [P, TT, HEADS, P]),
                elast=sb2("chunk_decay", [P, HEADS, TT]))
            delta_gates(nc, k, h, a)
            gla = named(scores=sb2("gla_scores", [P, TT, HEADS, P]), q_sum=sb2("q_sum", [P, 2, T]),
                        f_last=sb2("f_last", [P, 2, TT]), k_end=sb2("k_end", [P, TT, 2, P]))
            solve_and_decay(nc, k, h, a, gla)
            scans(nc, k, h, a, gla)
        head_norms(nc, k, h)
        k.total = sb("total_over_tiles", [P, T])
        output_product(nc, k, k.w_stream, layer * HYBRID_CHUNKS + PROJ_CHUNKS, h.qkv, KD, OUT_CHUNKS, k.x, ALPHA)
        layer_norm(nc, k, h)
        prefetch(nc, k, k.w_stream, (layer + 1) * HYBRID_CHUNKS, CHUNK)



def t5_buckets(dist):
    exact = N_BUCKETS // 2
    d = np.maximum(dist, 1).astype(np.float32)
    large = exact + (np.log(d / np.float32(exact)) / np.float32(math.log(BUCKET_MAX_DIST / exact))
                     * np.float32(N_BUCKETS - exact)).astype(np.int32)
    return np.where(dist < exact, dist, np.minimum(large, N_BUCKETS - 1))


def bucket_onehots():
    out = np.zeros((N_BUCKETS + 1, DIL_GROUPS, 384), np.float32)
    for g, rate in enumerate(DIL_RATES):
        c = np.arange(384) - (P - 1)
        m = P - c if g == 0 else -c
        ok = (m >= 0) & (m <= (P if g == 0 else P - 1)) & (m * ORDER[g] % rate == 0)
        b = t5_buckets(np.where(ok, m, 0) * ORDER[g])
        out[b, g, np.arange(384)] = ok
        out[N_BUCKETS, g] = np.where(ok, 0, NEG)
    return out


def rms_norm(nc, k, source, gain, squares, out=None, measure=False, store=None):
    ps, con, x = k.ps, k.con, k.x
    ones, eps = con[:, K_ONES:K_ONES + P], con[:, K_EPS:K_EPS + 1]
    with ExitStack() as stack, phase(nc, "square", "added", "square_sum", "inv_ln", "inv_norm", "scaled", "done",
                                     "done_pool", "new_square", "new_sum", "stored") as s:
        sq = stack.enter_context(sbuf(nc, "squares", [P, 3, T], F32))
        inv = stack.enter_context(sbuf(nc, "inverse_rms", [P, T], F32))

        def wait_new(eng, j):
            eng.wait_ge(s.done_pool if j % 2 else s.done, j // 2 + 1)

        with nc.Block() as block:
            if store is not None:
                @block.sync
                def _(sp):
                    for j in range(KD):
                        wait_new(sp, j)
                        sp.dma_start(store[:, j], x[:, j]).then_inc(s.stored, 16)
                    sp.wait_ge(s.stored, 16 * KD)

            @block.tensor
            def _(pe):
                if squares != "bank":
                    if squares == "here":
                        pe.wait_ge(s.added, KD - 1)
                    pe.matmul(ps[:, 7], ones, k.total[:], start=True, stop=True).then_inc(s.square_sum, 1)
                if measure:
                    pe.wait_ge(s.inv_ln, 1)
                    for j in range(KD):
                        pe.wait_ge(s.new_square, j + 1)
                        pe.matmul(ps[:, 7], ones, sq[:, j % 3], start=j == 0, stop=j == KD - 1).then_inc(s.new_sum, 1)

            @block.scalar
            def _(act):
                if squares == "here":
                    for j in range(KD):
                        if j >= 3:
                            act.wait_ge(s.added, max(j - 3, 1))
                        act.activation(sq[:, j % 3], source[:, j], ACT.Square).then_inc(s.square, 1)
                if squares != "bank":
                    act.wait_ge(s.square_sum, 1)
                act.activation(inv[:], ps[:, 7], ACT.Ln, bias=eps, scale=1.0 / D).then_inc(s.inv_ln, 1)
                act.wait_ge(s.inv_ln, 1)
                act.activation(inv[:], inv[:], ACT.Exp, scale=-0.5).then_inc(s.inv_norm, 1)
                if measure:
                    for j in range(KD):
                        wait_new(act, j)
                        if j >= 3:
                            act.wait_ge(s.new_sum, j - 2)
                        act.activation(sq[:, j % 3], x[:, j], ACT.Square).then_inc(s.new_square, 1)

            @block.vector
            def _(dve):
                if squares == "here":
                    add_squares(dve, s, sq, k.total)
                dve.wait_ge(s.inv_norm, 1)
                for j in range(KD):
                    g = k.second[:, C_GAIN + gain * KD + j:C_GAIN + gain * KD + j + 1]
                    dst = source if out is None else out
                    dve.scalar_tensor_tensor(dst[:, j], source[:, j], g, inv[:], ALU.mult, ALU.mult) \
                        .then_inc(s.scaled, 1)
                    if out is None and j % 2:
                        dve.wait_ge(s.scaled, j)
                        dve.tensor_tensor(x[:, j - 1], x[:, j - 1], source[:, j - 1], ALU.add).then_inc(s.done, 1)

            if out is None:
                @block.gpsimd
                def _(pool):
                    for j in range(1, KD, 2):
                        pool.wait_ge(s.scaled, j + 1)
                        pool.tensor_tensor(x[:, j], x[:, j], source[:, j], ALU.add).then_inc(s.done_pool, 1)


def stick_projections(nc, k, source, qk, v):
    n_groups = SB_CHUNKS // 2
    with operands(nc, k, KD), phase(nc, *GEMM) as s:
        st = Stream(k, k.w_stream, AT_STICK, SB_CHUNKS, CHUNK, 2, KD, source)
        ps = k.ps
        with nc.Block() as block:
            @block.sync
            def _(sp):
                st.load(sp, s)

            @block.tensor
            def _(pe):
                groups(pe, 0, 4, n_groups, lambda i: st.products(pe, s, i, ps, "feature"))
                groups(pe, 4, 6, n_groups, lambda i: st.products(pe, s, i, ps, "token"))

            @block.scalar
            def _(act):
                st.high(act, s, 0, 0)
                st.input_high(act, s)

                def features(scale):
                    def body(i):
                        for u in range(2):
                            st.high(act, s, 2 * i + u + 1, 1 - u)
                            for n in range(2):
                                tile = 4 * i + 2 * u + n
                                act.wait_ge(s.made, tile + 1)
                                act.mul(qk[:, tile], ps[:, 2 * u + n], scale).then_inc(s.freed, 1)
                    return body

                def values(i):
                    for u in range(2):
                        if not (static(i) and i == n_groups - 1 and u == 1):
                            st.high(act, s, 2 * i + u + 1, 1 - u)
                        for n in range(2):
                            act.wait_ge(s.made, 4 * i + 2 * u + n + 1)
                            act.copy(v[:, 2 * n:2 * n + 2, bass.ds((2 * i + u - 8) * 2 * P, 2 * P)],
                                     ps[:, 2 * u + n].rearrange("p (t n) -> p t n", t=2)).then_inc(s.freed, 1)
                groups(act, 0, 2, n_groups, features(64 ** -0.5))
                groups(act, 2, 4, n_groups, features(1.0))
                groups(act, 4, 6, n_groups, values)

            @block.vector
            def _(dve):
                st.low(dve, s, 0, 0)
                st.input_low(dve, s)

                def body(i):
                    for u in range(2):
                        if not (static(i) and i == n_groups - 1 and u == 1):
                            st.low(dve, s, 2 * i + u + 1, 1 - u)
                groups(dve, 0, n_groups, n_groups, body)


def stick_attention(nc, k, qk, v, out):
    ps, con = k.ps, k.con
    negtri, negones = con[:, K_NEGTRI:K_NEGTRI + P], con[:, K_NEGONES:K_NEGONES + P]
    pairs = SB_HEADS // 2
    units = [(p, jt) for p in range(pairs) for jt in reversed(range(TT))]
    n_units = len(units)
    with ExitStack() as stack, phase(nc, "z", "capped", "exp", "log", "softplus", "masked", "later", "sums", "weights",
                                     "kept", "out", "out_copy") as s:
        zc = stack.enter_context(sbuf(nc, "z_capped", [P, 2, 2, T], F32))
        softp = stack.enter_context(sbuf(nc, "softplus", [P, 2, 2, T], F32))
        later = stack.enter_context(sbuf(nc, "later_keys", [P, 2, 2, T], F32))
        w = stack.enter_context(sbuf(nc, "weights", [P, 2, 2, T], F32))

        def zbank(u):
            return ps[:, 2 * (u % 3):2 * (u % 3) + 2]

        def made_later(u):
            return (TT - 1) * (u // TT) + min(u % TT, TT - 1)

        with nc.Block() as block:
            @block.tensor
            def _(pe):
                def scores(u):
                    p, jt = units[u]
                    if u >= 3:
                        pe.wait_ge(s.weights, u - 2)
                    for y in range(2):
                        rows = slice(64 * y, 64 * y + 64)
                        mm = pe.matmul(zbank(u)[:, y, jt * P:], qk[rows, 8 + p, jt * P:(jt + 1) * P],
                                       qk[rows, p, jt * P:], start=True, stop=False, skip_group_check=True)
                    mm.then_inc(s.z, 1)

                def sums(u):
                    p, jt = units[u]
                    pe.wait_ge(s.softplus, u + 1)
                    pe.wait_ge(s.masked, u + 1)
                    if jt < TT - 1:
                        pe.wait_ge(s.later, 2 * made_later(u))
                    for y in range(2):
                        if jt < TT - 1:
                            pe.matmul(zbank(u)[:, y, (jt + 1) * P:], negones, later[:, u % 2, y, (jt + 1) * P:],
                                      start=False, stop=False, skip_group_check=True)
                        mm = pe.matmul(zbank(u)[:, y, jt * P:], negtri, softp[:, u % 2, y, jt * P:],
                                       start=False, stop=True, skip_group_check=True)
                    mm.then_inc(s.sums, 1)

                def values(u):
                    p, jt = units[u]
                    pe.wait_ge(s.kept, u + 1)
                    if jt == TT - 1 and p >= 2:
                        pe.wait_ge(s.out_copy, p - 1)
                    for y in range(2):
                        hd = 2 * p + y
                        mm = pe.matmul(ps[64 * y:64 * y + 64, 6 + p % 2, jt * P:], v[:, jt, hd * 64:hd * 64 + 64],
                                       w[:, u % 2, y, jt * P:], start=jt == TT - 1, stop=jt == 0,
                                       skip_group_check=True)
                    mm.then_inc(s.out, 1)
                for u in range(n_units + 2):
                    if u < n_units:
                        scores(u)
                    if 1 <= u <= n_units:
                        sums(u - 1)
                    if u >= 2:
                        values(u - 2)

            @block.vector
            def _(dve):
                def cap(u):
                    jt = units[u][1]
                    dve.wait_ge(s.z, u + 1)
                    if u >= 2:
                        dve.wait_ge(s.log, u - 1)
                        dve.wait_ge(s.softplus, u - 1)
                    dve.tensor_scalar(zc[:, u % 2, :, jt * P:], zbank(u)[:, :, jt * P:], 40.0, None, ALU.min) \
                        .then_inc(s.capped, 1)

                def softplus(u):
                    jt = units[u][1]
                    dve.wait_ge(s.log, u + 1)
                    if u >= 2:
                        dve.wait_ge(s.sums, u - 1)
                        dve.wait_ge(s.later, 2 * made_later(u - 1))
                    dve.tensor_tensor(softp[:, u % 2, :, jt * P:], zbank(u)[:, :, jt * P:], zc[:, u % 2, :, jt * P:],
                                      ALU.max).then_inc(s.softplus, 1)

                def copy_out(p):
                    dve.wait_ge(s.out, TT * (p + 1))
                    dve.tensor_copy(out[:, p], ps[:, 6 + p % 2]).then_inc(s.out_copy, 1)
                for u in range(n_units + 1):
                    if u >= 1:
                        softplus(u - 1)
                    if u < n_units:
                        cap(u)
                    if u >= 6 and (u - 6) % TT == 0:
                        copy_out((u - 6) // TT)
                copy_out(pairs - 1)

            @block.scalar
            def _(act):
                def logs(u):
                    jt = units[u][1]
                    z = zc[:, u % 2, :, jt * P:]
                    act.wait_ge(s.capped, u + 1)
                    act.activation(z, z, ACT.Exp).then_inc(s.exp, 1)
                    act.wait_ge(s.exp, u + 1)
                    act.activation(z, z, ACT.Ln, bias=con[:, K_ONE:K_ONE + 1]).then_inc(s.log, 1)

                def weights(u):
                    jt = units[u][1]
                    act.wait_ge(s.sums, u + 1)
                    if u >= 2:
                        act.wait_ge(s.out, u - 1)
                    act.activation(w[:, u % 2, :, jt * P:], zbank(u)[:, :, jt * P:], ACT.Exp).then_inc(s.weights, 1)
                for u in range(n_units + 1):
                    if u < n_units:
                        logs(u)
                    if u >= 1:
                        weights(u - 1)

            @block.gpsimd
            def _(pool):
                def keep(x, jt):
                    d = x[:, :, jt * P:(jt + 1) * P]
                    return pool.affine_select(out=d, in_=d, compare_op=ALU.is_gt, fill=0.0, base=0,
                                              pattern=[[0, 2], [1, P]], channel_multiplier=-1)
                for u in range(n_units + 1):
                    if u < n_units:
                        jt = units[u][1]
                        pool.wait_ge(s.softplus, u + 1)
                        keep(softp[:, u % 2], jt).then_inc(s.masked, 1)
                        pool.wait_ge(s.masked, u + 1)
                        if u >= 1:
                            pool.wait_ge(s.sums, u)
                        new, old = later[:, (u + 1) % 2], later[:, u % 2]
                        if jt == TT - 1:
                            pool.tensor_copy(new[:, :, jt * P:], softp[:, u % 2, :, jt * P:]).then_inc(s.later, 2)
                        elif jt > 0:
                            pool.wait_ge(s.later, 2 * made_later(u))
                            pool.tensor_copy(new[:, :, jt * P:(jt + 1) * P], softp[:, u % 2, :, jt * P:(jt + 1) * P]) \
                                .then_inc(s.later, 1)
                            pool.tensor_tensor(new[:, :, (jt + 1) * P:], old[:, :, (jt + 1) * P:],
                                               softp[:, u % 2, :, (jt + 1) * P:], ALU.add).then_inc(s.later, 1)
                    if u >= 1:
                        pool.wait_ge(s.weights, u)
                        keep(w[:, (u - 1) % 2], units[u - 1][1]).then_inc(s.kept, 1)


def ffn_up(nc, k, source, layer, h):
    ps = k.ps
    n_groups = UP_CHUNKS // 2
    taps = k.second[:, C_FTAP:C_FTAP + 2 * 3 * 2 * KF].rearrange("p (l w y c a) -> p l w y c a", l=2, w=3, y=2, a=1)
    bias = k.second[:, C_FBIAS:C_FBIAS + 2 * 2 * KF].rearrange("p (l y c a) -> p l y c a", l=2, y=2, a=1)
    with operands(nc, k, KD), ExitStack() as stack, phase(nc, *GEMM, "tap", "conv", "silu") as s:
        y = stack.enter_context(sbuf(nc, "conv", [P, 4, T], F32))
        st = Stream(k, k.w_stream, AT_UP[layer], UP_CHUNKS, CHUNK, 2, KD, source)
        with nc.Block() as block:
            @block.sync
            def _(sp):
                st.load(sp, s)

            @block.tensor
            def _(pe):
                groups(pe, 0, n_groups, n_groups, lambda i: st.products(pe, s, i, ps, "feature", s.conv, 2))

            @block.scalar
            def _(act):
                st.high(act, s, 0, 0)
                st.input_high(act, s)

                def body(i):
                    for u in range(2):
                        if not (static(i) and i == n_groups - 1 and u == 1):
                            st.high(act, s, 2 * i + u + 1, 1 - u)
                        for n in range(2):
                            b = 2 * u + n
                            act.wait_ge(s.made, 4 * i + b + 1)
                            if not (static(i) and i == 0):
                                act.wait_ge(s.freed, 2 * i - 1 + n)
                            act.activation(y[:, b], ps[:, b], ACT.Identity, scale=taps[:, layer, 2, u, 2 * i + n],
                                           bias=bias[:, layer, u, 2 * i + n]).then_inc(s.tap, 1)
                        for n in range(2):
                            if u == 0:
                                act.wait_ge(s.conv, 2 * (4 * i + n) + 2)
                                act.activation(y[:, n], y[:, n], ACT.Silu).then_inc(s.silu, 1)
                groups(act, 0, n_groups, n_groups, body)
                exp_and_log(act)

            @block.vector
            def _(dve):
                st.low(dve, s, 0, 0)
                st.input_low(dve, s)

                def body(i):
                    for u in range(2):
                        if not (static(i) and i == n_groups - 1 and u == 1):
                            st.low(dve, s, 2 * i + u + 1, 1 - u)
                        for n in range(2):
                            b = 2 * u + n
                            dve.wait_ge(s.tap, 4 * i + b + 1)
                            for back in (1, 2):
                                if back == 2:
                                    dve.wait_ge(s.conv, 2 * (4 * i + b) + 1)
                                dve.scalar_tensor_tensor(y[:, b, back:], ps[:, b, 0:T - back],
                                                         taps[:, layer, 2 - back, u, 2 * i + n], y[:, b, back:],
                                                         ALU.mult, ALU.add).then_inc(s.conv, 1)
                    dve.wait_ge(s.silu, 2 * i + 2)
                    dve.wait_ge(s.conv, 8 * i + 8)
                    for n in range(2):
                        dve.tensor_tensor(h[:, 2 * i + n], y[:, n], y[:, 2 + n], ALU.mult).then_inc(s.freed, 1)
                groups(dve, 0, n_groups, n_groups, body)


def ffn_down(nc, k, layer, h):
    ps = k.ps
    n_groups = DOWN_CHUNKS // 4
    cols = DOWN_BLOCKS * P
    with operands(nc, k, KF, cols), ExitStack() as stack, phase(nc, *GEMM, "square", "added") as s:
        sq = stack.enter_context(sbuf(nc, "squares", [P, 3, T], F32))
        st = Stream(k, k.w_down, layer * DOWN_CHUNKS, DOWN_CHUNKS, cols, 1, KF, h)
        with nc.Block() as block:
            @block.sync
            def _(sp):
                st.load(sp, s)

            @block.tensor
            def _(pe):
                def body(i):
                    for n in range(2):
                        if not (static(i) and i == 0):
                            pe.wait_ge(s.freed, 2 * i + n - 1)
                        for half in range(2):
                            pe.wait_ge(s.split, 4 * i + 2 * n + half + 1)
                            st.feature_tile(pe, ps[:, n], half, 0, DOWN_BLOCKS, DOWN_BLOCKS * half,
                                            half == 0, half == 1,
                                            s.in_lo if static(i) and i + n == 0 else None).then_inc(s.made, 1)
                groups(pe, 0, n_groups, n_groups, body)

            @block.scalar
            def _(act):
                for half in range(2):
                    st.high(act, s, half, half)
                    st.input_high(act, s, DOWN_BLOCKS * half, DOWN_BLOCKS * (half + 1))
                for tile in range(1, KD + 1):
                    if tile < KD:
                        for u in range(2):
                            st.high(act, s, 2 * tile + u, u)
                    square_tile(act, s, sq, h, tile - 1, s.freed)

            @block.gpsimd
            def _(pool):
                add_squares(pool, s, sq, k.total)

            @block.vector
            def _(dve):
                for half in range(2):
                    st.low(dve, s, half, half)
                    st.input_low(dve, s, DOWN_BLOCKS * half, DOWN_BLOCKS * (half + 1))

                def body(i):
                    for n in range(2):
                        for half in range(2):
                            c = 4 * i + 2 * n + half + 1
                            if static(i) and c == 1:
                                continue
                            if not (static(i) and i == n_groups - 1 and n == 1 and half == 1):
                                st.low(dve, s, c, 1 - half)
                        dve.wait_ge(s.made, 2 * (2 * i + n) + 2)
                        dve.tensor_copy(h[:, 2 * i + n], ps[:, n]).then_inc(s.freed, 1)
                groups(dve, 0, n_groups, n_groups, body)


def bias_tables(nc, k, rel_bias, bucket_onehot, tables):
    scratch = nc.dram_tensor("bias_rows", (DIL_GROUPS, DIL_HEADS, 384), F32, kind="Internal").ap()
    ps = k.ps
    flip = k.con[:, K_FLIP:K_FLIP + P]
    parts = [(g, n) for g in range(DIL_GROUPS) for n in range(4 if g == 0 else 2)]
    with ExitStack() as stack, phase(nc, "loaded", "ones", "rows", "copied", "written", "read", "flipped", "table") as s:
        rb = stack.enter_context(sbuf(nc, "bias_by_bucket", [N_BUCKETS + 1, DIL_GROUPS * DIL_HEADS], F32))
        onehot = stack.enter_context(sbuf(nc, "bucket_onehot", [N_BUCKETS + 1, DIL_GROUPS, 384], F32))
        rows = stack.enter_context(sbuf(nc, "bias_rows_sb", [DIL_HEADS, DIL_GROUPS, 384], F32))
        backward = [stack.enter_context(sbuf(nc, "table_backward", t.shape, F32)) for t in tables]

        def columns_of(x, n):
            return x[:].rearrange("p h j -> p (h j)")[:, n * T:(n + 1) * T]

        with nc.Block() as block:
            @block.sync
            def _(sp):
                sp.dma_start(rb[0:N_BUCKETS], rel_bias).then_inc(s.loaded, 16)
                sp.dma_start(onehot[:], bucket_onehot).then_inc(s.loaded, 16)
                sp.wait_ge(s.copied, DIL_GROUPS)
                sp.dma_start(scratch.rearrange("g h c -> h g c"), rows[:]).then_inc(s.written, 16)
                sp.wait_ge(s.written, 16)
                for g in range(DIL_GROUPS):
                    width = 2 * P if g == 0 else P
                    shifted = bass.AP(scratch.tensor, g * DIL_HEADS * 384, [[1, P], [384, DIL_HEADS], [1, width]])
                    sp.dma_start(backward[g][:], shifted).then_inc(s.read, 16)

            @block.vector
            def _(dve):
                dve.memset(rb[N_BUCKETS:N_BUCKETS + 1], 1.0).then_inc(s.ones, 1)
                for g in range(DIL_GROUPS):
                    dve.wait_ge(s.rows, g + 1)
                    dve.tensor_copy(rows[:, g], ps[0:DIL_HEADS, g, 0:384]).then_inc(s.copied, 1)
                for m, (g, n) in enumerate(parts):
                    dve.wait_ge(s.flipped, m + 1)
                    dve.tensor_copy(columns_of(tables[g], n), ps[:, m]).then_inc(s.table, 1)

            @block.tensor
            def _(pe):
                pe.wait_ge(s.loaded, 32)
                pe.wait_ge(s.ones, 1)
                for g in range(DIL_GROUPS):
                    pe.matmul(ps[0:DIL_HEADS, g, 0:384], rb[:, g * DIL_HEADS:(g + 1) * DIL_HEADS], onehot[:, g],
                              start=True, stop=True).then_inc(s.rows, 1)
                pe.wait_ge(s.read, 16 * DIL_GROUPS)
                for m, (g, n) in enumerate(parts):
                    pe.matmul(ps[:, m], flip, columns_of(backward[g], n), start=True, stop=True).then_inc(s.flipped, 1)


def by_class(x, rate):
    return x.rearrange("p (l c) -> p c l", c=rate)


def dilated_projections(nc, k, source, q, kk, v):
    n_groups = DIL_CHUNKS // 2
    with operands(nc, k, KD), phase(nc, *GEMM) as s:
        st = Stream(k, k.w_stream, AT_DILATED, DIL_CHUNKS, CHUNK, 2, KD, source)
        ps = k.ps

        def ordered_tokens(x, g, t):
            rate = ORDER[g]
            if rate == 1:
                return x[:, t * P:(t + 1) * P]
            return by_class(x, rate)[:, t]

        with nc.Block() as block:
            @block.sync
            def _(sp):
                st.load(sp, s)

            @block.tensor
            def _(pe):
                groups(pe, 0, 6, n_groups, lambda i: st.products(pe, s, i, ps, "feature"))
                for g in range(DIL_GROUPS):
                    st.products(pe, s, 6 + g, ps, "token", tokens=lambda x, t, g=g: ordered_tokens(x, g, t))

            @block.scalar
            def _(act):
                st.high(act, s, 0, 0)
                st.input_high(act, s)
                for i in range(n_groups):
                    for u in range(2):
                        if 2 * i + u + 1 < DIL_CHUNKS:
                            st.high(act, s, 2 * i + u + 1, 1 - u)
                        for n in range(2):
                            tile = 4 * i + 2 * u + n
                            src = ps[:, 2 * u + n]
                            act.wait_ge(s.made, tile + 1)
                            if tile < 24:
                                dst = (q if tile < 12 else kk)[:, tile % 12]
                                rate = ORDER[tile % 12 // 4]
                                if rate > 1:
                                    dst, src = dst.rearrange("p (c l) -> p c l", c=rate), by_class(src, rate)
                                act.mul(dst, src, 64 ** -0.5 if tile < 12 else 1.0).then_inc(s.freed, 1)
                            else:
                                act.copy(v[:, 2 * n:2 * n + 2, i - 6, u * 2 * P:(u + 1) * 2 * P],
                                         src.rearrange("p (t n) -> p t n", t=2)).then_inc(s.freed, 1)

            @block.vector
            def _(dve):
                st.low(dve, s, 0, 0)
                st.input_low(dve, s)

                def body(i):
                    for u in range(2):
                        if not (static(i) and i == n_groups - 1 and u == 1):
                            st.low(dve, s, 2 * i + u + 1, 1 - u)
                groups(dve, 0, n_groups, n_groups, body)


def dilated_scores(nc, k, q, kk, v, tables, num, top, total):
    ps, con = k.ps, k.con
    ident = con[:, K_IDENT:K_IDENT + P]
    units = [(0, 0, 0, 8, 1)] + [(0, t, h0, 4, 2) for t in range(1, TT) for h0 in (0, 4)] \
        + [(g, t, 0, 8, 1) for g in (1, 2) for t in range(TT)]
    n_units = len(units)
    tiles = [n for n, (g, t, h0, heads, _) in enumerate(units) if h0 + heads == DIL_HEADS]
    with ExitStack() as stack, phase(nc, "scores", "half", "biased", "exp", "turned", "turned_read", "out", "out_copy") as s:
        sc = stack.enter_context(sbuf(nc, "scores", [P, 2, 2 * T], F32))
        pt = stack.enter_context(sbuf(nc, "weights_turned", [P, 2, 8, P], F32))

        def exps(n):
            return sum(u[3] for u in units[:n])

        def tile_of(n):
            return sum(1 for m in tiles if m < n)

        with nc.Block() as block:
            @block.tensor
            def _(pe):
                def scores(n):
                    g, t, h0, heads, keys = units[n]
                    b = 2 * (n % 2)
                    if n >= 2:
                        pe.wait_ge(s.biased, n - 1)
                    for hd in range(h0, h0 + heads):
                        rows = slice(64 * (hd % 2), 64 * (hd % 2) + 64)
                        at = (hd - h0) // 2 * keys * P
                        f = 4 * g + hd // 2
                        mm = pe.matmul(ps[:, b + hd % 2, at:at + keys * P], q[rows, f, t * P:(t + 1) * P],
                                       kk[rows, f, (t + 1 - keys) * P:(t + 1) * P], start=True, stop=True)
                    mm.then_inc(s.scores, 1)

                def turn(n):
                    pe.wait_ge(s.exp, exps(n + 1))
                    if n >= 1:
                        pe.wait_ge(s.turned_read, 2 * n)
                    for m in range(8):
                        mm = pe.transpose(ps[:, 4 + m // 4, m % 4 * P:(m % 4 + 1) * P],
                                          sc[:, n % 2, m * P:(m + 1) * P], ident)
                        if m % 4 == 3:
                            mm.then_inc(s.turned, 1)

                def values(n):
                    g, t, h0, heads, keys = units[n]
                    out = 6 + tile_of(n) % 2
                    pe.wait_ge(s.turned_read, 2 * n + 2)
                    if tile_of(n) >= 2:
                        pe.wait_ge(s.out_copy, tile_of(n) - 1)
                    for hd in range(h0, h0 + heads):
                        for kt in range(keys):
                            m = (hd % 2) * 4 + (hd - h0) // 2 * keys + kt
                            mm = pe.matmul(ps[:, out, hd * 64:hd * 64 + 64], pt[:, n % 2, m],
                                           v[:, t + 1 - keys + kt, g, hd * 64:hd * 64 + 64],
                                           start=kt == 0, stop=kt == keys - 1)
                    mm.then_inc(s.out, 1)
                for n in range(n_units + 2):
                    if n < n_units:
                        scores(n)
                    if 1 <= n <= n_units:
                        turn(n - 1)
                    if n >= 2:
                        values(n - 2)

            @block.vector
            def _(dve):
                def bias(n):
                    g, t, h0, heads, keys = units[n]
                    b = 2 * (n % 2)
                    w = keys * P
                    hh = heads // 2
                    tab = tables[g][:, h0:h0 + heads, :]
                    if g == 0 and keys == 1:
                        tab = tab[:, :, P:]
                    dst = sc[:, n % 2].rearrange("p (y h w) -> p y h w", y=2, h=hh)
                    dve.wait_ge(s.scores, n + 1)
                    if n >= 2:
                        dve.wait_ge(s.turned, 2 * (n - 1))
                    for y in range(2):
                        dve.tensor_tensor(dst[:, y], ps[:, b + y].rearrange("p (h w) -> p h w", h=hh),
                                          tab.rearrange("p (h y) w -> p y h w", y=2)[:, y], ALU.add).then_inc(s.half, 1)
                    dve.wait_ge(s.half, 2 * n + 2)
                    dve.tensor_reduce(top[:, TT * g + t, h0:h0 + heads].rearrange("p (h y) -> p y h", y=2), dst, AX_X,
                                      ALU.max, negate=True).then_inc(s.biased, 1)

                def turned(n):
                    for half in range(2):
                        dve.wait_ge(s.turned, 2 * n + half + 1)
                        if n >= 2:
                            dve.wait_ge(s.out, n - 1)
                        dve.tensor_copy(pt[:, n % 2, 4 * half:4 * half + 4],
                                        ps[:, 4 + half].rearrange("p (m i) -> p m i", m=4)).then_inc(s.turned_read, 1)
                for n in range(n_units + 1):
                    if n < n_units:
                        bias(n)
                    if n >= 1:
                        turned(n - 1)

            @block.scalar
            def _(act):
                def exps(n):
                    g, t, h0, heads, keys = units[n]
                    act.wait_ge(s.biased, n + 1)
                    for hd in range(h0, h0 + heads):
                        at = hd % 2 * T + (hd - h0) // 2 * keys * P
                        x = sc[:, n % 2, at:at + keys * P]
                        act.activation(x, x, ACT.Exp, bias=top[:, TT * g + t, hd:hd + 1],
                                       accum_out=total[:, TT * g + t, hd:hd + 1]).then_inc(s.exp, 1)

                def copy_out(n):
                    g, t = units[n][0:2]
                    act.wait_ge(s.out, n + 1)
                    act.copy(num[:, TT * g + t], ps[:, 6 + tile_of(n) % 2]).then_inc(s.out_copy, 1)
                for n in range(n_units + 3):
                    if n < n_units:
                        exps(n)
                    if n - 3 in tiles:
                        copy_out(n - 3)


def dilated_merge(nc, k, num, top, total, out):
    ps, con = k.ps, k.con
    ident = con[:, K_IDENT:K_IDENT + P]
    G = DIL_GROUPS
    with ExitStack() as stack, phase(nc, "turned", "rows", "step", "exp", "weight", "columns", "column", "scaled",
                                     "features", "merged") as s:
        rows = stack.enter_context(sbuf(nc, "top_and_total", [DIL_HEADS, 2, G, T], F32))
        low = stack.enter_context(sbuf(nc, "least_negative", [DIL_HEADS, T], F32))
        den = stack.enter_context(sbuf(nc, "denominator", [DIL_HEADS, G, T], F32))
        col = stack.enter_context(sbuf(nc, "weight_columns", [P, G * TT, DIL_HEADS], F32))
        tops, totals = rows[:, 0], rows[:, 1]

        with nc.Block() as block:
            @block.tensor
            def _(pe):
                for g in range(G):
                    for n, src in enumerate((top, total)):
                        for t in range(TT):
                            mm = pe.transpose(ps[0:DIL_HEADS, 2 * g + n, t * P:(t + 1) * P], src[:, TT * g + t], ident)
                        mm.then_inc(s.turned, 1)
                pe.wait_ge(s.weight, G)
                for g in range(G):
                    for t in range(TT):
                        rate = ORDER[g]
                        if rate == 1:
                            src = tops[:, g, t * P:(t + 1) * P]
                        else:
                            src = by_class(tops[:, g], rate)[:, t]
                        n = TT * g + t
                        mm = pe.transpose(ps[:, 6, n * DIL_HEADS:(n + 1) * DIL_HEADS], src,
                                          ident[0:DIL_HEADS, 0:DIL_HEADS])
                mm.then_inc(s.columns, 1)
                for n in range(G * TT):
                    pe.wait_ge(s.scaled, n + 1)
                    if n >= 4:
                        pe.wait_ge(s.merged, n - 3)
                    for f in range(TT):
                        mm = pe.transpose(ps[:, n % 4, f * P:(f + 1) * P], num[:, n, f * P:(f + 1) * P], ident)
                    mm.then_inc(s.features, 1)

            @block.scalar
            def _(act):
                for g in range(G):
                    rate = ORDER[g]
                    for n in range(2):
                        act.wait_ge(s.turned, 2 * g + n + 1)
                        src = ps[0:DIL_HEADS, 2 * g + n]
                        dst = rows[:, n, g]
                        if rate > 1:
                            src, dst = src.rearrange("p (c l) -> p c l", c=rate), by_class(dst, rate)
                        act.copy(dst, src).then_inc(s.rows, 1)
                act.wait_ge(s.step, 5)
                act.activation(tops, tops, ACT.Exp, scale=-1.0).then_inc(s.exp, 1)

            @block.vector
            def _(dve):
                steps = [0]

                def step(ins):
                    steps[0] += 1
                    ins.then_inc(s.step, 1)
                    dve.wait_ge(s.step, steps[0])
                dve.wait_ge(s.rows, 2 * G)
                step(dve.tensor_tensor(low[:], tops[:, 0], tops[:, 1], ALU.min))
                step(dve.tensor_tensor(low[:], low[:], tops[:, 2], ALU.min))
                for g in range(G):
                    step(dve.tensor_tensor(tops[:, g], tops[:, g], low[:], ALU.subtract))
                dve.wait_ge(s.exp, 1)
                step(dve.tensor_tensor(den[:], tops, totals, ALU.mult))
                step(dve.tensor_tensor(low[:], den[:, 0], den[:, 1], ALU.add))
                step(dve.tensor_tensor(low[:], low[:], den[:, 2], ALU.add))
                step(dve.reciprocal(low[:], low[:]))
                for g in range(G):
                    dve.tensor_tensor(tops[:, g], tops[:, g], low[:], ALU.mult).then_inc(s.weight, 1)
                dve.wait_ge(s.columns, 1)
                dve.tensor_copy(col[:].rearrange("p n h -> p (n h)"), ps[:, 6, 0:G * TT * DIL_HEADS]).then_inc(s.column, 1)
                for n in range(G * TT):
                    g, t = n // TT, n % TT
                    rate = ORDER[g]
                    dve.wait_ge(s.features, n + 1)
                    src = ps[:, n % 4].rearrange("p (f i) -> p f i", f=TT)
                    if rate == 1:
                        dve.tensor_copy(out[:, :, t * P:(t + 1) * P], src).then_inc(s.merged, 1)
                        continue
                    dve.wait_ge(s.merged, TT * g)
                    dst = out[:].rearrange("p f (l c) -> p c f l", c=rate)[:, t]
                    dve.tensor_tensor(dst, dst, src, ALU.add).then_inc(s.merged, 1)

            @block.gpsimd
            def _(pool):
                pool.wait_ge(s.column, 1)
                for n in range(G * TT):
                    x = num[:, n].rearrange("p (h e) -> p h e", h=DIL_HEADS)
                    pool.tensor_tensor(x, x, col[:, n].unsqueeze(2).to_broadcast([P, DIL_HEADS, 64]), ALU.mult) \
                        .then_inc(s.scaled, 1)


def second_block(nc, k, second_params, rel_bias, bucket_onehot, out_t):
    with ExitStack() as stack:
        def sb(name, shape, where=stack):
            return where.enter_context(sbuf(nc, name, shape, F32))
        k.second = sb("second_parameters", [P, N_SECOND])
        with phase(nc, "params") as s, nc.Block() as block:
            @block.sync
            def _(sp):
                sp.dma_start(k.second[:], second_params).then_inc(s.params, 16)
                sp.wait_ge(s.params, 16)

        def mixer_out(layer, source, inputs, chunks, base, next_base):
            with ExitStack() as inner:
                m = sb("mixed", [P, KD, T], inner)
                k.total = sb("total_over_tiles", [P, T], inner)
                output_product(nc, k, k.w_stream, base, source, inputs, chunks, m)
                prefetch(nc, k, k.w_stream, next_base, CHUNK)
                rms_norm(nc, k, m, 4 * layer + 1, "total", measure=True)

        def feed_forward(layer, next_base, store=None):
            with ExitStack() as inner:
                h = sb("hidden", [P, KF, T], inner)
                k.total = sb("total_over_tiles", [P, T], inner)
                with ExitStack() as up:
                    xn = sb("normed", [P, KD, T], up)
                    rms_norm(nc, k, k.x, 4 * layer + 2, "bank", out=xn)
                    ffn_up(nc, k, xn, layer, h)
                prefetch(nc, k, k.w_down, layer * DOWN_CHUNKS, DOWN_BLOCKS * P)
                ffn_down(nc, k, layer, h)
                if next_base is not None:
                    prefetch(nc, k, k.w_stream, next_base, CHUNK)
                rms_norm(nc, k, h, 4 * layer + 3, "total", measure=store is None, store=store)

        with ExitStack() as mixer:
            v = sb("stick_v", [P, TT, D], mixer)
            o = sb("stick_out", [P, KD, T], mixer)
            qk = sb("stick_qk", [P, 2 * KD, T], mixer)
            with ExitStack() as inner:
                xn = sb("normed", [P, KD, T], inner)
                k.total = sb("total_over_tiles", [P, T], inner)
                rms_norm(nc, k, k.x, 0, "here", out=xn)
                stick_projections(nc, k, xn, qk, v)
            prefetch(nc, k, k.w_stream, AT_STICK_OUT, CHUNK)
            stick_attention(nc, k, qk, v, o)
            mixer_out(0, o, KD, OUT_CHUNKS, AT_STICK_OUT, AT_UP[0])
        feed_forward(0, AT_DILATED)
        with ExitStack() as mixer:
            num = sb("numerators", [P, DIL_GROUPS * TT, T], mixer)
            top = sb("negative_maxima", [P, DIL_GROUPS * TT, DIL_HEADS], mixer)
            total = sb("totals", [P, DIL_GROUPS * TT, DIL_HEADS], mixer)
            with ExitStack() as inner:
                q = sb("dilated_q", [P, 4 * DIL_GROUPS, T], inner)
                kk = sb("dilated_k", [P, 4 * DIL_GROUPS, T], inner)
                v = sb("dilated_v", [P, TT, DIL_GROUPS, T], inner)
                rms_norm(nc, k, k.x, 4, "bank", out=num[:, 0:KD])
                dilated_projections(nc, k, num, q, kk, v)
                prefetch(nc, k, k.w_stream, AT_DILATED_OUT, CHUNK)
                with ExitStack() as tab:
                    tables = [sb(f"bias_{g}", [P, DIL_HEADS, 2 * P if g == 0 else P], tab)
                              for g in range(DIL_GROUPS)]
                    bias_tables(nc, k, rel_bias, bucket_onehot, tables)
                    dilated_scores(nc, k, q, kk, v, tables, num, top, total)
            o = sb("dilated_out", [P, TT, T], mixer)
            dilated_merge(nc, k, num, top, total, o)
            mixer_out(1, o, TT, DIL_OUT_CHUNKS, AT_DILATED_OUT, AT_UP[1])
        feed_forward(1, None, out_t)



def program(nc, x_t, w_stream, w_down, layer_params, gate_w2, second_params, rel_bias, bucket_onehot, consts, out_t):
    NAMES.clear()
    with ExitStack() as stack:
        def sb(name, shape):
            return stack.enter_context(sbuf(nc, name, shape, F32))
        k = Shared()
        k.w_stream, k.w_down, k.layer_params, k.gate_w2 = w_stream, w_down, layer_params, gate_w2
        k.con, k.x, k.raw = sb("constants", [P, N_CONST]), sb("residual", [P, KD, T]), sb("weights_raw", [P, 2, CHUNK])
        k.ps = stack.enter_context(nc.psum_tensor("psum", [P, 8, T], F32))
        k.landed = [stack.enter_context(nc.semaphore(f"weights_landed_{u}")) for u in range(2)]
        with phase(nc, "loaded") as s, nc.Block() as block:
            @block.sync
            def _(sp):
                sp.dma_start(k.con[:], consts).then_inc(s.loaded, 16)
                sp.dma_start(k.x[:], x_t).then_inc(s.loaded, 16)
                sp.wait_ge(s.loaded, 32)
        prefetch(nc, k, w_stream, 0, CHUNK)
        with nc.Fori(0, LAYERS) as layer:
            hybrid_layer(nc, k, layer)
        second_block(nc, k, second_params, rel_bias, bucket_onehot, out_t)


def feature_chunks(w):
    kt, n = w.shape[0] // P, w.shape[1]
    per = CHUNK // (kt * P)
    return w.reshape(kt, P, n // (per * P), per, P).transpose(2, 1, 3, 0, 4).reshape(-1, P, CHUNK)


def token_chunks(w):
    return w.reshape(KD, P, -1, 2 * P).transpose(2, 1, 0, 3).reshape(-1, P, CHUNK)


def columns(v):
    v = v.reshape(-1, v.shape[-1] // P, P)
    return v.transpose(2, 0, 1).reshape(P, -1)


def interleaved(a, b):
    return np.stack([a, b], 1).reshape(-1, *a.shape[1:])


def layout(x, w_in, conv_w, dn_a_log, dn_dt_bias, gla_gate_w2, gla_gate_b, dn_norm_g, gla_norm_g, w_out, ln_g, ln_b,
           rel_bias_2, norm_gains_2, sb_w_qkv_2, sb_w_o_2, dil_w_qkv_2, dil_w_o_2, ffn_w_up_2, ffn_conv_w_2,
           ffn_conv_b_2, ffn_w_down_2, **unused):
    at = np.cumsum([0, 1536, 512, 8, 512, 512, 512, 16])
    stream, params = [], []
    for n in range(LAYERS):
        w = w_in[n]
        qkv, z, ba, gqk, gv, gz, gr = (w[:, a:b] for a, b in zip(at[:-1], at[1:]))
        stream += [feature_chunks(m) for m in (qkv, z, gz, gqk)] + [token_chunks(gv), feature_chunks(w_out[n])]
        params.append(np.concatenate([
            columns(conv_w[n]), columns(gla_gate_b[n]), columns(dn_norm_g[n]), columns(gla_norm_g[n]), columns(ln_g[n]),
            columns(ln_b[n]), np.broadcast_to(dn_a_log[n], (P, HEADS)), np.broadcast_to(dn_dt_bias[n], (P, HEADS)),
            ba.reshape(KD, P, 8).transpose(1, 0, 2).reshape(P, -1),
            gr.reshape(KD, P, 16).transpose(1, 0, 2).reshape(P, -1)], 1))
    up = [interleaved(feature_chunks(w[:, :FF]), feature_chunks(w[:, FF:])) for w in ffn_w_up_2]
    stream += [feature_chunks(sb_w_qkv_2[0][:, :2 * D]), token_chunks(sb_w_qkv_2[0][:, 2 * D:]),
               feature_chunks(sb_w_o_2[0]), up[0],
               feature_chunks(dil_w_qkv_2[0][:, :3072]), token_chunks(dil_w_qkv_2[0][:, 3072:]),
               feature_chunks(dil_w_o_2[0]), up[1]]
    down = ffn_w_down_2.reshape(LAYERS, 2, DOWN_BLOCKS, P, KD, P).transpose(0, 4, 1, 3, 2, 5) \
        .reshape(LAYERS * DOWN_CHUNKS, P, DOWN_BLOCKS * P)
    second = np.concatenate([columns(norm_gains_2), columns(ffn_conv_w_2), columns(ffn_conv_b_2)], 1)
    return {
        "x_t": x[0].reshape(T, KD, P).transpose(2, 1, 0), "w_stream": np.concatenate(stream), "w_down": down,
        "layer_params": np.stack(params), "gate_w2": gla_gate_w2, "second_params": second, "rel_bias": rel_bias_2,
        "bucket_onehot": bucket_onehots(), "consts": constants(),
    }


def kernel(**inputs):
    from concourse import bacc
    from concourse.bass_utils import run_bass_kernel_spmd

    arrays = {n: np.ascontiguousarray(a) for n, a in layout(**inputs).items()}
    nc = bacc.Bacc("TRN2", target_bir_lowering=False, num_devices=1)
    args = [nc.dram_tensor(n, a.shape, mybir.dt.from_np(a.dtype), kind="ExternalInput").ap() for n, a in arrays.items()]
    args.append(nc.dram_tensor("out_t", (P, KD, T), F32, kind="ExternalOutput").ap())
    program(nc, *args)
    got = run_bass_kernel_spmd(nc, [arrays], core_ids=[0]).results[0]["out_t"]
    return np.ascontiguousarray(got.transpose(2, 1, 0)).reshape(1, T, D)
```
